# Optimizing a Trainium2 kernel written in Bass

```python
import math
import jax, jax.numpy as jnp
from jax import lax
import numpy as np

D_MODEL = 1024
BATCH = 1
SEQ = 512
DEPTH = 2

GRID_W = 64
CTX_LEN = 256

N_HEADS = 8
N_KV_HEADS = 2
HEAD_DIM = 64
ATTN_W = N_HEADS * HEAD_DIM
KV_W = N_KV_HEADS * HEAD_DIM
WINDOW = 128
BLOCK = 128
ROPE_THETA = 10000.0
AXIS_ROT = HEAD_DIM // 2

HY_CH = D_MODEL // 4
HY_ORDER = 2
HY_SHORT = 3
HY_EMB = 33
HY_BANDS = (HY_EMB - 1) // 2
HY_FILTER_W = 64
HY_TARGET = 1e-2
HY_FAST = 0.3
HY_SLOW = 1.5

CV_CH = D_MODEL // 4
CV_K = 31

K0 = ATTN_W
V0 = K0 + KV_W
HY0 = V0 + KV_W
CV0 = HY0 + (HY_ORDER + 1) * HY_CH
IN_W = CV0 + 2 * CV_CH
MIX_W = ATTN_W + HY_CH + CV_CH

D_FF = 2816
FFN_K = 3

EPS = 1e-6
NEG_INF = -1e30
F32 = jnp.float32

kernel_name = "hybrid_parallel_mixer_dit"

def rms_norm(t, g):
    t32 = t.astype(F32)
    y = t32 * lax.rsqrt(jnp.mean(t32 * t32, axis=-1, keepdims=True) + EPS) * g.astype(F32)
    return y.astype(t.dtype)

def layer_norm(t, g, b):
    t32 = t.astype(F32)
    mu = jnp.mean(t32, axis=-1, keepdims=True)
    var = jnp.mean(jnp.square(t32 - mu), axis=-1, keepdims=True)
    return ((t32 - mu) * lax.rsqrt(var + EPS) * g.astype(F32) + b.astype(F32)).astype(t.dtype)

def modulate(t, shift, scale):
    return t * (1 + scale) + shift

def dwconv(t, w, b):
    k, ch = w.shape
    pad = (k - 1) // 2
    y = lax.conv_general_dilated(t, w.astype(t.dtype)[:, None, :], window_strides=(1,),
                                 padding=[(pad, pad)], dimension_numbers=('NWC', 'WIO', 'NWC'),
                                 feature_group_count=ch)
    return y + b.astype(t.dtype)

def heads(t, n):
    b, l, _ = t.shape
    return t.reshape(b, l, n, HEAD_DIM)

def axial_rope_tables(rows):
    row = jnp.repeat(jnp.arange(rows, dtype=F32), GRID_W)
    col = jnp.tile(jnp.arange(GRID_W, dtype=F32), rows)
    inv = ROPE_THETA ** (-jnp.arange(0, AXIS_ROT, 2, dtype=F32) / AXIS_ROT)
    ang = jnp.stack([row[:, None] * inv, col[:, None] * inv], axis=1)
    return jnp.cos(ang), jnp.sin(ang)

def apply_rope(t, cos, sin):
    b, l, h, dh = t.shape
    t2 = t.astype(F32).reshape(b, l, h, 2, 2, AXIS_ROT // 2)
    a, bb = t2[..., 0, :], t2[..., 1, :]
    cs, sn = cos[None, :, None], sin[None, :, None]
    out = jnp.stack([a * cs - bb * sn, bb * cs + a * sn], axis=-2)
    return out.reshape(b, l, h, dh).astype(t.dtype)

def window_attention(q, k, v, k_ctx, v_ctx, sink):
    b, l, h, dh = q.shape
    nb = l // BLOCK
    g = h // N_KV_HEADS
    scale = HEAD_DIM ** -0.5
    qb = q.reshape(b, nb, BLOCK, N_KV_HEADS, g, dh)

    def band(t):
        tp = jnp.pad(t, ((0, 0), (BLOCK, BLOCK), (0, 0), (0, 0))).reshape(b, nb + 2, BLOCK, N_KV_HEADS, dh)
        return jnp.concatenate([tp[:, :-2], tp[:, 1:-1], tp[:, 2:]], axis=2)

    kb, vb = band(k), band(v)
    qi = jnp.arange(BLOCK)[:, None]
    kj = jnp.arange(3 * BLOCK)[None, :]
    kpos = (jnp.arange(nb)[:, None, None] - 1) * BLOCK + kj[None]
    mask = (jnp.abs(kj - BLOCK - qi) <= WINDOW)[None] & (kpos >= 0) & (kpos < l)

    s_loc = jnp.einsum('bnqkgd,bnckd->bnkgqc', qb, kb, preferred_element_type=F32) * scale
    s_loc = jnp.where(mask[None, :, None, None], s_loc, NEG_INF)
    s_ctx = jnp.einsum('bnqkgd,bckd->bnkgqc', qb, k_ctx, preferred_element_type=F32) * scale
    sink_b = sink.astype(F32).reshape(1, 1, N_KV_HEADS, g, 1, 1)
    m = jnp.maximum(jnp.maximum(s_loc.max(-1, keepdims=True), s_ctx.max(-1, keepdims=True)), sink_b)
    p_loc = jnp.exp(s_loc - m)
    p_ctx = jnp.exp(s_ctx - m)
    denom = p_loc.sum(-1) + p_ctx.sum(-1) + jnp.exp(sink_b - m)[..., 0]
    o = (jnp.einsum('bnkgqc,bnckd->bnqkgd', p_loc, vb.astype(F32))
         + jnp.einsum('bnkgqc,bckd->bnqkgd', p_ctx, v_ctx.astype(F32)))
    o = o / jnp.transpose(denom, (0, 1, 4, 2, 3))[..., None]
    return o.reshape(b, l, h * dh).astype(q.dtype)

def context_attention(q, k, v, sink):
    b, lc, h, dh = q.shape
    g = h // N_KV_HEADS
    qg = q.reshape(b, lc, N_KV_HEADS, g, dh)
    s = jnp.einsum('bqkgd,bckd->bkgqc', qg, k, preferred_element_type=F32) * (HEAD_DIM ** -0.5)
    sink_b = jnp.broadcast_to(sink.astype(F32).reshape(1, N_KV_HEADS, g, 1, 1), s.shape[:-1] + (1,))
    pr = jax.nn.softmax(jnp.concatenate([s, sink_b], axis=-1), axis=-1)[..., :-1]
    o = jnp.einsum('bkgqc,bckd->bqkgd', pr, v.astype(F32))
    return o.reshape(b, lc, h * dh).astype(q.dtype)

def hyena_filters(l, w1, b1, f1, w2, b2, f2, w3):
    t = jnp.linspace(0.0, 1.0, l, dtype=F32)[:, None]
    w = (2.0 * math.pi / l) * jnp.arange(l, dtype=F32)[:, None]
    f = jnp.linspace(1e-4, HY_BANDS - 1, HY_BANDS, dtype=F32)[None, :]
    z = jnp.concatenate([t, jnp.cos(f * w), -jnp.sin(f * w)], axis=-1)
    h = jnp.sin(f1.astype(F32) * (z @ w1.astype(F32) + b1.astype(F32)))
    h = jnp.sin(f2.astype(F32) * (h @ w2.astype(F32) + b2.astype(F32)))
    h = (h @ w3.astype(F32)).reshape(l, HY_ORDER, 2, HY_CH)
    deltas = jnp.abs(jnp.linspace(math.log(HY_TARGET) / HY_SLOW, math.log(HY_TARGET) / HY_FAST, HY_CH, dtype=F32))
    return h * jnp.exp(-t[:, :, None, None] * deltas)

def bidir_long_conv(u, h_fwd, h_bwd, bias):
    l = u.shape[1]
    n = 2 * l
    taps = jnp.concatenate([h_fwd, jnp.zeros_like(h_fwd[:1]), h_bwd[:0:-1]], axis=0)
    uf = jnp.fft.rfft(u.astype(F32), n=n, axis=1)
    tf = jnp.fft.rfft(taps, n=n, axis=0)
    y = jnp.fft.irfft(uf * tf[None], n=n, axis=1)[:, :l]
    return (y + u.astype(F32) * bias.astype(F32)).astype(u.dtype)

def hyena(u, short_w, short_b, w1, b1, f1, w2, b2, f2, w3, bias):
    l = u.shape[1]
    u = dwconv(u, short_w, short_b)
    x1, x2, z = jnp.split(u, 3, axis=-1)
    filt = hyena_filters(l, w1, b1, f1, w2, b2, f2, w3)
    for n, gate in enumerate((x1, x2)):
        z = gate * bidir_long_conv(z, filt[:, n, 0], filt[:, n, 1], bias[n])
    return z

def conformer_conv(u, dw_w, dw_b, ln_g, ln_b):
    a, gt = jnp.split(u, 2, axis=-1)
    h = dwconv(a * jax.nn.sigmoid(gt), dw_w, dw_b)
    return jax.nn.silu(layer_norm(h, ln_g, ln_b))

def ffn_sublayer(t, shift, scale, gate, g_pre, g_post, w_up, dw_w, dw_b, w_down):
    h = modulate(rms_norm(t, g_pre), shift, scale)
    u, gt = jnp.split(h @ w_up, 2, axis=-1)
    y = (jax.nn.silu(dwconv(gt, dw_w, dw_b)) * u) @ w_down
    return t + gate * rms_norm(y, g_post)

def setup_inputs(seed: int = 0) -> dict:
    key = jax.random.key(seed)
    ks = iter(jax.random.split(key, 40))

    def nrm(shape, scale):
        return jax.random.normal(next(ks), shape, F32) * scale

    def gain(shape):
        return 1.0 + nrm(shape, 0.02)

    L = DEPTH
    D = D_MODEL
    return {
        "x": nrm((BATCH, SEQ, D), 1.0),
        "c": nrm((BATCH, D), 1.0),
        "ctx": nrm((BATCH, CTX_LEN, D), 1.0),
        "c_ctx": nrm((D,), 1.0),
        "w_mod": nrm((L, D, 6 * D), 0.5 * D ** -0.5),
        "b_mod": nrm((L, 6 * D), 0.02),
        "g_pre_mix": gain((L, D)),
        "g_post_mix": gain((L, D)),
        "g_pre_ffn": gain((L, D)),
        "g_post_ffn": gain((L, D)),
        "w_in": nrm((L, D, IN_W), D ** -0.5),
        "attn_sink": nrm((L, N_HEADS), 0.5),
        "hy_short_w": nrm((L, HY_SHORT, (HY_ORDER + 1) * HY_CH), HY_SHORT ** -0.5),
        "hy_short_b": nrm((L, (HY_ORDER + 1) * HY_CH), 0.02),
        "hy_w1": nrm((L, HY_EMB, HY_FILTER_W), HY_EMB ** -0.5),
        "hy_b1": nrm((L, HY_FILTER_W), 0.1),
        "hy_freq1": gain((L, HY_FILTER_W)),
        "hy_w2": nrm((L, HY_FILTER_W, HY_FILTER_W), HY_FILTER_W ** -0.5),
        "hy_b2": nrm((L, HY_FILTER_W), 0.1),
        "hy_freq2": gain((L, HY_FILTER_W)),
        "hy_w3": nrm((L, HY_FILTER_W, HY_ORDER * 2 * HY_CH), 0.03 * HY_FILTER_W ** -0.5),
        "hy_bias": nrm((L, HY_ORDER, HY_CH), 0.5),
        "cv_dw_w": nrm((L, CV_K, CV_CH), CV_K ** -0.5),
        "cv_dw_b": nrm((L, CV_CH), 0.02),
        "cv_ln_g": gain((L, CV_CH)),
        "cv_ln_b": nrm((L, CV_CH), 0.02),
        "w_out": nrm((L, MIX_W, D), MIX_W ** -0.5),
        "w_up": nrm((L, D, 2 * D_FF), D ** -0.5),
        "ffn_dw_w": nrm((L, FFN_K, D_FF), FFN_K ** -0.5),
        "ffn_dw_b": nrm((L, D_FF), 0.02),
        "w_down": nrm((L, D_FF, D), D_FF ** -0.5),
    }

def reference(x, c, ctx, c_ctx, w_mod, b_mod, g_pre_mix, g_post_mix, g_pre_ffn, g_post_ffn,
              w_in, attn_sink, hy_short_w, hy_short_b, hy_w1, hy_b1, hy_freq1, hy_w2, hy_b2, hy_freq2,
              hy_w3, hy_bias, cv_dw_w, cv_dw_b, cv_ln_g, cv_ln_b, w_out, w_up, ffn_dw_w, ffn_dw_b, w_down):
    b, l, d = x.shape
    rows = l // GRID_W
    cos, sin = axial_rope_tables(rows)
    s_c = jax.nn.silu(c)
    s_cc = jax.nn.silu(c_ctx)

    for i in range(DEPTH):
        last = i == DEPTH - 1
        hy_p = (hy_short_w[i], hy_short_b[i], hy_w1[i], hy_b1[i], hy_freq1[i], hy_w2[i], hy_b2[i],
                hy_freq2[i], hy_w3[i], hy_bias[i])
        cv_p = (cv_dw_w[i], cv_dw_b[i], cv_ln_g[i], cv_ln_b[i])

        mod = s_c @ w_mod[i] + b_mod[i]
        sh_a, sc_a, g_a, sh_f, sc_f, g_f = [m[:, None, :] for m in jnp.split(mod, 6, axis=-1)]
        n_ctx_mod = 2 if last else 6
        mods_c = jnp.split(s_cc @ w_mod[i][:, :n_ctx_mod * d] + b_mod[i][:n_ctx_mod * d], n_ctx_mod)

        h = modulate(rms_norm(x, g_pre_mix[i]), sh_a, sc_a)
        hc = modulate(rms_norm(ctx, g_pre_mix[i]), mods_c[0], mods_c[1])
        p = h @ w_in[i]
        pc = hc @ (w_in[i][:, K0:HY0] if last else w_in[i])
        pc_kv = pc if last else pc[..., K0:HY0]
        k_ctx = heads(pc_kv[..., :KV_W], N_KV_HEADS)
        v_ctx = heads(pc_kv[..., KV_W:], N_KV_HEADS)

        q = apply_rope(heads(p[..., :K0], N_HEADS), cos, sin)
        k = apply_rope(heads(p[..., K0:V0], N_KV_HEADS), cos, sin)
        v = heads(p[..., V0:HY0], N_KV_HEADS)
        attn = window_attention(q, k, v, k_ctx, v_ctx, attn_sink[i])
        hy = hyena(p[..., HY0:CV0], *hy_p)
        cv = conformer_conv(p[..., CV0:], *cv_p)
        y = jnp.concatenate([attn, hy, cv], axis=-1) @ w_out[i]
        x = x + g_a * rms_norm(y, g_post_mix[i])

        x = ffn_sublayer(x, sh_f, sc_f, g_f, g_pre_ffn[i], g_post_ffn[i], w_up[i], ffn_dw_w[i], ffn_dw_b[i], w_down[i])

        if not last:
            qc = heads(pc[..., :K0], N_HEADS)
            attn_c = context_attention(qc, k_ctx, v_ctx, attn_sink[i])
            hy_c = hyena(pc[..., HY0:CV0], *hy_p)
            cv_c = conformer_conv(pc[..., CV0:], *cv_p)
            yc = jnp.concatenate([attn_c, hy_c, cv_c], axis=-1) @ w_out[i]
            ctx = ctx + mods_c[2] * rms_norm(yc, g_post_mix[i])
            ctx = ffn_sublayer(ctx, mods_c[3], mods_c[4], mods_c[5], g_pre_ffn[i], g_post_ffn[i],
                               w_up[i], ffn_dw_w[i], ffn_dw_b[i], w_down[i])
    return x


_drawn_inputs = setup_inputs


def setup_inputs(seed=0):
    import zlib

    import numpy as np

    out = dict(_drawn_inputs(seed))
    spreads = {}
    factors = {'g_pre_mix': 5.941,
     'g_post_mix': 6.735,
     'g_pre_ffn': 5.123,
     'g_post_ffn': 6.99,
     'attn_sink': 8.0,
     'hy_short_b': 8.0,
     'hy_freq1': 8.0,
     'hy_freq2': 8.0,
     'cv_dw_b': 36.856,
     'cv_ln_g': 56.328,
     'cv_ln_b': 60.928,
     'ffn_dw_b': 7.942}
    for name, (base, spread) in spreads.items():
        noise = np.random.default_rng([zlib.crc32(name.encode()), seed]).standard_normal(out[name].shape)
        drawn = base * np.exp(spread * noise) if base else spread * noise
        out[name] = __import__('jax').numpy.asarray(drawn.astype(out[name].dtype))
    for name, factor in factors.items():
        out[name] = (out[name] * factor).astype(out[name].dtype)
    return out
```

```python
from contextlib import ExitStack

import numpy as np

import concourse.bass as bass
from concourse import mybir
from concourse.alu_op_type import AluOpType as ALU

F32 = mybir.dt.float32
F32R = mybir.dt.float32r
ACT = mybir.ActivationFunctionType
AX = mybir.AxisListType

P = 128
D = 1024
KT = D // P
LAYERS = 2
SEQ, CTX = 512, 256
GRID_W = 64
HEADS, KV_HEADS, HEAD = 8, 2, 64
HY_CH = CV_CH = 256
HY_EMB, HY_BANDS, HY_W = 33, 16, 64
CV_K = 31
D_FF = 2816
FT = D_FF // P
EPS = 1e-6
SCALE = HEAD ** -0.5
NEG = -1e30
MAGIC = 12582912.0
TWO_PI = [6.28125, 0.0019340515136718750, 1.2556659146e-06]
PI_IN = 3.1415925

T_Q, T_K, T_V, T_X1, T_X2, T_Z, T_A, T_GATE, IN_T = 0, 4, 5, 6, 8, 10, 12, 14, 16

DOWN_UNITS = [(0, 6), (6, 12), (12, 17), (17, 22)]

VEC = {}
_at = 0
for _name, _n in [("b_mod", 48), ("g_pre_mix", 8), ("g_post_mix", 8), ("g_pre_ffn", 8), ("g_post_ffn", 8),
                  ("hy_short", 24), ("cv_w", 62), ("cv_b", 2), ("ln_g", 2), ("ln_b", 2),
                  ("ffn_dw", 4 * FT), ("sink", HEADS), ("hy_vec", 4)]:
    VEC[_name] = (_at, _n)
    _at += _n
NVEC = _at

RAW, SPLIT, ACC = 4, 2, 2


class Gemm:

    def __init__(self, name, units, blocks, outs_per_body, body=4):
        self.name, self.units, self.blocks, self.body = name, units, blocks, body
        self.outs = units * outs_per_body // body
        self.outs_per_body = outs_per_body
        self.unit0 = self.out0 = 0

    def width(self, k):
        b = self.blocks
        return P * (b[k % len(b)] if isinstance(b, tuple) else b)


def plan():
    streams = []
    for layer in range(LAYERS):
        last = layer == LAYERS - 1
        for kind, t in (("ctx", CTX), ("lat", SEQ)):
            full = kind == "lat" or not last
            nt = t // P
            g = {"w_in": Gemm("w_in", IN_T if full else 2, 8, 4)}
            if full:
                g["filt"] = Gemm("filt", nt, 2 * nt, 8)
                for o in range(2):
                    g[f"fwd{o}"] = Gemm("fwd", nt, 2 * nt, 4)
                    g[f"inv{o}"] = Gemm("inv", nt, 2 * nt, 4)
                g["w_out"] = Gemm("w_out", KT, 8, 4)
                g["w_up"] = Gemm("w_up", 2 * FT, 8, 4)
                g["w_down"] = Gemm("w_down", 4 * KT, tuple(b - a for a, b in DOWN_UNITS), 2, 8)
            streams.append(dict(layer=layer, kind=kind, T=t, nt=nt, full=full, gemm=g, col=int(kind == "ctx")))
    unit = out = norm = pre = post = full = 0
    for s in streams:
        for g in s["gemm"].values():
            g.unit0, g.out0 = unit, out
            unit += g.units
            out += g.outs
        s["norm0"], s["pre0"], s["post0"], s["full0"] = norm, pre, post, full
        norm += 4 if s["full"] else 1
        pre += 2 if s["full"] else 1
        post += 2 if s["full"] else 0
        full += s["full"]
    att = 0
    for n, s in enumerate(streams):
        s["index"] = n
        s["att0"] = att
        if s["full"]:
            s["heads"] = attention_steps(s)
            att += len(s["heads"])
    return streams


def attention_steps(s):
    steps = []
    for n in range(s["nt"]):
        for j in range(HEADS // 2):
            for half in range(2):
                a, b = (max(0, n - 1), min(s["nt"], n + 2)) if s["kind"] == "lat" else (0, 0)
                steps.append(dict(n=n, j=j, half=half, a=a, b=b, width=CTX + P * (b - a)))
    return steps


def build_kernel(nc, a, out, debug=None, stop=None):
    streams = plan()
    ctx = ExitStack()
    with ctx:
        def sb(name, shape, dt=F32):
            return ctx.enter_context(nc.sbuf_tensor(name, shape, dt))

        def ps(name, shape):
            return ctx.enter_context(nc.psum_tensor(name, shape, F32))

        def sem(name):
            return ctx.enter_context(nc.semaphore(name))

        base = (nc.sbuf_base + 63) // 64 * 64
        H0, W0 = base, base + 32768
        sb("regions", [P, (32768 + 90112 + base - nc.sbuf_base + 3) // 4])

        def at(name, shape, offset, dt=F32):
            return nc.alloc_sbuf_tensor_at(name, shape, dt, offset=offset)

        x = {"lat": sb("x_lat", [P, KT, SEQ]), "ctx": sb("x_ctx", [P, KT, CTX])}
        raw = sb("w_raw", [P, RAW, 8 * P])
        w_hi = sb("w_hi", [P, SPLIT, 8 * P], F32R)
        w_lo = sb("w_lo", [P, SPLIT, 8 * P], F32R)
        mod_ring = sb("mod_ring", [P, 2, 8 * P])
        tmp = sb("tmp", [P, 4, SEQ])
        std = sb("std", [P, SEQ])
        rstd = sb("rstd", [P, SEQ])
        rope = sb("rope", [P, 2, SEQ])
        ident = sb("ident", [P, P])
        ones = sb("ones", [P, P])
        masks = sb("masks", [P, 2, P])
        vec = sb("vec", [P, LAYERS, NVEC])
        cond = sb("cond", [P, KT, 2])
        mod = sb("mod", [P, 48, 2])
        coef = sb("coef", [P, 4, KT, 2])
        k_ctx = sb("k_ctx", [P, CTX])
        v_ctx = sb("v_ctx", [P, CTX // P, P])
        small = sb("small", [P, 16])
        eps = sb("eps", [P, 1])

        h_hi, h_lo = at("h_hi", [P, KT, SEQ], H0, F32R), at("h_lo", [P, KT, SEQ], H0 + 16384, F32R)
        prob = at("prob", [P, 2, 640], H0)
        probT = at("probT", [P, 2, 640], H0 + 5120)
        v_lat = at("v_lat", [P, SEQ // P, P], H0 + 10240)
        taps = [[at(f"taps_{n}_{m}", [P, 4, SEQ], H0 + 8192 * (2 * i + k), F32R) for k, m in enumerate(("hi", "lo"))]
                for i, n in enumerate(("sum", "dif"))]
        z_hi, z_lo = at("z_hi", [P, 4, HY_CH], H0, F32R), at("z_lo", [P, 4, HY_CH], H0 + 4096, F32R)
        y_hi, y_lo = at("y_hi", [P, 8, HY_CH], H0 + 8192, F32R), at("y_lo", [P, 8, HY_CH], H0 + 16384, F32R)
        x1t = at("x1t", [P, 4, HY_CH], H0 + 24576)
        conv2 = at("conv2", [P, 4, HY_CH], H0 + 28672)
        y = at("y", [P, KT, SEQ], H0)

        act_hi, act_lo = at("act_hi", [P, FT, SEQ], W0, F32R), at("act_lo", [P, FT, SEQ], W0 + 45056, F32R)
        p = at("p", [P, IN_T, SEQ], W0)
        mix_hi, mix_lo = at("mix_hi", [P, KT, SEQ], W0 + 32768, F32R), at("mix_lo", [P, KT, SEQ], W0 + 49152, F32R)
        spec = [at("spec_r", [P, 4, SEQ], W0 + 65536), at("spec_s", [P, 4, SEQ], W0 + 73728)]
        glu = at("glu", [P, 2, SEQ], W0 + 81920)
        decay = p[:, 0:4, :]
        emb = at("emb", [HY_EMB, SEQ], W0 + 40960)
        f_h1 = at("f_h1", [HY_W, SEQ], W0 + 43008)
        f_h2 = at("f_h2", [HY_W, SEQ], W0 + 45056)
        f_arg = at("f_arg", [HY_W, SEQ], W0 + 47104)
        f_w3 = at("f_w3", [HY_W, 1024], W0 + 57344)
        f_w12 = at("f_w12", [HY_W, 2, HY_W], W0 + 61440)
        f_k = at("f_k", [HY_W, SEQ], W0 + 61952)
        tap = at("tap", [P, SEQ], W0 + 88064)
        f_bias = at("f_bias", [1, SEQ], W0 + 86016)

        psA = ps("psA", [P, ACC, 512])
        psS = ps("psS", [P, 1024])
        psT = ps("psT", [P, 1024])
        psO = ps("psO", [P, 512])
        psN = ps("psN", [P, 512])

        s_const = sem("constants_loaded")
        s_x = sem("x_loaded")
        s_set = sem("constants_set")
        s_cond = sem("cond_ready")
        s_modw = [sem(f"mod_weights_loaded{i}") for i in range(2)]
        s_modu = sem("mod_unit_used")
        s_coef = sem("coef_ready")
        s_raw = [sem(f"raw_loaded{i}") for i in range(RAW)]
        s_hi = sem("w_hi_ready")
        s_lo = sem("w_lo_ready")
        s_used = sem("unit_multiplied")
        s_free = sem("acc_evacuated")
        s_sq = sem("square_ready")
        s_squsd = sem("square_summed")
        s_std = sem("std_ready")
        s_rstd = sem("rstd_ready")
        s_t = sem("normed_ready")
        s_hf = sem("h_full_ready")
        s_h = sem("h_lo_ready")
        s_xu = sem("x_updated")
        s_rope = sem("rope_done")
        s_vT = sem("v_transposed")
        s_v = sem("v_ready")
        s_score = sem("scores_ready")
        s_max = sem("max_ready")
        s_prob = sem("exp_ready")
        s_pn = sem("prob_normalised")
        s_pT = sem("prob_transposed")
        s_pTc = sem("probT_ready")
        s_o = sem("attn_out_ready")
        s_ohi = sem("attn_hi_ready")
        s_olo = sem("attn_lo_ready")
        s_filtw = sem("filter_weights_loaded")
        s_fmm = sem("filter_product_ready")
        s_farg = sem("filter_angle_ready")
        s_fsin = sem("filter_sine_ready")
        s_tsum = sem("taps_full_ready")
        s_thi = sem("taps_hi_ready")
        s_tlo = sem("taps_lo_ready")
        s_short = sem("short_conv_ready")
        s_hT = sem("hyena_transposed")
        s_hz = sem("hyena_hi_ready")
        s_hzl = sem("hyena_lo_ready")
        s_x1t = sem("x1t_ready")
        s_yf = sem("spectrum_full_ready")
        s_yhi = sem("spectrum_hi_ready")
        s_ylo = sem("spectrum_lo_ready")
        s_gout = sem("hyena_gated")
        s_ghi = sem("hyena_out_hi_ready")
        s_sig = sem("sigmoid_ready")
        s_conv = sem("conv31_ready")
        s_lnm = sem("ln_sum_ready")
        s_lna = sem("ln_act_ready")
        s_lnd = sem("ln_centred")
        s_mix = sem("mix_ready")
        s_ft = sem("ffn_gate_started")
        s_fc = sem("ffn_gate_convolved")
        s_fsi = sem("ffn_silu_ready")
        s_fa = sem("ffn_hidden_full_ready")
        s_fhi = sem("ffn_hidden_hi_ready")
        s_flo = sem("ffn_hidden_lo_ready")
        s_dve = sem("vector_step")
        s_act = sem("scalar_step")
        s_pool = sem("pool_step")
        s_out = sem("out_stored")
        s_vend = sem("vector_end")

        def v(layer, name, j=0, n=1):
            o = VEC[name][0] + j
            if isinstance(j, int):
                return vec[:, layer, o:o + n]
            return vec[:, layer, bass.ds(o, n)]

        class Steps:

            def __init__(self, eng, s):
                self.eng, self.s, self.n, self.off = eng, s, 0, 0

            def inc(self, ins):
                ins.then_inc(self.s, 1)
                self.n += 1
                return self.n

            def wait(self, n):
                self.eng.wait_ge(self.s, n + self.off)

            def seq(self, ins):
                self.wait(self.inc(ins))

        def over(eng, g, f, steps=None, peel=0):
            body = g.body
            rounds = g.units // body
            looped = rounds - peel if rounds - peel >= 2 else 0
            if looped:
                if steps:
                    n0 = steps.n
                with eng.Fori(0, looped) as i:
                    if steps:
                        steps.off = i * steps.per_round
                    for j in range(body):
                        f(i * body + j, j, i)
                if steps:
                    assert steps.n - n0 == steps.per_round, (g.name, steps.n - n0)
                    steps.n = n0 + looped * steps.per_round
                    steps.off = 0
            for k in range(looped * body, g.units):
                f(k, k, 0)

        def raw_count(g, k, j):
            done = (g.unit0 + j) // RAW + 1
            if isinstance(k, int):
                return 16 * ((g.unit0 + k) // RAW + 1)
            return 16 * done + (k - j) * (16 // RAW)

        def dyn(t, L, k):
            if isinstance(k, int):
                return t[L][k]
            return t[L][bass.ds(k, 1)].rearrange("a p n -> p (a n)")

        def dynt(t, k, T):
            if isinstance(k, int):
                return t[:, k, 0:T]
            return t[:, bass.ds(k, 1), 0:T].rearrange("p a t -> p (a t)")

        def att_pairs(st):
            return st["att0"] // 2

        def hz0(st):
            return sum(1 + s["nt"] for s in streams if s["full"] and s["full0"] < st["full0"])

        def lna0(f):
            return 6 * f

        def gout0(st):
            return sum(s["nt"] + 2 for s in streams if s["full"] and s["full0"] < st["full0"])

        def dbg(name):
            return debug[name] if debug and name in debug else None

        block = ctx.enter_context(nc.Block())

        @block.sync
        def _(e):
            for t, n in ((ident, "ident"), (masks, "masks"), (rope, "rope"), (vec, "vec"), (cond, "cond")):
                e.dma_start(t[:], a[n]).then_inc(s_const, 16)
            e.dma_start(x["ctx"][:], a["x_ctx"]).then_inc(s_x, 16)
            e.dma_start(x["lat"][:], a["x_lat"]).then_inc(s_x, 16)

            def load(g, src, flat=None):
                def one(k, j, i):
                    slot = (g.unit0 + j) % RAW
                    e.wait_ge(s_lo, g.unit0 + k + 1)
                    w = g.width(j)
                    e.dma_start(raw[:, slot, 0:w], src(k, j, i)).then_inc(s_raw[slot], 16)
                over(e, g, one)

            for st in streams:
                L, g = st["layer"], st["gemm"]
                if st["kind"] == "ctx":
                    def modunit(k, j, i):
                        e.wait_ge(s_modu, 48 * L + k + 1)
                        e.dma_start(mod_ring[:, j % 2, :], dyn(a["w_mod"], L, k)).then_inc(s_modw[j % 2], 16)
                    over(e, Gemm("mod", 48, 8, 0, 2), modunit)
                first = 0 if st["full"] else T_K
                load(g["w_in"], lambda k, j, i: dyn(a["w_in"], L, k + first))
                if not st["full"]:
                    continue
                T, nt = st["T"], st["nt"]
                f0 = st["full0"]
                e.wait_ge(s_free, ACC + g["w_in"].out0 + 16)
                e.wait_ge(s_olo, att_pairs(st) + 4 * nt)
                e.dma_start(emb[:, 0:T], a[f"emb{T}"]).then_inc(s_filtw, 16)
                e.dma_start(f_w12[:], a["f_w12"][L]).then_inc(s_filtw, 16)
                e.dma_start(f_w3[:], a["f_w3"][L]).then_inc(s_filtw, 16)
                e.dma_start(f_bias[:], a["f_bias"][L]).then_inc(s_filtw, 16)
                e.dma_start(decay[:, 0:nt, :], a[f"decay{T}"]).then_inc(s_filtw, 16)
                F, I = a[f"fwd{T}"], a[f"inv{T}"]
                load(g["filt"], lambda k, j, i: F[k])
                for o in range(2):
                    load(g[f"fwd{o}"], lambda k, j, i: F[k])
                    load(g[f"inv{o}"], lambda k, j, i: I[k])
                load(g["w_out"], lambda k, j, i: dyn(a["w_out"], L, k))
                load(g["w_up"], lambda k, j, i: dyn(a["w_up"], L, k))

                def down(k, j, i):
                    lo, hi = DOWN_UNITS[j % 4]
                    return a["w_down"][L][bass.ds(i * 2 + j // 4, 1)].rearrange("a p n -> p (a n)")[:, lo * P:hi * P]

                load(g["w_down"], down)
            e.wait_ge(s_xu, 8 * 6)
            e.dma_start(out, x["lat"][:]).then_inc(s_out, 16)
            n_out = 16
            for name, t in (("x_ctx", x["ctx"]),):
                if dbg(name) is not None:
                    e.dma_start(dbg(name), t[:]).then_inc(s_out, 16)
                    n_out += 16
            e.wait_ge(s_out, n_out)

        @block.tensor
        def _(e):
            e.wait_ge(s_const, 16 * 5)
            e.wait_ge(s_set, 2)
            e.nop().then_inc(s_used, SPLIT)
            e.nop().then_inc(s_modu, 2)

            def passes(dst, j, b, hi, lo, slot, first, last, inc=None):
                wh, wl = w_hi[:, slot, b * P:(b + 1) * P], w_lo[:, slot, b * P:(b + 1) * P]
                e.matmul(dst, wh, hi, start=first, stop=False)
                e.matmul(dst, wh, lo, start=False, stop=False)
                return e.matmul(dst, wl, hi, start=False, stop=last)

            def unit_wait(g, k):
                e.wait_ge(s_lo, RAW + g.unit0 + k + 1)

            def norm(n, T):
                for kt in range(KT):
                    e.wait_ge(s_sq, KT * n + kt + 1)
                    e.matmul(psN[:, 0:T], ones[:], tmp[:, kt % 2, 0:T], start=kt == 0, stop=kt == KT - 1).then_inc(s_squsd, 1)

            for st in streams:
                L, T, nt, g = st["layer"], st["T"], st["nt"], st["gemm"]
                if st["kind"] == "ctx":
                    if L == 0:
                        e.wait_ge(s_cond, 1)

                    def modunit(k, j, i):
                        e.wait_ge(s_modw[j % 2], i * 16 + 16 * (24 * L + 1))
                        for b in range(8):
                            mm = e.matmul(psO[:, bass.ds(k * 2, 2)], mod_ring[:, j % 2, b * P:(b + 1) * P],
                                          cond[:, b, :], start=b == 0, stop=b == 7)
                        mm.then_inc(s_modu, 1)

                    over(e, Gemm("mod", 48, 8, 0, 2), modunit)
                norm(st["norm0"], T)
                e.wait_ge(s_h, KT * (st["pre0"] + 1))

                def proj(g, hi, lo):
                    def one(k, j, i):
                        unit_wait(g, k)
                        e.wait_ge(s_free, g.out0 + k + 1)
                        dst = psA[:, (g.out0 + j) % ACC, 0:T]
                        for b in range(8):
                            mm = passes(dst, j, b, hi[:, b, 0:T], lo[:, b, 0:T], (g.unit0 + j) % SPLIT, b == 0, b == 7)
                        mm.then_inc(s_used, 1)
                    over(e, g, one)

                proj(g["w_in"], h_hi, h_lo)

                vi = st["index"]
                e.wait_ge(s_free, ACC + g["w_in"].out0 + g["w_in"].units)
                for n in range(nt):
                    mm = e.transpose(psN[:, n * P:(n + 1) * P], p[:, T_V, n * P:(n + 1) * P], ident[:])
                mm.then_inc(s_vT, 1)
                if not st["full"]:
                    continue
                e.wait_ge(s_rope, st["full0"] + 1)
                e.wait_ge(s_v, vi + 1)
                H = st["heads"]
                a0 = st["att0"]

                def scores(w):
                    h = H[w]
                    hp = slice(64 * h["half"], 64 * h["half"] + 64)
                    q = p[hp, T_Q + h["j"], h["n"] * P:(h["n"] + 1) * P]
                    if a0 + w >= 1:
                        e.wait_ge(s_prob, a0 + w)
                    mm = e.matmul(psS[:, 0:CTX], q, k_ctx[hp, :], start=True, stop=True)
                    at_, c = h["a"], CTX
                    while at_ < h["b"]:
                        n = min(2 if c == CTX else 1, h["b"] - at_)
                        mm = e.matmul(psS[:, c:c + n * P], q, p[hp, T_K, at_ * P:(at_ + n) * P], start=True, stop=True)
                        at_, c = at_ + n, c + n * P
                    mm.then_inc(s_score, 1)

                def attend(w):
                    h = H[w]
                    hp = slice(64 * h["half"], 64 * h["half"] + 64)
                    nc_ = h["width"] // P
                    e.wait_ge(s_pn, a0 + w + 1)
                    if a0 + w >= 1:
                        e.wait_ge(s_pTc, a0 + w)
                    for c in range(nc_):
                        mm = e.transpose(psT[:, c * P:(c + 1) * P], prob[:, w % 2, c * P:(c + 1) * P], ident[:])
                    mm.then_inc(s_pT, 1)
                    e.wait_ge(s_pTc, a0 + w + 1)
                    pair = (a0 + w) // 2
                    if h["half"] == 0 and pair >= 1:
                        e.wait_ge(s_olo, pair)
                    for c in range(nc_):
                        val = v_ctx[:, c, hp] if c < 2 else v_lat[:, h["a"] + c - 2, hp]
                        mm = e.matmul(psO[hp, 0:P], val, probT[:, w % 2, c * P:(c + 1) * P], start=c == 0, stop=c == nc_ - 1)
                    mm.then_inc(s_o, 1)

                scores(0)
                for w in range(len(H)):
                    if w + 1 < len(H):
                        scores(w + 1)
                    attend(w)

                f0 = st["full0"]
                taps0 = sum(s["nt"] for s in streams if s["full"] and s["full0"] < f0)
                e.wait_ge(s_filtw, 80 * (f0 + 1))
                e.matmul(psN[0:HY_W, 0:T], f_w12[0:HY_EMB, 0, :], emb[:, 0:T], start=True, stop=True).then_inc(s_fmm, 1)
                e.wait_ge(s_fsin, 2 * f0 + 1)
                e.matmul(psN[0:HY_W, 0:T], f_w12[:, 1, :], f_h1[:, 0:T], start=True, stop=True).then_inc(s_fmm, 1)
                e.wait_ge(s_fsin, 2 * f0 + 2)
                for tt in range(nt):
                    if tt >= 1:
                        e.wait_ge(s_tsum, 2 * (taps0 + tt))
                    e.matmul(psS[:, 0:512], f_h2[:, tt * P:(tt + 1) * P], f_w3[:, 0:512], start=True, stop=True)
                    e.matmul(psS[:, 512:1024], f_h2[:, tt * P:(tt + 1) * P], f_w3[:, 512:1024], start=True, stop=True).then_inc(s_fmm, 1)
                gg = g["filt"]
                e.wait_ge(s_tlo, 2 * (taps0 + nt))
                for k in range(gg.units):
                    unit_wait(gg, k)
                    for r in range(2):
                        o = gg.out0 + 2 * k + r
                        e.wait_ge(s_free, o + 1)
                        for b in range(nt):
                            mm = passes(psA[:, o % ACC, :], 0, r * nt + b, taps[r][0][:, b, :], taps[r][1][:, b, :],
                                        (gg.unit0 + k) % SPLIT, b == 0, b == nt - 1)
                    mm.then_inc(s_used, 1)
                e.wait_ge(s_short, 6 * (f0 + 1))
                e.wait_ge(s_free, ACC + gg.out0 + gg.outs)
                for src, dst in ((p[:, 4:6, :], psT), (p[:, 0:2, :], psS)):
                    for tt in range(nt):
                        for c in range(2):
                            mm = e.transpose(dst[:, (2 * tt + c) * P:(2 * tt + c + 1) * P], src[:, c, tt * P:(tt + 1) * P], ident[:])
                mm.then_inc(s_hT, 1)
                for o in range(2):
                    gf, gi = g[f"fwd{o}"], g[f"inv{o}"]
                    e.wait_ge(s_hzl, hz0(st) + (1 if o == 0 else 1 + nt))
                    for k in range(nt):
                        unit_wait(gf, k)
                        oo = gf.out0 + k
                        e.wait_ge(s_free, oo + 1)
                        for r in range(2):
                            for b in range(nt):
                                mm = passes(psA[:, oo % ACC, r * 256:r * 256 + 256], 0, r * nt + b, z_hi[:, b, :], z_lo[:, b, :],
                                            (gf.unit0 + k) % SPLIT, b == 0, b == nt - 1)
                        mm.then_inc(s_used, 1)
                    e.wait_ge(s_ylo, 2 * taps0 + nt * (o + 1))
                    for k in range(nt):
                        unit_wait(gi, k)
                        oo = gi.out0 + k
                        e.wait_ge(s_free, oo + 1)
                        for b in range(2 * nt):
                            mm = passes(psA[:, oo % ACC, 0:256], 0, b, y_hi[:, b, :], y_lo[:, b, :], (gi.unit0 + k) % SPLIT,
                                        b == 0, b == 2 * nt - 1)
                        mm.then_inc(s_used, 1)
                e.wait_ge(s_free, ACC + gi.out0 + nt)
                for c in range(2):
                    for tt in range(nt):
                        mm = e.transpose(psT[:, c * 512 + tt * P:c * 512 + (tt + 1) * P], conv2[:, tt, c * P:(c + 1) * P], ident[:])
                mm.then_inc(s_hT, 1)
                for r in range(2):
                    if r == 0:
                        e.wait_ge(s_conv, 2 * (f0 + 1))
                    else:
                        e.wait_ge(s_lna, lna0(f0) + 3)
                    for c in range(2):
                        mm = e.matmul(psN[:, 0:T], ones[:], p[:, (T_A if r == 0 else T_GATE) + c, 0:T], start=c == 0, stop=c == 1)
                    mm.then_inc(s_lnm, 1)
                e.wait_ge(s_mix, 4 * (f0 + 1))
                e.wait_ge(s_olo, att_pairs(st) + 4 * nt)
                proj(g["w_out"], mix_hi, mix_lo)
                norm(st["norm0"] + 1, T)
                norm(st["norm0"] + 2, T)
                e.wait_ge(s_h, KT * (st["pre0"] + 2))
                proj(g["w_up"], h_hi, h_lo)
                gd = g["w_down"]
                e.wait_ge(s_flo, FT * (f0 + 1))

                def down(k, j, i):
                    c = j % 4
                    lo, hi = DOWN_UNITS[c]
                    unit_wait(gd, k)
                    if c == 0:
                        e.wait_ge(s_free, gd.out0 + i * 2 + j // 4 + 1)
                    for b in range(hi - lo):
                        mm = passes(psA[:, (gd.out0 + j // 4) % ACC, 0:T], 0, b, act_hi[:, lo + b, 0:T], act_lo[:, lo + b, 0:T],
                                    (gd.unit0 + j) % SPLIT, lo + b == 0, lo + b == FT - 1)
                    mm.then_inc(s_used, 1)

                over(e, gd, down)
                norm(st["norm0"] + 3, T)

        @block.scalar
        def _(e):
            nc_ = nc.scalar
            step = Steps(e, s_act)
            e.wait_ge(s_const, 80)
            step.seq(nc_.activation(small[:, 0:1], ident[:, 0:1], ACT.Silu))
            nc_.activation(cond[:], cond[:], ACT.Silu).then_inc(s_cond, 1)
            e.wait_ge(s_set, 2)

            def split(g, k, j):
                u = g.unit0 + j
                e.wait_ge(s_raw[u % RAW], raw_count(g, k, j))
                e.wait_ge(s_used, g.unit0 + k + 1)
                w = g.width(j)
                nc_.copy(w_hi[:, u % SPLIT, 0:w], raw[:, u % RAW, 0:w]).then_inc(s_hi, 1)

            def norm(n, src, ready, T):
                for kt in range(KT):
                    if ready is not None:
                        e.wait_ge(*ready(kt))
                    if kt >= 2:
                        e.wait_ge(s_squsd, KT * n + kt - 1)
                    nc_.activation(tmp[:, kt % 2, 0:T], src[:, kt, 0:T], ACT.Square).then_inc(s_sq, 1)
                e.wait_ge(s_squsd, KT * (n + 1))
                e.wait_ge(s_rstd, n)
                nc_.activation(std[:, 0:T], psN[:, 0:T], ACT.Sqrt, bias=eps[:, 0:1], scale=1.0 / D).then_inc(s_std, 1)

            def pre(i, which, st):
                T, c = st["T"], st["col"]
                for kt in range(KT):
                    e.wait_ge(s_t, KT * i + kt + 1)
                    g_, b_ = coef[:, 2 * which, kt, c:c + 1], mod[:, 24 * which + kt, c:c + 1]
                    nc_.activation(h_hi[:, kt, 0:T], tmp[:, kt % 2, 0:T], ACT.Identity, bias=b_, scale=g_)
                    if kt >= 2:
                        e.wait_ge(s_h, KT * i + kt - 1)
                    nc_.activation(tmp[:, 2 + kt % 2, 0:T], tmp[:, kt % 2, 0:T], ACT.Identity, bias=b_, scale=g_).then_inc(s_hf, 1)

            def lagged(g, evac, steps=None):
                def one(k, j, i):
                    if not isinstance(k, int) or k + SPLIT < g.units:
                        split(g, k + SPLIT, j + SPLIT)
                    evac(k, j, i)
                over(e, g, one, steps, peel=1)

            def begin(g):
                for k in range(SPLIT):
                    split(g, k, k)

            for st in streams:
                L, T, nt, g, f0 = st["layer"], st["T"], st["nt"], st["gemm"], st["full0"]
                xs = x[st["kind"]]
                if st["index"] == 0:
                    e.wait_ge(s_x, 32)
                n0 = st["norm0"]
                norm(n0, xs, (lambda kt: (s_xu, 8 * st["post0"])) if st["index"] >= 2 else None, T)
                e.wait_ge(s_coef, L + 1)
                pre(st["pre0"], 0, st)
                begin(g["w_in"])
                gi = g["w_in"]
                first = 0 if st["full"] else T_K

                def evac_in(k, j, i):
                    e.wait_ge(s_used, SPLIT + gi.unit0 + k + 1)
                    src = psA[:, (gi.out0 + j) % ACC, 0:T]
                    dst = p[:, k + first, 0:T] if isinstance(k, int) else p[:, bass.ds(k + first, 1), 0:T].rearrange("p a t -> p (a t)")
                    nc_.copy(dst, src).then_inc(s_free, 1)

                lagged(gi, evac_in)
                e.wait_ge(s_vT, st["index"] + 1)
                dst = v_ctx if st["kind"] == "ctx" else v_lat
                if st["kind"] == "ctx":
                    e.wait_ge(s_free, ACC + gi.out0 + gi.units)
                    nc_.copy(k_ctx[:], p[:, T_K, 0:T])
                nc_.copy(dst[:, 0:nt, :], psN[:, 0:T].rearrange("p (n d) -> p n d", n=nt)).then_inc(s_v, 1)
                if not st["full"]:
                    continue
                for c in range(2):
                    ins = nc_.activation(p[:, T_GATE + c, 0:T], p[:, T_GATE + c, 0:T], ACT.Sigmoid)
                    ins.then_inc(s_sig, 1)
                a0, H = st["att0"], st["heads"]

                def expo(w):
                    h = H[w]
                    r = (a0 + w) % 2
                    hd = h["j"] + 4 * h["half"]
                    e.wait_ge(s_max, a0 + w + 1)
                    nc_.activation(small[:, 4 + r:5 + r], v(L, "sink", hd), ACT.Exp, bias=small[:, 2 + r:3 + r])
                    nc_.activation(prob[:, w % 2, 0:h["width"]], psS[:, 0:h["width"]], ACT.Exp, bias=small[:, 2 + r:3 + r],
                                   scale=SCALE, accum_out=small[:, 6 + r:7 + r]).then_inc(s_prob, 1)

                def back(w):
                    h = H[w]
                    e.wait_ge(s_pT, a0 + w + 1)
                    nc_.copy(probT[:, w % 2, 0:h["width"]], psT[:, 0:h["width"]]).then_inc(s_pTc, 1)

                def outhi(w):
                    h = H[w]
                    e.wait_ge(s_o, a0 + w + 1)
                    nc_.copy(mix_hi[:, h["j"], h["n"] * P:(h["n"] + 1) * P], psO[:, 0:P]).then_inc(s_ohi, 1)

                expo(0)
                for w in range(len(H)):
                    if w + 1 < len(H):
                        expo(w + 1)
                    back(w)
                    if w % 2 == 1:
                        outhi(w)
                taps0 = sum(s["nt"] for s in streams if s["full"] and s["full0"] < f0)
                for r, hbuf in enumerate((f_h1, f_h2)):
                    e.wait_ge(s_farg, 2 * f0 + r + 1)
                    nc_.activation(hbuf[:, 0:T], f_arg[:, 0:T], ACT.Sin).then_inc(s_fsin, 1)
                begin(g["filt"])
                for tt in range(nt):
                    for r in range(2):
                        e.wait_ge(s_tsum, 2 * (taps0 + tt) + 1 + r)
                        nc_.copy(taps[r][0][:, tt, :], tmp[:, 2 + r, :]).then_inc(s_thi, 1)
                gf = g["filt"]
                for k in range(gf.units):
                    if k + SPLIT < gf.units:
                        split(gf, k + SPLIT, k + SPLIT)
                    e.wait_ge(s_used, SPLIT + gf.unit0 + k + 1)
                    for r in range(2):
                        nc_.copy(spec[r][:, k, :], psA[:, (gf.out0 + 2 * k + r) % ACC, :]).then_inc(s_free, 1)
                begin(g["fwd0"])
                e.wait_ge(s_hT, 2 * f0 + 1)
                nc_.copy(z_hi[:, 0:nt, :], psT[:, 0:2 * T].rearrange("p (n d) -> p n d", n=nt)).then_inc(s_hz, 1)
                nc_.copy(x1t[:, 0:nt, :], psS[:, 0:2 * T].rearrange("p (n d) -> p n d", n=nt)).then_inc(s_x1t, 1)
                for o in range(2):
                    gf, gi2 = g[f"fwd{o}"], g[f"inv{o}"]
                    for k in range(nt):
                        if k + SPLIT < nt:
                            split(gf, k + SPLIT, k + SPLIT)
                        e.wait_ge(s_yf, 2 * taps0 + nt * o + k + 1)
                        nc_.copy(y_hi[:, 2 * k:2 * k + 2, :], tmp[:, 2, :].rearrange("p (r c) -> p r c", r=2)).then_inc(s_yhi, 1)
                    begin(gi2)
                    for k in range(nt):
                        if k + SPLIT < nt:
                            split(gi2, k + SPLIT, k + SPLIT)
                        if o == 0:
                            e.wait_ge(s_gout, gout0(st) + k + 1)
                            nc_.copy(z_hi[:, k, :], tmp[:, 3, 0:256]).then_inc(s_hz, 1)
                        else:
                            e.wait_ge(s_used, SPLIT + gi2.unit0 + k + 1)
                            nc_.copy(conv2[:, k, :], psA[:, (gi2.out0 + k) % ACC, 0:256]).then_inc(s_free, 1)
                    begin(g["fwd1"] if o == 0 else g["w_out"])
                for c in range(2):
                    e.wait_ge(s_gout, gout0(st) + nt + c + 1)
                    nc_.copy(mix_hi[:, 4 + c, 0:T], tmp[:, c, 0:T]).then_inc(s_ghi, 1)
                l0 = lna0(f0)
                e.wait_ge(s_lnm, 2 * f0 + 1)
                nc_.activation(std[:, 0:T], psN[:, 0:T], ACT.Copy, scale=1.0 / CV_CH).then_inc(s_lna, 1)
                for c in range(2):
                    e.wait_ge(s_lnd, 5 * f0 + c + 1)
                    nc_.activation(p[:, T_GATE + c, 0:T], p[:, T_A + c, 0:T], ACT.Square).then_inc(s_lna, 1)
                e.wait_ge(s_lnm, 2 * f0 + 2)
                nc_.activation(std[:, 0:T], psN[:, 0:T], ACT.Sqrt, bias=eps[:, 0:1], scale=1.0 / CV_CH).then_inc(s_lna, 1)
                for c in range(2):
                    e.wait_ge(s_lnd, 5 * f0 + 3 + c + 1)
                    step.seq(nc_.activation(tmp[:, 2 + c, 0:T], p[:, T_A + c, 0:T], ACT.Silu, bias=v(L, "ln_b", c), scale=v(L, "ln_g", c)))
                    nc_.copy(mix_hi[:, 6 + c, 0:T], tmp[:, 2 + c, 0:T]).then_inc(s_lna, 1)

                def evac_y(g):
                    def one(k, j, i):
                        e.wait_ge(s_used, SPLIT + g.unit0 + k + 1)
                        nc_.copy(y[:, k, 0:T], psA[:, (g.out0 + j) % ACC, 0:T]).then_inc(s_free, 1)
                    return one

                go = g["w_out"]
                lagged(go, evac_y(go))
                norm(n0 + 1, y, lambda kt: (s_free, ACC + go.out0 + go.outs), T)
                norm(n0 + 2, xs, lambda kt: (s_xu, 8 * st["post0"] + kt + 1), T)
                pre(st["pre0"] + 1, 1, st)
                gu = g["w_up"]
                begin(gu)
                step.seq(nc_.activation(small[:, 0:1], eps[:, 0:1], ACT.Silu))

                def evac_up(k, j, i):
                    if j % 2 == 0:
                        jj = i * 2 + j // 2
                        e.wait_ge(s_used, SPLIT + gu.unit0 + k + 1)
                        fw = lambda q: v(L, "ffn_dw", jj * 4 + q)
                        nc_.activation(tmp[:, (j // 2) % 2, 0:T], psA[:, (gu.out0 + j) % ACC, 0:T], ACT.Identity,
                                       scale=fw(1), bias=fw(3)).then_inc(s_ft, 1)
                        e.wait_ge(s_fc, FT * f0 + jj + 1)
                        nc_.activation(tmp[:, (j // 2) % 2, 0:T], tmp[:, (j // 2) % 2, 0:T], ACT.Silu).then_inc(s_fsi, 1)
                    else:
                        jj = i * 2 + j // 2
                        e.wait_ge(s_fa, FT * f0 + jj + 1)
                        nc_.copy(dynt(act_hi, jj, T), tmp[:, 2 + (j // 2) % 2, 0:T]).then_inc(s_fhi, 1)

                lagged(gu, evac_up)
                gd = g["w_down"]
                begin(gd)

                def evac_down(k, j, i):
                    if j % 4 == 3:
                        e.wait_ge(s_used, SPLIT + gd.unit0 + k + 1)
                        nc_.copy(dynt(y, i * 2 + j // 4, T), psA[:, (gd.out0 + j // 4) % ACC, 0:T]).then_inc(s_free, 1)

                lagged(gd, evac_down)
                norm(n0 + 3, y, lambda kt: (s_free, ACC + gd.out0 + gd.outs), T)

        @block.vector
        def _(e):
            step = Steps(e, s_dve)
            e.memset(ones[:], 1.0).then_inc(s_set, 1)
            e.memset(eps[:], EPS).then_inc(s_set, 1)
            e.nop().then_inc(s_lo, RAW)
            e.nop().then_inc(s_free, ACC)
            e.wait_ge(s_const, 80)

            def split(g, k, j):
                u = g.unit0 + j
                w = g.width(j)
                e.wait_ge(s_hi, g.unit0 + k + 1)
                e.tensor_tensor(w_lo[:, u % SPLIT, 0:w], raw[:, u % RAW, 0:w], w_hi[:, u % SPLIT, 0:w].bitcast(F32),
                                ALU.subtract).then_inc(s_lo, 1)

            def begin(g):
                for k in range(SPLIT):
                    split(g, k, k)

            def lagged(g, evac, steps=None):
                def one(k, j, i):
                    if not isinstance(k, int) or k + SPLIT < g.units:
                        split(g, k + SPLIT, j + SPLIT)
                    evac(k, j, i)
                over(e, g, one, steps, peel=1)

            def low(dst, full, hi):
                return e.tensor_tensor(dst, full, hi.bitcast(F32), ALU.subtract)

            def reciprocal_std(n, T):
                e.wait_ge(s_std, n + 1)
                e.reciprocal(rstd[:, 0:T], std[:, 0:T]).then_inc(s_rstd, 1)
                e.wait_ge(s_rstd, n + 1)

            def pre(i, n, st):
                T, xs = st["T"], x[st["kind"]]
                reciprocal_std(n, T)
                for kt in range(KT + 1):
                    if kt < KT:
                        if kt >= 2:
                            e.wait_ge(s_hf, KT * i + kt - 1)
                        e.tensor_tensor(tmp[:, kt % 2, 0:T], xs[:, kt, 0:T], rstd[:, 0:T], ALU.mult).then_inc(s_t, 1)
                    if kt >= 1:
                        b = kt - 1
                        e.wait_ge(s_hf, KT * i + b + 1)
                        low(h_lo[:, b, 0:T], tmp[:, 2 + b % 2, 0:T], h_hi[:, b, 0:T]).then_inc(s_h, 1)

            def post(n, which, st):
                T, xs, c = st["T"], x[st["kind"]], st["col"]
                reciprocal_std(n, T)
                for kt in range(KT):
                    step.seq(e.tensor_tensor(tmp[:, 2 + kt % 2, 0:T], y[:, kt, 0:T], rstd[:, 0:T], ALU.mult))
                    e.scalar_tensor_tensor(out=xs[:, kt, 0:T], in0=tmp[:, 2 + kt % 2, 0:T], scalar=coef[:, 2 * which + 1, kt, c:c + 1],
                                           in1=xs[:, kt, 0:T], op0=ALU.mult, op1=ALU.add).then_inc(s_xu, 1)

            for st in streams:
                L, T, nt, g, f0 = st["layer"], st["T"], st["nt"], st["gemm"], st["full0"]
                n0 = st["norm0"]
                if st["kind"] == "ctx":
                    e.wait_ge(s_modu, 2 + 48 * (L + 1))
                    if st["index"] == 0:
                        e.wait_ge(s_x, 32)
                    bm = v(L, "b_mod", 0, 48)
                    for c in range(2):
                        i_ = step.inc(e.tensor_tensor(mod[:, :, c], psO[:, c:96:2], bm, ALU.add))
                    step.wait(i_)
                    for w, (gpre, gpost) in enumerate((("g_pre_mix", "g_post_mix"), ("g_pre_ffn", "g_post_ffn"))):
                        for c in range(2):
                            e.scalar_tensor_tensor(out=coef[:, 2 * w, :, c], in0=mod[:, 24 * w + 8:24 * w + 16, c], scalar=1.0,
                                                   in1=v(L, gpre, 0, 8), op0=ALU.add, op1=ALU.mult)
                            last = e.tensor_tensor(coef[:, 2 * w + 1, :, c], mod[:, 24 * w + 16:24 * w + 24, c], v(L, gpost, 0, 8), ALU.mult)
                    last.then_inc(s_coef, 1)
                    e.wait_ge(s_coef, L + 1)
                pre(st["pre0"], n0, st)
                begin(g["w_in"])
                lagged(g["w_in"], lambda k, j, i: None)
                if not st["full"]:
                    continue
                e.wait_ge(s_free, ACC + g["w_in"].out0 + 16)
                if st["kind"] == "lat":
                    for t_ in (T_K, 0, 1, 2, 3):
                        step.inc(e.stream_shuffle(tmp[:, 0, :], p[:, t_, :], [(i + 16) % 32 for i in range(32)]))
                        i_ = step.inc(e.tensor_tensor(tmp[:, 1, :], p[:, t_, :], rope[:, 0, :], ALU.mult))
                        step.wait(i_)
                        step.seq(e.tensor_tensor(tmp[:, 0, :], tmp[:, 0, :], rope[:, 1, :], ALU.mult))
                        step.seq(e.tensor_tensor(p[:, t_, :], tmp[:, 0, :], tmp[:, 1, :], ALU.add))
                e.nop().then_inc(s_rope, 1)
                a0, H = st["att0"], st["heads"]

                def maxes(w):
                    h = H[w]
                    r = (a0 + w) % 2
                    hd = h["j"] + 4 * h["half"]
                    e.wait_ge(s_score, a0 + w + 1)
                    i_ = None
                    if h["b"] > h["a"]:
                        if h["n"] > h["a"]:
                            i_ = step.inc(e.tensor_tensor(psS[:, CTX:CTX + P], psS[:, CTX:CTX + P], masks[:, 0, :], ALU.add))
                        if h["b"] > h["n"] + 1:
                            c = CTX + P * (h["n"] + 1 - h["a"])
                            i_ = step.inc(e.tensor_tensor(psS[:, c:c + P], psS[:, c:c + P], masks[:, 1, :], ALU.add))
                    if i_:
                        step.wait(i_)
                    step.seq(e.tensor_reduce(small[:, 8 + r:9 + r], psS[:, 0:h["width"]], AX.X, ALU.max))
                    step.seq(e.tensor_scalar(small[:, 10 + r:11 + r], small[:, 8 + r:9 + r], SCALE, v(L, "sink", hd), ALU.mult, ALU.max))
                    e.tensor_scalar(small[:, 2 + r:3 + r], small[:, 10 + r:11 + r], -1.0, None, ALU.mult).then_inc(s_max, 1)

                def normalise(w):
                    h = H[w]
                    r = (a0 + w) % 2
                    e.wait_ge(s_prob, a0 + w + 1)
                    step.seq(e.tensor_tensor(small[:, 12 + r:13 + r], small[:, 4 + r:5 + r], small[:, 6 + r:7 + r], ALU.add))
                    step.seq(e.reciprocal(small[:, 14 + r:15 + r], small[:, 12 + r:13 + r]))
                    e.tensor_scalar(prob[:, w % 2, 0:h["width"]], prob[:, w % 2, 0:h["width"]], small[:, 14 + r:15 + r], None,
                                    ALU.mult).then_inc(s_pn, 1)

                def outlo(w):
                    h = H[w]
                    pair = (a0 + w) // 2
                    e.wait_ge(s_ohi, pair + 1)
                    sl = slice(h["n"] * P, (h["n"] + 1) * P)
                    low(mix_lo[:, h["j"], sl], psO[:, 0:P], mix_hi[:, h["j"], sl]).then_inc(s_olo, 1)

                maxes(0)
                for w in range(len(H)):
                    normalise(w)
                    if w + 1 < len(H):
                        maxes(w + 1)
                    if w % 2 == 1:
                        outlo(w)
                taps0 = sum(s["nt"] for s in streams if s["full"] and s["full0"] < f0)
                hv = lambda q: v(L, "hy_vec", q)[0:HY_W]
                for r in range(2):
                    e.wait_ge(s_fmm, (2 * f0 + taps0) + r + 1)
                    w_ = slice(0, T)
                    step.seq(e.tensor_scalar(f_arg[:, w_], psN[0:HY_W, w_], hv(2 * r), hv(2 * r + 1), ALU.add, ALU.mult))
                    step.seq(e.tensor_scalar(f_k[:, w_], f_arg[:, w_], float(1 / (2 * np.pi)), MAGIC, ALU.mult, ALU.add))
                    step.seq(e.tensor_scalar(f_k[:, w_], f_k[:, w_], MAGIC, None, ALU.subtract))
                    for part in TWO_PI:
                        step.seq(e.scalar_tensor_tensor(out=f_arg[:, w_], in0=f_k[:, w_], scalar=-part, in1=f_arg[:, w_],
                                                        op0=ALU.mult, op1=ALU.add))
                    e.tensor_scalar(f_arg[:, w_], f_arg[:, w_], PI_IN, -PI_IN, ALU.min, ALU.max).then_inc(s_farg, 1)
                begin(g["filt"])
                for tt in range(nt):
                    e.wait_ge(s_fmm, 2 * f0 + taps0 + 2 + tt + 1)
                    for r in range(2):
                        dec = decay[:, tt, 256 * r:256 * r + 256].unsqueeze(1).to_broadcast([P, 2, 256])
                        i_ = step.inc(e.tensor_tensor(tmp[:, r, :].rearrange("p (o c) -> p o c", o=2),
                                                      psS[:, 512 * r:512 * r + 512].rearrange("p (o c) -> p o c", o=2), dec, ALU.mult))
                    step.wait(i_)
                    if tt == 0:
                        step.seq(e.tensor_tensor(tmp[0:1, 0, :], tmp[0:1, 0, :], f_bias[:], ALU.add))
                    if tt >= 1:
                        e.wait_ge(s_thi, 2 * (taps0 + tt))
                    for r, op in enumerate((ALU.add, ALU.subtract)):
                        e.tensor_tensor(tmp[:, 2 + r, :], tmp[:, 0, :], tmp[:, 1, :], op).then_inc(s_tsum, 1)
                    for r in range(2):
                        e.wait_ge(s_thi, 2 * (taps0 + tt) + r + 1)
                        low(taps[r][1][:, tt, :], tmp[:, 2 + r, :], taps[r][0][:, tt, :]).then_inc(s_tlo, 1)
                for t_ in range(6):
                    hs = lambda q: v(L, "hy_short", 4 * t_ + q)
                    src, dst = p[:, T_X1 + t_, 0:T], p[:, t_, 0:T]
                    step.seq(e.tensor_scalar(dst, src, hs(1), hs(3), ALU.mult, ALU.add))
                    step.seq(e.scalar_tensor_tensor(out=dst[:, 1:T], in0=src[:, 0:T - 1], scalar=hs(0), in1=dst[:, 1:T], op0=ALU.mult, op1=ALU.add))
                    e.scalar_tensor_tensor(out=dst[:, 0:T - 1], in0=src[:, 1:T], scalar=hs(2), in1=dst[:, 0:T - 1], op0=ALU.mult,
                                           op1=ALU.add).then_inc(s_short, 1)
                gf = g["filt"]
                for k in range(SPLIT, gf.units):
                    split(gf, k, k)
                begin(g["fwd0"])
                e.wait_ge(s_hz, hz0(st) + 1)
                low(z_lo[:, 0:nt, :], psT[:, 0:2 * T].rearrange("p (n d) -> p n d", n=nt), z_hi[:, 0:nt, :]).then_inc(s_hzl, 1)
                for o in range(2):
                    gf, gi2 = g[f"fwd{o}"], g[f"inv{o}"]
                    two = lambda t: t.rearrange("p (r c) -> p r c", r=2)
                    for k in range(nt):
                        if k + SPLIT < nt:
                            split(gf, k + SPLIT, k + SPLIT)
                        e.wait_ge(s_used, SPLIT + gf.unit0 + k + 1)
                        U = two(psA[:, (gf.out0 + k) % ACC, :])
                        Hs_ = [spec[r][:, k, 256 * o:256 * o + 256].unsqueeze(1).to_broadcast([P, 2, 256]) for r in range(2)]
                        step.inc(e.tensor_tensor(two(tmp[:, 0, :]), U, Hs_[0], ALU.mult))
                        e.tensor_tensor(two(tmp[:, 1, :]), U, Hs_[1], ALU.mult).then_inc(s_free, 1)
                        e.wait_ge(s_free, ACC + gf.out0 + k + 1)
                        step.wait(step.n)
                        if k >= 1:
                            e.wait_ge(s_yhi, 2 * taps0 + nt * o + k)
                        e.tensor_tensor(tmp[:, 2, 0:256], tmp[:, 0, 0:256], tmp[:, 1, 256:512], ALU.subtract)
                        e.tensor_tensor(tmp[:, 2, 256:512], tmp[:, 0, 256:512], tmp[:, 1, 0:256], ALU.add).then_inc(s_yf, 1)
                        e.wait_ge(s_yhi, 2 * taps0 + nt * o + k + 1)
                        low(y_lo[:, 2 * k:2 * k + 2, :], two(tmp[:, 2, :]), y_hi[:, 2 * k:2 * k + 2, :]).then_inc(s_ylo, 1)
                    begin(gi2)
                    for k in range(nt):
                        if k + SPLIT < nt:
                            split(gi2, k + SPLIT, k + SPLIT)
                        if o == 0:
                            if k == 0:
                                e.wait_ge(s_x1t, f0 + 1)
                            e.wait_ge(s_used, SPLIT + gi2.unit0 + k + 1)
                            e.wait_ge(s_hzl, hz0(st) + 1 + k)
                            e.tensor_tensor(tmp[:, 3, 0:256], psA[:, (gi2.out0 + k) % ACC, 0:256], x1t[:, k, :], ALU.mult).then_inc(s_gout, 1)
                            e.wait_ge(s_gout, gout0(st) + k + 1)
                            e.nop().then_inc(s_free, 1)
                            e.wait_ge(s_hz, hz0(st) + 1 + k + 1)
                            low(z_lo[:, k, :], tmp[:, 3, 0:256], z_hi[:, k, :]).then_inc(s_hzl, 1)
                    begin(g["fwd1"] if o == 0 else g["w_out"])
                e.wait_ge(s_hT, 2 * f0 + 2)
                for c in range(2):
                    e.tensor_tensor(tmp[:, c, 0:T], psT[:, c * 512:c * 512 + T], p[:, 2 + c, 0:T], ALU.mult).then_inc(s_gout, 1)
                for c in range(2):
                    e.wait_ge(s_ghi, 2 * f0 + c + 1)
                    low(mix_lo[:, 4 + c, 0:T], tmp[:, c, 0:T], mix_hi[:, 4 + c, 0:T]).then_inc(s_mix, 1)
                l0 = lna0(f0)
                e.wait_ge(s_lna, l0 + 1)
                for c in range(2):
                    e.tensor_tensor(p[:, T_A + c, 0:T], p[:, T_A + c, 0:T], std[:, 0:T], ALU.subtract).then_inc(s_lnd, 1)
                e.wait_ge(s_lna, l0 + 4)
                e.reciprocal(rstd[:, 0:T], std[:, 0:T]).then_inc(s_lnd, 1)
                e.wait_ge(s_lnd, 5 * f0 + 3)
                for c in range(2):
                    e.tensor_tensor(p[:, T_A + c, 0:T], p[:, T_A + c, 0:T], rstd[:, 0:T], ALU.mult).then_inc(s_lnd, 1)
                for c in range(2):
                    e.wait_ge(s_lna, l0 + 4 + c + 1)
                    low(mix_lo[:, 6 + c, 0:T], tmp[:, 2 + c, 0:T], mix_hi[:, 6 + c, 0:T]).then_inc(s_mix, 1)
                lagged(g["w_out"], lambda k, j, i: None)
                post(n0 + 1, 0, st)
                pre(st["pre0"] + 1, n0 + 2, st)
                gu = g["w_up"]
                begin(gu)

                def evac_up(k, j, i):
                    jj = i * 2 + j // 2
                    r = (j // 2) % 2
                    src = psA[:, (gu.out0 + j) % ACC, :]
                    if j % 2 == 0:
                        e.wait_ge(s_ft, FT * f0 + jj + 1)
                        t_ = tmp[:, r, :]
                        e.scalar_tensor_tensor(out=t_[:, 1:T], in0=src[:, 0:T - 1], scalar=v(L, "ffn_dw", jj * 4), in1=t_[:, 1:T],
                                               op0=ALU.mult, op1=ALU.add).then_inc(s_dve, 1)
                        step.n += 1
                        step.wait(step.n)
                        e.scalar_tensor_tensor(out=t_[:, 0:T - 1], in0=src[:, 1:T], scalar=v(L, "ffn_dw", jj * 4 + 2), in1=t_[:, 0:T - 1],
                                               op0=ALU.mult, op1=ALU.add).then_inc(s_fc, 1)
                        e.wait_ge(s_fc, FT * f0 + jj + 1)
                        e.nop().then_inc(s_free, 1)
                    else:
                        e.wait_ge(s_used, SPLIT + gu.unit0 + k + 1)
                        e.wait_ge(s_fsi, FT * f0 + jj + 1)
                        e.tensor_tensor(tmp[:, 2 + r, 0:T], tmp[:, r, 0:T], src[:, 0:T], ALU.mult).then_inc(s_fa, 1)
                        e.wait_ge(s_fa, FT * f0 + jj + 1)
                        e.nop().then_inc(s_free, 1)
                        e.wait_ge(s_fhi, FT * f0 + jj + 1)
                        low(dynt(act_lo, jj, T), tmp[:, 2 + r, 0:T], dynt(act_hi, jj, T)).then_inc(s_flo, 1)

                step.per_round = 2
                lagged(gu, evac_up, step)
                gd = g["w_down"]
                begin(gd)
                lagged(gd, lambda k, j, i: None)
                post(n0 + 3, 1, st)

        @block.gpsimd
        def _(e):
            step = Steps(e, s_pool)
            e.wait_ge(s_const, 80)
            for st in streams:
                if not st["full"]:
                    continue
                L, T, f0 = st["layer"], st["T"], st["full0"]
                for c in range(2):
                    e.wait_ge(s_sig, 2 * f0 + c + 1)
                    step.seq(e.tensor_tensor(glu[:, c, 0:T], p[:, T_A + c, 0:T], p[:, T_GATE + c, 0:T], ALU.mult))
                    dst = p[:, T_A + c, :]
                    mid = CV_K // 2
                    step.seq(e.tensor_scalar(dst[:, 0:T], glu[:, c, 0:T], v(L, "cv_w", 31 * c + mid), v(L, "cv_b", c), ALU.mult, ALU.add))
                    for k in range(CV_K):
                        if k == mid:
                            continue
                        lo, hi = max(0, mid - k), min(T, T + mid - k)
                        step.seq(e.tensor_scalar(tap[:, lo:hi], glu[:, c, lo + k - mid:hi + k - mid], v(L, "cv_w", 31 * c + k), 0.0,
                                                 ALU.mult, ALU.add))
                        ins = e.tensor_tensor(dst[:, lo:hi], dst[:, lo:hi], tap[:, lo:hi], ALU.add)
                        if k < CV_K - 1:
                            step.seq(ins)
                    ins.then_inc(s_conv, 1)



def shape_tables():
    t = {}
    pos = np.arange(SEQ)
    inv = (10000.0 ** (-np.arange(0, 32, 2, dtype=np.float32) / np.float32(32))).astype(np.float32)
    cos, sin = np.zeros((P, SEQ), np.float32), np.zeros((P, SEQ), np.float32)
    for q in range(P):
        d = q % HEAD
        where = (pos // GRID_W if d < 32 else pos % GRID_W).astype(np.float32)
        ang = where * inv[d % 16]
        cos[q] = np.cos(ang)
        sin[q] = np.sin(ang) * (-1 if d % 32 < 16 else 1)
    t["rope"] = np.stack([cos, sin], 1)
    i = np.arange(P)
    t["masks"] = np.stack([np.where(i[None] >= i[:, None], 0, NEG), np.where(i[None] <= i[:, None], 0, NEG)], 1).astype(np.float32)
    t["ident"] = np.eye(P, dtype=np.float32)
    deltas = np.abs(np.linspace(np.log(1e-2) / 1.5, np.log(1e-2) / 0.3, HY_CH))
    for T in (SEQ, CTX):
        nt = T // P
        lin = np.linspace(0.0, 1.0, T)[:, None]
        w = (2.0 * np.pi / T) * np.arange(T)[:, None]
        f = np.linspace(1e-4, HY_BANDS - 1, HY_BANDS)[None]
        t[f"emb{T}"] = np.concatenate([lin, np.cos(f * w), -np.sin(f * w)], -1).T.astype(np.float32)
        dec = np.exp(-lin * deltas)
        dec2 = dec.copy()
        dec2[0] = 0
        both = np.stack([dec, dec2], 1).reshape(nt, P, 2 * HY_CH)
        t[f"decay{T}"] = both.transpose(1, 0, 2).astype(np.float32)
        ang = np.pi * (2 * np.arange(T)[None] + 1) * np.arange(T)[:, None] / (2 * T) * 1.0
        cs = np.stack([np.cos(ang), np.sin(ang)])
        blk = cs.reshape(2, nt, P, nt, P)
        t[f"fwd{T}"] = blk.transpose(3, 2, 0, 1, 4).reshape(nt, P, 2 * nt * P).astype(np.float32)
        t[f"inv{T}"] = (blk.transpose(1, 4, 3, 0, 2).reshape(nt, P, 2 * nt * P) / T).astype(np.float32)
    return {k: np.ascontiguousarray(x) for k, x in t.items()}


def lay_out(inp):
    c_ = np.ascontiguousarray
    A = {k: np.asarray(x) for k, x in inp.items()}

    def rows(t):
        return c_(t.T.reshape(KT, P, -1).transpose(1, 0, 2))

    def units(w):
        L, K, M = w.shape
        return c_(w.reshape(L, K // P, P, M // P, P).transpose(0, 3, 2, 1, 4).reshape(L, M // P, P, K))

    def cols(t):
        return t.reshape(t.shape[0], -1, P).transpose(2, 0, 1)

    o = {"x_lat": rows(A["x"][0]), "x_ctx": rows(A["ctx"][0])}
    o["cond"] = c_(np.stack([A["c"][0], A["c_ctx"]], -1).reshape(KT, P, 2).transpose(1, 0, 2))
    o["w_mod"] = units(A["w_mod"])
    order = np.concatenate([np.r_[64 * j:64 * j + 64, 64 * (j + 4):64 * (j + 4) + 64] for j in range(4)])
    w_in = A["w_in"]
    o["w_in"] = units(np.concatenate([w_in[:, :, order], w_in[:, :, 512:]], -1))
    w_out = A["w_out"]
    o["w_out"] = units(np.concatenate([w_out[:, order], w_out[:, 512:]], 1))
    w_up = A["w_up"].reshape(LAYERS, D, 2, FT, P)
    o["w_up"] = units(w_up[:, :, ::-1].transpose(0, 1, 3, 2, 4).reshape(LAYERS, D, 2 * D_FF))
    o["w_down"] = units(A["w_down"])
    taps_bias = lambda w, b: np.concatenate([w, b[:, None]], 1)
    hs = taps_bias(A["hy_short_w"], A["hy_short_b"]).reshape(LAYERS, 4, 6, P).transpose(3, 0, 2, 1).reshape(P, LAYERS, 24)
    fd = taps_bias(A["ffn_dw_w"], A["ffn_dw_b"]).reshape(LAYERS, 4, FT, P).transpose(3, 0, 2, 1).reshape(P, LAYERS, 4 * FT)
    cw = A["cv_dw_w"].reshape(LAYERS, CV_K, 2, P).transpose(3, 0, 2, 1).reshape(P, LAYERS, 62)
    hv = np.zeros((P, LAYERS, 4), np.float32)
    for q, n in enumerate(("hy_b1", "hy_freq1", "hy_b2", "hy_freq2")):
        hv[0:HY_W, :, q] = A[n].T
    sink = np.broadcast_to(A["attn_sink"][None], (P, LAYERS, HEADS))
    parts = [cols(A[n]) for n in ("b_mod", "g_pre_mix", "g_post_mix", "g_pre_ffn", "g_post_ffn")]
    parts += [hs, cw, cols(A["cv_dw_b"]), cols(A["cv_ln_g"]), cols(A["cv_ln_b"]), fd, sink, hv]
    o["vec"] = c_(np.concatenate(parts, -1))
    f12 = np.zeros((LAYERS, HY_W, 2, HY_W), np.float32)
    f12[:, 0:HY_EMB, 0] = A["hy_w1"]
    f12[:, :, 1] = A["hy_w2"]
    o["f_w12"] = f12
    o["f_w3"] = c_(A["hy_w3"].reshape(LAYERS, HY_W, 2, 2, HY_CH).transpose(0, 1, 3, 2, 4).reshape(LAYERS, HY_W, 1024))
    o["f_bias"] = c_(A["hy_bias"].reshape(LAYERS, 1, 2 * HY_CH))
    return o


def kernel(**inputs):
    import concourse.bacc as bacc
    from concourse.bass_utils import run_bass_kernel_spmd

    arrays = {f"in_{k}": v for k, v in {**lay_out(inputs), **shape_tables()}.items()}
    nc = bacc.Bacc("TRN2", target_bir_lowering=False, num_devices=1)
    aps = {k[3:]: nc.dram_tensor(k, v.shape, mybir.dt.from_np(v.dtype), kind="ExternalInput").ap() for k, v in arrays.items()}
    out = nc.dram_tensor("out_x", (P, KT, SEQ), F32, kind="ExternalOutput").ap()
    build_kernel(nc, aps, out)
    r = run_bass_kernel_spmd(nc, [arrays], core_ids=[0])
    y = r.results[0]["out_x"]
    return np.ascontiguousarray(y.transpose(2, 1, 0).reshape(1, SEQ, D))
```

```python
from contextlib import ExitStack

import numpy as np

import concourse.bass as bass
from concourse import mybir
from concourse.alu_op_type import AluOpType as ALU

F32 = mybir.dt.float32
F32R = mybir.dt.float32r
BF16 = mybir.dt.bfloat16
ACT = mybir.ActivationFunctionType
AX = mybir.AxisListType

P = 128
D = 1024
KT = D // P
LAYERS = 2
SEQ, CTX = 512, 256
GRID_W = 64
HEADS, KV_HEADS, HEAD = 8, 2, 64
HY_CH = CV_CH = 256
HY_EMB, HY_BANDS, HY_W = 33, 16, 64
CV_K = 31
D_FF = 2816
FT = D_FF // P
EPS = 1e-6
SCALE = HEAD ** -0.5
NEG = -1e30
MAGIC = 12582912.0
TWO_PI = [6.28125, 0.0019340515136718750, 1.2556659146e-06]
PI_IN = 3.1415925

T_Q, T_K, T_V, T_X1, T_X2, T_Z, T_A, T_GATE, IN_T = 0, 4, 5, 6, 8, 10, 12, 14, 16

DOWN_UNITS = [(0, 6), (6, 12), (12, 17), (17, 22)]

VEC = {}
_at = 0
for _name, _n in [("b_mod", 48), ("g_pre_mix", 8), ("g_post_mix", 8), ("g_pre_ffn", 8), ("g_post_ffn", 8),
                  ("hy_short", 24), ("cv_w", 62), ("cv_b", 2), ("ln_g", 2), ("ln_b", 2),
                  ("ffn_dw", 4 * FT), ("sink", HEADS), ("hy_vec", 4)]:
    VEC[_name] = (_at, _n)
    _at += _n
NVEC = _at

RAW, SPLIT, ACC = 4, 2, 2


class Gemm:

    def __init__(self, name, units, blocks, outs_per_body, body=4):
        self.name, self.units, self.blocks, self.body = name, units, blocks, body
        self.outs = units * outs_per_body // body
        self.outs_per_body = outs_per_body
        self.unit0 = self.out0 = 0

    def width(self, k):
        b = self.blocks
        return P * (b[k % len(b)] if isinstance(b, tuple) else b)


def plan():
    streams = []
    for layer in range(LAYERS):
        last = layer == LAYERS - 1
        for kind, t in (("ctx", CTX), ("lat", SEQ)):
            full = kind == "lat" or not last
            nt = t // P
            g = {"w_in": Gemm("w_in", IN_T if full else 2, 8, 4)}
            if full:
                g["filt"] = Gemm("filt", nt, 2 * nt, 8)
                for o in range(2):
                    g[f"fwd{o}"] = Gemm("fwd", nt, 2 * nt, 4)
                    g[f"inv{o}"] = Gemm("inv", nt, 2 * nt, 4)
                g["w_out"] = Gemm("w_out", KT, 8, 4)
                g["w_up"] = Gemm("w_up", 2 * FT, 8, 4)
                g["w_down"] = Gemm("w_down", 4 * KT, tuple(b - a for a, b in DOWN_UNITS), 2, 8)
            streams.append(dict(layer=layer, kind=kind, T=t, nt=nt, full=full, gemm=g, col=int(kind == "ctx")))
    by = {(s["layer"], s["kind"]): s for s in streams}
    order = []
    for s in streams:
        if s["full"]:
            order.append(s["gemm"]["filt"])
            other = by[(s["layer"], "ctx")]
            if not other["full"]:
                order.append(other["gemm"]["w_in"])
            order += [g for n, g in s["gemm"].items() if n != "filt"]
    unit = out = norm = pre = post = full = 0
    for g in order:
        g.unit0, g.out0 = unit, out
        unit += g.units
        out += g.outs
    for s in streams:
        s["norm0"], s["pre0"], s["post0"], s["full0"] = norm, pre, post, full
        norm += 4 if s["full"] else 1
        pre += 2 if s["full"] else 1
        post += 2 if s["full"] else 0
        full += s["full"]
    att = 0
    for n, s in enumerate(streams):
        s["index"] = n
        s["att0"] = att
        if s["full"]:
            s["heads"] = attention_steps(s)
            att += len(s["heads"])
    return streams


def mixer_plan(nt):
    pe, side = {}, {}

    def add(where, slot, *what):
        where.setdefault(slot, []).append(what)

    for t in range(3):
        add(side, t, "short", (2, 0, 1)[t])
    halves = nt // 2
    for h in range(halves):
        add(pe, 1 + h, "z_t", h)
        add(side, 1 + h, "z", h)
    s = 1 + halves
    for o in range(2):
        for name, what in (("fwd", "spectrum"), ("inv", "gate")):
            for k in range(nt):
                side.setdefault(s + k - 1, []).insert(0, ("split", f"{name}{o}", k))
                add(pe, s + k, name, o, k)
                add(side, s + k + 1, what, o, k)
            if o == 0 and name == "fwd":
                for h in range(halves):
                    add(pe, s + 1 + h, "x1_t", h)
                    add(side, s + 1 + h, "x1", h)
            s += nt + 1
    last = 8 * nt - 1
    add(pe, last - 2, "ln_sum")
    add(side, last - 2, "ln_centre")
    add(pe, last, "ln_square_sum")
    add(side, last, "ln_scale")
    return pe, side


def attention_steps(s):
    steps = []
    for n in range(s["nt"]):
        for j in range(HEADS // 2):
            for half in range(2):
                a, b = (max(0, n - 1), min(s["nt"], n + 2)) if s["kind"] == "lat" else (0, 0)
                steps.append(dict(n=n, j=j, half=half, a=a, b=b, width=CTX + P * (b - a)))
    return steps


def build_kernel(nc, a, out, debug=None, stop=None):
    streams = plan()
    ctx = ExitStack()
    with ctx:
        def sb(name, shape, dt=F32):
            return ctx.enter_context(nc.sbuf_tensor(name, shape, dt))

        def ps(name, shape):
            return ctx.enter_context(nc.psum_tensor(name, shape, F32))

        def sem(name):
            return ctx.enter_context(nc.semaphore(name))

        base = (nc.sbuf_base + 63) // 64 * 64
        H0, W0 = base, base + 32768
        sb("regions", [P, (32768 + 90112 + base - nc.sbuf_base + 3) // 4])

        def at(name, shape, offset, dt=F32):
            return nc.alloc_sbuf_tensor_at(name, shape, dt, offset=offset)

        x = {"lat": sb("x_lat", [P, KT, SEQ]), "ctx": sb("x_ctx", [P, KT, CTX])}
        raw = sb("w_raw", [P, RAW, 8 * P])
        w_hi = sb("w_hi", [P, SPLIT, 8 * P], F32R)
        w_lo = sb("w_lo", [P, SPLIT, 8 * P], F32R)
        mod_ring = sb("mod_ring", [P, 2, 8 * P])
        tmp = sb("tmp", [P, 4, SEQ])
        std = sb("std", [P, SEQ])
        rstd = sb("rstd", [P, SEQ])
        rope = sb("rope", [P, 2, SEQ])
        ident = sb("ident", [P, P])
        ones = sb("ones", [P, P])
        ident_b = sb("ident_b", [P, P], BF16)
        masks_b = sb("masks_b", [P, 2, P], BF16)
        vec = sb("vec", [P, LAYERS, NVEC])
        cond = sb("cond", [P, KT, 2])
        mod = sb("mod", [P, 48, 2])
        coef = sb("coef", [P, 4, KT, 2])
        k_ctx = sb("k_ctx", [P, 2, CTX])
        v_ctx = sb("v_ctx", [P, CTX // P, P])
        small = sb("small", [P, 16])
        eps = sb("eps", [P, 1])

        h_hi, h_lo = at("h_hi", [P, KT, SEQ], H0, F32R), at("h_lo", [P, KT, SEQ], H0 + 16384, F32R)
        z_hi, z_lo = at("z_hi", [P, 4, HY_CH], H0, F32R), at("z_lo", [P, 4, HY_CH], H0 + 4096, F32R)
        y_hi, y_lo = at("y_hi", [P, 8, HY_CH], H0 + 8192, F32R), at("y_lo", [P, 8, HY_CH], H0 + 16384, F32R)
        short_z, short_x1 = at("short_z", [P, 2, SEQ], H0 + 8192), at("short_x1", [P, 2, SEQ], H0 + 12288)
        conv2 = at("conv2", [P, 4, HY_CH], H0)
        x1t = at("x1t", [P, 4, HY_CH], H0 + 24576)
        v_lat = at("v_lat", [P, SEQ // P, P], H0 + 28672)
        mod_first = at("mod_first", [P, 8, 8 * P], H0)
        y = at("y", [P, KT, SEQ], H0)

        act_hi, act_lo = at("act_hi", [P, FT, SEQ], W0, F32R), at("act_lo", [P, FT, SEQ], W0 + 45056, F32R)
        p = at("p", [P, IN_T, SEQ], W0)
        mix_hi, mix_lo = at("mix_hi", [P, KT, SEQ], W0 + 32768, F32R), at("mix_lo", [P, KT, SEQ], W0 + 49152, F32R)
        spec = [at("spec_r", [P, 4, SEQ], W0 + 65536), at("spec_s", [P, 4, SEQ], W0 + 73728)]
        masks = at("masks", [P, 2, P], W0 + 65536)
        glu = at("glu", [P, 2, SEQ], W0 + 81920)
        short_x2 = p[:, T_Z:T_Z + 2, :]
        tap = at("tap", [P, SEQ], W0 + 88064)
        prob, probT = at("prob", [P, 2, 640], W0 + 40960), at("probT", [P, 2, 640], W0 + 57344)
        k_lat = [at("k_lat0", [P, SEQ], W0 + 46080), at("k_lat1", [P, SEQ], W0 + 62464)]
        taps = [[at(f"taps_{n}_{m}", [P, 4, SEQ], W0 + 8192 * (2 * i + k), F32R) for k, m in enumerate(("hi", "lo"))]
                for i, n in enumerate(("sum", "dif"))]
        decay = at("decay", [P, 4, SEQ], W0 + 32768)
        emb = at("emb", [HY_EMB, SEQ], W0 + 40960)
        f_h1 = at("f_h1", [HY_W, SEQ], W0 + 43008)
        f_h2 = at("f_h2", [HY_W, SEQ], W0 + 45056)
        f_arg = at("f_arg", [HY_W, SEQ], W0 + 47104)
        f_w3 = at("f_w3", [HY_W, 1024], W0 + 57344)
        f_w12 = at("f_w12", [HY_W, 2, HY_W], W0 + 61440)
        f_k = at("f_k", [HY_W, SEQ], W0 + 61952)
        f_bias = at("f_bias", [1, SEQ], W0 + 86016)

        psA = ps("psA", [P, ACC, 512])
        psS = ps("psS", [P, 1024])
        psT = ps("psT", [P, 1024])
        psO = ps("psO", [P, 512])
        psN = ps("psN", [P, 512])

        s_const = sem("constants_loaded")
        s_x = sem("x_ctx_loaded")
        s_xl = sem("x_lat_loaded")
        s_rt = sem("rope_table_loaded")
        s_set = sem("constants_set")
        s_cond = sem("cond_ready")
        s_modw = [sem(f"mod_weights_loaded{i}") for i in range(2)]
        s_modf = [sem(f"mod_first_loaded{i}") for i in range(8)]
        s_modu = sem("mod_unit_used")
        s_coef = sem("coef_ready")
        s_raw = [sem(f"raw_loaded{i}") for i in range(RAW)]
        s_hi = sem("w_hi_ready")
        s_lo = sem("w_lo_ready")
        s_used = sem("unit_multiplied")
        s_free = sem("acc_evacuated")
        s_sq = sem("square_ready")
        s_squsd = sem("square_summed")
        s_std = sem("std_ready")
        s_rstd = sem("rstd_ready")
        s_t = sem("normed_ready")
        s_hf = sem("h_full_ready")
        s_h = sem("h_lo_ready")
        s_xu = sem("x_updated")
        s_rope = sem("rope_done")
        s_vT = sem("v_transposed")
        s_v = sem("v_ready")
        s_score = sem("scores_ready")
        s_max = sem("max_ready")
        s_prob = sem("exp_ready")
        s_pn = sem("prob_normalised")
        s_pT = sem("prob_transposed")
        s_pTc = sem("probT_ready")
        s_o = sem("attn_out_ready")
        s_ohi = sem("attn_hi_ready")
        s_olo = sem("attn_lo_ready")
        s_filtw = sem("filter_weights_loaded")
        s_fmm = sem("filter_product_ready")
        s_farg = sem("filter_angle_ready")
        s_fsin = sem("filter_sine_ready")
        s_tsum = sem("taps_full_ready")
        s_thi = sem("taps_hi_ready")
        s_tlo = sem("taps_lo_ready")
        s_short = sem("short_conv_ready")
        s_zT = sem("z_transposed")
        s_x1T = sem("x1_transposed")
        s_yT = sem("conv2_transposed")
        s_hz = sem("hyena_hi_ready")
        s_hzl = sem("hyena_lo_ready")
        s_x1t = sem("x1t_ready")
        s_yf = sem("spectrum_full_ready")
        s_yhi = sem("spectrum_hi_ready")
        s_ylo = sem("spectrum_lo_ready")
        s_gout = sem("hyena_gated")
        s_ghi = sem("hyena_out_hi_ready")
        s_sig = sem("sigmoid_ready")
        s_conv = sem("conv31_ready")
        s_lnm = sem("ln_sum_ready")
        s_lna = sem("ln_act_ready")
        s_lnd = sem("ln_centred")
        s_mix = sem("mix_ready")
        s_ft = sem("ffn_gate_started")
        s_fc = sem("ffn_gate_convolved")
        s_fsi = sem("ffn_silu_ready")
        s_fa = sem("ffn_hidden_full_ready")
        s_fhi = sem("ffn_hidden_hi_ready")
        s_flo = sem("ffn_hidden_lo_ready")
        s_dve = sem("vector_step")
        s_act = sem("scalar_step")
        s_pool = sem("pool_step")
        s_out = sem("out_stored")
        s_vend = sem("vector_end")

        def v(layer, name, j=0, n=1):
            o = VEC[name][0] + j
            if isinstance(j, int):
                return vec[:, layer, o:o + n]
            return vec[:, layer, bass.ds(o, n)]

        class Steps:

            def __init__(self, eng, s):
                self.eng, self.s, self.n, self.off = eng, s, 0, 0

            def inc(self, ins):
                ins.then_inc(self.s, 1)
                self.n += 1
                return self.n

            def wait(self, n):
                self.eng.wait_ge(self.s, n + self.off)

            def seq(self, ins):
                self.wait(self.inc(ins))

        FULL = [s for s in streams if s["full"]]

        def taps_before(st):
            return sum(s["nt"] for s in FULL if s["full0"] < st["full0"])

        def halves_before(st):
            return taps_before(st) // 2

        def rope_before(st):
            return 5 * sum(s["kind"] == "lat" for s in FULL if s["full0"] < st["full0"])

        def follows(st):
            later = [s for s in FULL if s["full0"] == st["full0"] + 1]
            return later[0] if later else None

        def mod_extra(st, name):
            if name == "w_in" and st["index"] == 0:
                return 2, 16
            if name == "w_up" and st["index"] == 1:
                return 1, 48
            return 0, 0

        def over(eng, g, f, steps=None, peel=0, head=0):
            body = g.body
            rounds = g.units // body - head
            looped = rounds - peel if rounds - peel >= 2 else 0
            for k in range(head * body if looped else 0):
                f(k, k, 0)
            head = head if looped else 0
            if looped:
                if steps:
                    n0 = steps.n
                with eng.Fori(head, head + looped) as i:
                    if steps:
                        steps.off = (i - head) * steps.per_round if head else i * steps.per_round
                    for j in range(body):
                        f(i * body + j, j, i)
                if steps:
                    assert steps.n - n0 == steps.per_round, (g.name, steps.n - n0)
                    steps.n = n0 + looped * steps.per_round
                    steps.off = 0
            for k in range((head + looped) * body, g.units):
                f(k, k, 0)

        def raw_count(g, k, j):
            done = (g.unit0 + j) // RAW + 1
            if isinstance(k, int):
                return 16 * ((g.unit0 + k) // RAW + 1)
            return 16 * done + (k - j) * (16 // RAW)

        def dyn(t, L, k):
            if isinstance(k, int):
                return t[L][k]
            return t[L][bass.ds(k, 1)].rearrange("a p n -> p (a n)")

        def dynt(t, k, T):
            if isinstance(k, int):
                return t[:, k, 0:T]
            return t[:, bass.ds(k, 1), 0:T].rearrange("p a t -> p (a t)")

        def att_pairs(st):
            return st["att0"] // 2

        def hz0(st):
            return sum(s["nt"] // 2 + s["nt"] for s in FULL if s["full0"] < st["full0"])

        def lna0(f):
            return 6 * f

        def gout0(st):
            return sum(s["nt"] + 2 for s in streams if s["full"] and s["full0"] < st["full0"])

        def dbg(name):
            return debug[name] if debug and name in debug else None

        block = ctx.enter_context(nc.Block())

        @block.sync
        def _(e):
            for t, n in ((cond, "cond"), (ident, "ident"), (masks, "masks"), (vec, "vec")):
                e.dma_start(t[:], a[n]).then_inc(s_const, 16)
            e.dma_start(x["ctx"][:], a["x_ctx"]).then_inc(s_x, 16)

            def load(g, src, riders=(0, 0)):
                per, m0 = riders

                def one(k, j, i):
                    slot = (g.unit0 + j) % RAW
                    e.wait_ge(s_lo, g.unit0 + k + 1)
                    w = g.width(j)
                    e.dma_start(raw[:, slot, 0:w], src(k, j, i)).then_inc(s_raw[slot], 16)
                    for q in range(per):
                        mod_load(m0 // 48, m0 % 48, k * per + q, j * per + q)
                over(e, g, one)

            def mod_load(L, m0, c, slot):
                e.wait_ge(s_modu, c + 48 * L + m0 - 1)
                e.dma_start(mod_ring[:, slot % 2, :], dyn(a["w_mod"], L, c + m0)).then_inc(s_modw[slot % 2], 16)

            def filters(st):
                T, nt = st["T"], st["nt"]
                if st["full0"]:
                    before = FULL[st["full0"] - 1]["gemm"]["w_down"]
                    e.wait_ge(s_used, SPLIT + before.unit0 + before.units)
                e.dma_start(emb[:, 0:T], a[f"emb{T}"]).then_inc(s_filtw, 16)
                e.dma_start(f_w12[:], a["f_w12"][st["layer"]]).then_inc(s_filtw, 16)
                e.dma_start(f_w3[:], a["f_w3"][st["layer"]]).then_inc(s_filtw, 16)
                e.dma_start(f_bias[:], a["f_bias"][st["layer"]]).then_inc(s_filtw, 16)
                e.dma_start(decay[:, 0:nt, :], a[f"decay{T}"]).then_inc(s_filtw, 16)
                load(st["gemm"]["filt"], lambda k, j, i: a[f"fwd{T}"][k])

            for st in streams:
                L, T, g = st["layer"], st["T"], st["gemm"]
                if st["index"] == 0:
                    for m in range(16):
                        if m >= 8:
                            e.wait_ge(s_modu, m - 7)
                        e.dma_start(mod_first[:, m % 8, :], a["w_mod"][0][m]).then_inc(s_modf[m % 8], 16)
                        if m == 3:
                            filters(st)
                    e.dma_start(x["lat"][:], a["x_lat"]).then_inc(s_xl, 16)
                    e.dma_start(rope[:], a["rope"]).then_inc(s_rt, 16)
                first = 0 if st["full"] else T_K
                load(g["w_in"], lambda k, j, i: dyn(a["w_in"], L, k + first), mod_extra(st, "w_in"))
                if not st["full"]:
                    continue
                F, I = a[f"fwd{T}"], a[f"inv{T}"]
                for o in range(2):
                    load(g[f"fwd{o}"], lambda k, j, i: F[k])
                    load(g[f"inv{o}"], lambda k, j, i: I[k])
                load(g["w_out"], lambda k, j, i: dyn(a["w_out"], L, k))
                load(g["w_up"], lambda k, j, i: dyn(a["w_up"], L, k), mod_extra(st, "w_up"))
                if mod_extra(st, "w_up")[0]:
                    for m in range(44, 48):
                        mod_load(1, 0, m, m)

                def down(k, j, i):
                    lo, hi = DOWN_UNITS[j % 4]
                    return a["w_down"][L][bass.ds(i * 2 + j // 4, 1)].rearrange("a p n -> p (a n)")[:, lo * P:hi * P]

                load(g["w_down"], down)
                if follows(st):
                    filters(follows(st))
            e.wait_ge(s_xu, 8 * 6)
            e.dma_start(out, x["lat"][:]).then_inc(s_out, 16)
            n_out = 16
            for name, t in (("x_ctx", x["ctx"]),):
                if dbg(name) is not None:
                    e.dma_start(dbg(name), t[:]).then_inc(s_out, 16)
                    n_out += 16
            e.wait_ge(s_out, n_out)

        @block.tensor
        def _(e):
            e.wait_ge(s_set, 6)
            e.nop().then_inc(s_used, SPLIT)

            def passes(dst, b, hi, lo, slot, first, last):
                wh, wl = w_hi[:, slot, b * P:(b + 1) * P], w_lo[:, slot, b * P:(b + 1) * P]
                e.matmul(dst, wh, hi, start=first, stop=False)
                e.matmul(dst, wh, lo, start=False, stop=False)
                return e.matmul(dst, wl, hi, start=False, stop=last)

            def unit_wait(g, k):
                e.wait_ge(s_lo, RAW + g.unit0 + k + 1)

            def norm(n, T):
                for kt in range(KT):
                    e.wait_ge(s_sq, KT * n + kt + 1)
                    e.matmul(psN[:, 0:T], ones[:], tmp[:, kt % 2, 0:T], start=kt == 0, stop=kt == KT - 1).then_inc(s_squsd, 1)

            def mod_unit(w, m):
                dst = psO[:, 2 * m:2 * m + 2] if isinstance(m, int) else psO[:, bass.ds(m * 2, 2)]
                for b in range(8):
                    mm = e.matmul(dst, w[:, b * P:(b + 1) * P], cond[:, b, :], start=b == 0, stop=b == 7)
                mm.then_inc(s_modu, 1)

            def mod_riders(st, name, k, j, i, body=4):
                per, m0 = mod_extra(st, name)
                for q in range(per):
                    c = j * per + q
                    e.wait_ge(s_modw[c % 2], i * (16 * body * per // 2) + 16 * ((m0 - 16 + c) // 2 + 1))
                    mod_unit(mod_ring[:, c % 2, :], i * (body * per) + m0 % 48 + c)

            def filters(st, between):
                T, nt, f0, taps0, g = st["T"], st["nt"], st["full0"], taps_before(st), st["gemm"]["filt"]
                e.wait_ge(s_filtw, 80 * (f0 + 1))
                e.matmul(psN[0:HY_W, 0:T], f_w12[0:HY_EMB, 0, :], emb[:, 0:T], start=True, stop=True).then_inc(s_fmm, 1)
                e.wait_ge(s_farg, 2 * f0 + 1)
                between(0)
                e.wait_ge(s_fsin, 2 * f0 + 1)
                e.matmul(psS[0:HY_W, 0:T], f_w12[:, 1, :], f_h1[:, 0:T], start=True, stop=True).then_inc(s_fmm, 1)
                between(1)
                e.wait_ge(s_fsin, 2 * f0 + 2)
                for tt in range(nt):
                    if tt >= 1:
                        e.wait_ge(s_tsum, 2 * (taps0 + tt))
                    e.matmul(psS[:, 0:512], f_h2[:, tt * P:(tt + 1) * P], f_w3[:, 0:512], start=True, stop=True)
                    e.matmul(psS[:, 512:1024], f_h2[:, tt * P:(tt + 1) * P], f_w3[:, 512:1024], start=True, stop=True).then_inc(s_fmm, 1)
                    between(2 + tt)
                e.wait_ge(s_tlo, 2 * (taps0 + nt))
                for k in range(g.units):
                    unit_wait(g, k)
                    for r in range(2):
                        o = g.out0 + 2 * k + r
                        e.wait_ge(s_free, o + 1)
                        for b in range(nt):
                            mm = passes(psA[:, o % ACC, :], r * nt + b, taps[r][0][:, b, :], taps[r][1][:, b, :],
                                        (g.unit0 + k) % SPLIT, b == 0, b == nt - 1)
                    mm.then_inc(s_used, 1)

            def proj(st, name, hi, lo, tile_ready):
                g, T = st["gemm"][name], st["T"]

                def one(k, j, i):
                    unit_wait(g, k)
                    e.wait_ge(s_free, g.out0 + k + 1)
                    dst = psA[:, (g.out0 + j) % ACC, 0:T]
                    for b in range(8):
                        if isinstance(k, int) and k == 0:
                            for wait in tile_ready(b):
                                e.wait_ge(*wait)
                        mm = passes(dst, b, hi[:, b, 0:T], lo[:, b, 0:T], (g.unit0 + j) % SPLIT, b == 0, b == 7)
                    mm.then_inc(s_used, 1)
                    mod_riders(st, name, k, j, i)
                over(e, g, one, head=1)

            def attention_and_mixers(st):
                T, nt, g, H, a0, f0 = st["T"], st["nt"], st["gemm"], st["heads"], st["att0"], st["full0"]
                taps0 = taps_before(st)

                def scores(w):
                    h = H[w]
                    q = p[:, T_Q + h["j"], h["n"] * P:(h["n"] + 1) * P]
                    if st["kind"] == "lat":
                        e.wait_ge(s_rope, rope_before(st) + 2 + h["j"] if h["n"] == 0 else rope_before(st) + 5)
                    if a0 + w >= 1:
                        e.wait_ge(s_prob, a0 + w)
                    blocks = list(range(h["a"], h["b"]))
                    mm = e.matmul(psS[:, 0:CTX], q, k_ctx[:, h["half"], :], start=True, stop=True)
                    for c, some in ((CTX, blocks[:2]), (CTX + 2 * P, blocks[2:])):
                        if not some:
                            continue
                        edge = [(c + P * (b - some[0]), int(b > h["n"])) for b in some if b != h["n"]]
                        mm = e.matmul(psS[:, c:c + P * len(some)], q, k_lat[h["half"]][:, some[0] * P:(some[-1] + 1) * P],
                                      start=True, stop=True)
                        for at_, side_ in edge:
                            mm = e.matmul(psS[:, at_:at_ + P], ident_b[:], masks_b[:, side_, :], start=False, stop=True,
                                          skip_group_check=True)
                    mm.then_inc(s_score, 1)

                def transposes(w):
                    e.wait_ge(s_pn, a0 + w + 1)
                    if a0 + w >= 1:
                        e.wait_ge(s_pTc, a0 + w)
                    for c in range(H[w]["width"] // P):
                        mm = e.transpose(psT[:, c * P:(c + 1) * P], prob[:, w % 2, c * P:(c + 1) * P], ident[:])
                    mm.then_inc(s_pT, 1)

                def values(w):
                    h = H[w]
                    pair = (a0 + w) // 2
                    e.wait_ge(s_pTc, a0 + w + 1)
                    if pair >= 1:
                        e.wait_ge(s_olo, pair)
                    chunks = h["width"] // P
                    for c in range(chunks):
                        for half in range(2):
                            hp = slice(64 * half, 64 * half + 64)
                            val = v_ctx[:, c, hp] if c < 2 else v_lat[:, h["a"] + c - 2, hp]
                            mm = e.matmul(psO[hp, 0:P], val, probT[:, half, c * P:(c + 1) * P], start=c == 0, stop=c == chunks - 1)
                    mm.then_inc(s_o, 1)

                def transpose_half(src, h, done):
                    for tt in range(2):
                        for c in range(2):
                            at_ = (2 * h + tt) * P
                            mm = e.transpose(psN[:, (2 * tt + c) * P:(2 * tt + c + 1) * P], src[:, c, at_:at_ + P], ident[:])
                    mm.then_inc(done, 1)

                def mixer(what, *arg):
                    if what == "z_t":
                        e.wait_ge(s_short, 6 * f0 + 2)
                        if arg[0]:
                            e.wait_ge(s_hzl, hz0(st) + arg[0])
                        transpose_half(short_z, arg[0], s_zT)
                    elif what == "x1_t":
                        e.wait_ge(s_short, 6 * f0 + 4)
                        e.wait_ge(s_hzl, hz0(st) + nt // 2)
                        if arg[0]:
                            e.wait_ge(s_x1t, halves_before(st) + arg[0])
                        transpose_half(short_x1, arg[0], s_x1T)
                    elif what == "fwd":
                        o, k = arg
                        gf = g[f"fwd{o}"]
                        e.wait_ge(s_hzl, hz0(st) + nt // 2 + nt * o)
                        unit_wait(gf, k)
                        oo = gf.out0 + k
                        e.wait_ge(s_free, oo + 1)
                        for r in range(2):
                            for b in range(nt):
                                mm = passes(psA[:, oo % ACC, r * 256:r * 256 + 256], r * nt + b, z_hi[:, b, :], z_lo[:, b, :],
                                            (gf.unit0 + k) % SPLIT, b == 0, b == nt - 1)
                        mm.then_inc(s_used, 1)
                    elif what == "inv":
                        o, k = arg
                        gi = g[f"inv{o}"]
                        e.wait_ge(s_ylo, 2 * taps0 + nt * (o + 1))
                        unit_wait(gi, k)
                        oo = gi.out0 + k
                        e.wait_ge(s_free, oo + 1)
                        for b in range(2 * nt):
                            mm = passes(psA[:, oo % ACC, 0:256], b, y_hi[:, b, :], y_lo[:, b, :], (gi.unit0 + k) % SPLIT,
                                        b == 0, b == 2 * nt - 1)
                        mm.then_inc(s_used, 1)
                    else:
                        r = int(what == "ln_square_sum")
                        e.wait_ge(s_lna, 6 * f0 + 3) if r else e.wait_ge(s_conv, 2 * (f0 + 1))
                        for c in range(2):
                            mm = e.matmul(psN[:, 0:T], ones[:], p[:, (T_GATE if r else T_A) + c, 0:T], start=c == 0, stop=c == 1)
                        mm.then_inc(s_lnm, 1)

                pe_plan, _ = mixer_plan(nt)
                scores(0)
                for w in range(len(H)):
                    if w + 1 < len(H):
                        scores(w + 1)
                    if w >= 2 and w % 2 == 0:
                        values(w - 1)
                    for what in pe_plan.get(w, ()):
                        mixer(*what)
                    transposes(w)
                values(len(H) - 1)
                e.wait_ge(s_free, ACC + g["inv1"].out0 + nt)
                e.wait_ge(s_lna, 6 * f0 + 4)
                for c in range(2):
                    for tt in range(nt):
                        mm = e.transpose(psT[:, c * 512 + tt * P:c * 512 + (tt + 1) * P], conv2[:, tt, c * P:(c + 1) * P], ident[:])
                mm.then_inc(s_yT, 1)

            for st in streams:
                L, T, nt, g, f0 = st["layer"], st["T"], st["nt"], st["gemm"], st["full0"]
                if st["index"] == 0:
                    def startup(n):
                        if n == 0:
                            norm(0, T)
                            e.wait_ge(s_cond, 1)
                        for m in {0: range(0, 4), 1: range(4, 8), 2: range(8, 10), 3: range(10, 16)}[n]:
                            e.wait_ge(s_modf[m % 8], 16 * (m // 8 + 1))
                            mod_unit(mod_first[:, m % 8, :], m)
                    filters(st, startup)
                else:
                    norm(st["norm0"], T)
                proj(st, "w_in", h_hi, h_lo, lambda b: [(s_h, KT * st["pre0"] + b + 1)])
                e.wait_ge(s_free, ACC + g["w_in"].out0 + g["w_in"].units)
                for n in range(nt):
                    mm = e.transpose(psN[:, n * P:(n + 1) * P], p[:, T_V, n * P:(n + 1) * P], ident[:])
                mm.then_inc(s_vT, 1)
                if not st["full"]:
                    continue
                e.wait_ge(s_coef, 2)
                e.wait_ge(s_v, st["index"] + 1)
                attention_and_mixers(st)
                proj(st, "w_out", mix_hi, mix_lo, lambda b: [(s_olo, att_pairs(st) + 4 * nt)] if b < 4 else [(s_mix, 4 * f0 + b - 3)])
                norm(st["norm0"] + 1, T)
                norm(st["norm0"] + 2, T)
                proj(st, "w_up", h_hi, h_lo, lambda b: [(s_h, KT * (st["pre0"] + 1) + b + 1)])
                if mod_extra(st, "w_up")[0]:
                    for m in range(92, 96):
                        e.wait_ge(s_modw[m % 2], 16 * ((m - 16) // 2 + 1))
                        mod_unit(mod_ring[:, m % 2, :], m - 48)
                gd = g["w_down"]
                e.wait_ge(s_flo, FT * (f0 + 1))

                def down(k, j, i):
                    c = j % 4
                    lo, hi = DOWN_UNITS[c]
                    unit_wait(gd, k)
                    if c == 0:
                        e.wait_ge(s_free, gd.out0 + i * 2 + j // 4 + 1)
                    for b in range(hi - lo):
                        mm = passes(psA[:, (gd.out0 + j // 4) % ACC, 0:T], b, act_hi[:, lo + b, 0:T], act_lo[:, lo + b, 0:T],
                                    (gd.unit0 + j) % SPLIT, lo + b == 0, lo + b == FT - 1)
                    mm.then_inc(s_used, 1)

                over(e, gd, down)
                if follows(st):
                    filters(follows(st), lambda n: norm(st["norm0"] + 3, T) if n == 0 else None)
                else:
                    norm(st["norm0"] + 3, T)

        @block.scalar
        def _(e):
            nc_ = nc.scalar
            step = Steps(e, s_act)
            e.wait_ge(s_const, 64)
            step.seq(nc_.activation(small[:, 0:1], ident[:, 0:1], ACT.Silu))
            nc_.activation(cond[:], cond[:], ACT.Silu).then_inc(s_cond, 1)
            e.wait_ge(s_set, 2)

            def split(g, k, j):
                u = g.unit0 + j
                e.wait_ge(s_raw[u % RAW], raw_count(g, k, j))
                e.wait_ge(s_used, g.unit0 + k + 1)
                w = g.width(j)
                nc_.copy(w_hi[:, u % SPLIT, 0:w], raw[:, u % RAW, 0:w]).then_inc(s_hi, 1)

            def norm(n, src, ready, T):
                for kt in range(KT):
                    if ready is not None:
                        e.wait_ge(*ready(kt))
                    if kt >= 2:
                        e.wait_ge(s_squsd, KT * n + kt - 1)
                    nc_.activation(tmp[:, kt % 2, 0:T], src[:, kt, 0:T], ACT.Square).then_inc(s_sq, 1)
                e.wait_ge(s_squsd, KT * (n + 1))
                e.wait_ge(s_rstd, n)
                nc_.activation(std[:, 0:T], psN[:, 0:T], ACT.Sqrt, bias=eps[:, 0:1], scale=1.0 / D).then_inc(s_std, 1)

            def pre(i, which, st):
                T, c = st["T"], st["col"]
                for kt in range(KT):
                    e.wait_ge(s_t, KT * i + kt + 1)
                    g_, b_ = coef[:, 2 * which, kt, c:c + 1], mod[:, 24 * which + kt, c:c + 1]
                    nc_.activation(h_hi[:, kt, 0:T], tmp[:, kt % 2, 0:T], ACT.Identity, bias=b_, scale=g_)
                    if kt >= 2:
                        e.wait_ge(s_h, KT * i + kt - 1)
                    nc_.activation(tmp[:, 2 + kt % 2, 0:T], tmp[:, kt % 2, 0:T], ACT.Identity, bias=b_, scale=g_).then_inc(s_hf, 1)

            def lagged(g, evac, steps=None):
                def one(k, j, i):
                    if not isinstance(k, int) or k + SPLIT < g.units:
                        split(g, k + SPLIT, j + SPLIT)
                    evac(k, j, i)
                over(e, g, one, steps, peel=1)

            def begin(g):
                for k in range(SPLIT):
                    split(g, k, k)

            def filters(st):
                T, nt, f0, taps0, g = st["T"], st["nt"], st["full0"], taps_before(st), st["gemm"]["filt"]
                for r, hbuf in enumerate((f_h1, f_h2)):
                    e.wait_ge(s_farg, 2 * f0 + r + 1)
                    nc_.activation(hbuf[:, 0:T], f_arg[:, 0:T], ACT.Sin).then_inc(s_fsin, 1)
                begin(g)
                for tt in range(nt):
                    for r in range(2):
                        e.wait_ge(s_tsum, 2 * (taps0 + tt) + 1 + r)
                        nc_.copy(taps[r][0][:, tt, :], tmp[:, 2 + r, :]).then_inc(s_thi, 1)
                for k in range(g.units):
                    if k + SPLIT < g.units:
                        split(g, k + SPLIT, k + SPLIT)
                    e.wait_ge(s_used, SPLIT + g.unit0 + k + 1)
                    for r in range(2):
                        nc_.copy(spec[r][:, k, :], psA[:, (g.out0 + 2 * k + r) % ACC, :]).then_inc(s_free, 1)

            def attention_and_mixers(st):
                L, T, nt, g, H, a0, f0 = st["layer"], st["T"], st["nt"], st["gemm"], st["heads"], st["att0"], st["full0"]
                taps0 = taps_before(st)

                def expo(w):
                    h = H[w]
                    r = (a0 + w) % 2
                    hd = h["j"] + 4 * h["half"]
                    e.wait_ge(s_max, a0 + w + 1)
                    nc_.activation(small[:, 4 + r:5 + r], v(L, "sink", hd), ACT.Exp, bias=small[:, 2 + r:3 + r])
                    nc_.activation(prob[:, w % 2, 0:h["width"]], psS[:, 0:h["width"]], ACT.Exp, bias=small[:, 2 + r:3 + r],
                                   scale=SCALE, accum_out=small[:, 6 + r:7 + r]).then_inc(s_prob, 1)

                def back(w):
                    e.wait_ge(s_pT, a0 + w + 1)
                    width = H[w]["width"]
                    nc_.copy(probT[:, w % 2, 0:width], psT[:, 0:width]).then_inc(s_pTc, 1)

                def out_hi(w):
                    h = H[w]
                    e.wait_ge(s_o, (a0 + w) // 2 + 1)
                    nc_.copy(mix_hi[:, h["j"], h["n"] * P:(h["n"] + 1) * P], psO[:, 0:P]).then_inc(s_ohi, 1)

                def mixer(what, *arg):
                    if what == "split":
                        split(g[arg[0]], arg[1], arg[1])
                    elif what == "z":
                        h, = arg
                        e.wait_ge(s_zT, halves_before(st) + h + 1)
                        nc_.copy(z_hi[:, 2 * h:2 * h + 2, :], psN[:].rearrange("p (n d) -> p n d", n=2)).then_inc(s_hz, 1)
                    elif what == "x1":
                        h, = arg
                        e.wait_ge(s_x1T, halves_before(st) + h + 1)
                        nc_.copy(x1t[:, 2 * h:2 * h + 2, :], psN[:].rearrange("p (n d) -> p n d", n=2)).then_inc(s_x1t, 1)
                    elif what == "spectrum":
                        o, k = arg
                        e.wait_ge(s_yf, 2 * taps0 + nt * o + k + 1)
                        nc_.copy(y_hi[:, 2 * k:2 * k + 2, :], tmp[:, 2, :].rearrange("p (r c) -> p r c", r=2)).then_inc(s_yhi, 1)
                    elif what == "gate":
                        o, k = arg
                        gi = g[f"inv{o}"]
                        if o == 0:
                            e.wait_ge(s_gout, gout0(st) + k + 1)
                            nc_.copy(z_hi[:, k, :], tmp[:, 3, 0:256]).then_inc(s_hz, 1)
                        else:
                            e.wait_ge(s_used, SPLIT + gi.unit0 + k + 1)
                            nc_.copy(conv2[:, k, :], psA[:, (gi.out0 + k) % ACC, 0:256]).then_inc(s_free, 1)
                    elif what == "ln_centre":
                        e.wait_ge(s_lnm, 2 * f0 + 1)
                        nc_.activation(std[:, 0:T], psN[:, 0:T], ACT.Copy, scale=1.0 / CV_CH).then_inc(s_lna, 1)
                        for c in range(2):
                            e.wait_ge(s_lnd, 5 * f0 + c + 1)
                            nc_.activation(p[:, T_GATE + c, 0:T], p[:, T_A + c, 0:T], ACT.Square).then_inc(s_lna, 1)
                    elif what == "ln_scale":
                        e.wait_ge(s_lnm, 2 * f0 + 2)
                        nc_.activation(std[:, 0:T], psN[:, 0:T], ACT.Sqrt, bias=eps[:, 0:1], scale=1.0 / CV_CH).then_inc(s_lna, 1)

                _, side_plan = mixer_plan(nt)
                expo(0)
                for w in range(len(H)):
                    if w + 1 < len(H):
                        expo(w + 1)
                    for what in side_plan.get(w, ()):
                        mixer(*what)
                    if w >= 2 and w % 2 == 0:
                        out_hi(w - 1)
                    back(w)
                out_hi(len(H) - 1)
                for c in range(2):
                    e.wait_ge(s_lnd, 5 * f0 + 3 + c + 1)
                    step.inc(nc_.activation(tmp[:, 2 + c, 0:T], p[:, T_A + c, 0:T], ACT.Silu, bias=v(L, "ln_b", c), scale=v(L, "ln_g", c)))
                for c in range(2):
                    e.wait_ge(s_gout, gout0(st) + nt + c + 1)
                    nc_.copy(mix_hi[:, 4 + c, 0:T], tmp[:, c, 0:T]).then_inc(s_ghi, 1)
                step.wait(step.n)
                for c in range(2):
                    nc_.copy(mix_hi[:, 6 + c, 0:T], tmp[:, 2 + c, 0:T]).then_inc(s_lna, 1)

            for st in streams:
                L, T, nt, g, f0 = st["layer"], st["T"], st["nt"], st["gemm"], st["full0"]
                xs = x[st["kind"]]
                if st["index"] == 0:
                    e.wait_ge(s_x, 16)
                if st["index"] == 1:
                    e.wait_ge(s_xl, 16)
                n0 = st["norm0"]
                norm(n0, xs, (lambda kt: (s_xu, 8 * st["post0"])) if st["index"] >= 2 else None, T)
                if st["index"] == 0:
                    filters(st)
                e.wait_ge(s_coef, 1 if L == 0 else 3)
                pre(st["pre0"], 0, st)
                begin(g["w_in"])
                gi = g["w_in"]
                first = 0 if st["full"] else T_K

                def evac_in(k, j, i):
                    e.wait_ge(s_used, SPLIT + gi.unit0 + k + 1)
                    src = psA[:, (gi.out0 + j) % ACC, 0:T]
                    dst = p[:, k + first, 0:T] if isinstance(k, int) else p[:, bass.ds(k + first, 1), 0:T].rearrange("p a t -> p (a t)")
                    nc_.copy(dst, src).then_inc(s_free, 1)

                lagged(gi, evac_in)
                dst = v_lat
                if st["kind"] == "ctx":
                    dst = v_ctx
                    e.wait_ge(s_free, ACC + gi.out0 + gi.units)
                    for half in range(2):
                        hp = slice(64 * half, 64 * half + 64)
                        nc_.copy(k_ctx[hp, half, :], p[hp, T_K, 0:T])
                e.wait_ge(s_vT, st["index"] + 1)
                nc_.copy(dst[:, 0:nt, :], psN[:, 0:T].rearrange("p (n d) -> p n d", n=nt)).then_inc(s_v, 1)
                if not st["full"]:
                    continue
                e.wait_ge(s_free, ACC + gi.out0 + gi.units)
                for c in range(2):
                    nc_.activation(p[:, T_GATE + c, 0:T], p[:, T_GATE + c, 0:T], ACT.Sigmoid).then_inc(s_sig, 1)
                attention_and_mixers(st)
                go = g["w_out"]
                begin(go)

                def evac_out(k, j, i):
                    e.wait_ge(s_used, SPLIT + go.unit0 + k + 1)
                    nc_.copy(y[:, k, 0:T], psA[:, (go.out0 + j) % ACC, 0:T]).then_inc(s_free, 1)

                lagged(go, evac_out)
                norm(n0 + 1, y, lambda kt: (s_free, ACC + go.out0 + go.outs), T)
                norm(n0 + 2, xs, lambda kt: (s_xu, 8 * st["post0"] + kt + 1), T)
                pre(st["pre0"] + 1, 1, st)
                gu = g["w_up"]
                begin(gu)
                step.seq(nc_.activation(small[:, 0:1], eps[:, 0:1], ACT.Silu))

                def evac_up(k, j, i):
                    jj = i * 2 + j // 2
                    r = (j // 2) % 2
                    if j % 2 == 0:
                        e.wait_ge(s_used, SPLIT + gu.unit0 + k + 1)
                        nc_.activation(tmp[:, r, 0:T], psA[:, (gu.out0 + j) % ACC, 0:T], ACT.Identity,
                                       scale=v(L, "ffn_dw", jj * 4 + 1), bias=v(L, "ffn_dw", jj * 4 + 3)).then_inc(s_ft, 1)
                        e.wait_ge(s_fc, FT * f0 + jj + 1)
                        nc_.activation(tmp[:, r, 0:T], tmp[:, r, 0:T], ACT.Silu).then_inc(s_fsi, 1)
                    else:
                        e.wait_ge(s_fa, FT * f0 + jj + 1)
                        nc_.copy(dynt(act_hi, jj, T), tmp[:, 2 + r, 0:T]).then_inc(s_fhi, 1)

                lagged(gu, evac_up)
                gd = g["w_down"]
                begin(gd)

                def evac_down(k, j, i):
                    if j % 4 == 3:
                        e.wait_ge(s_used, SPLIT + gd.unit0 + k + 1)
                        nc_.copy(dynt(y, i * 2 + j // 4, T), psA[:, (gd.out0 + j // 4) % ACC, 0:T]).then_inc(s_free, 1)

                lagged(gd, evac_down)
                norm(n0 + 3, y, lambda kt: (s_free, ACC + gd.out0 + gd.outs), T)
                if follows(st):
                    filters(follows(st))

        @block.vector
        def _(e):
            step = Steps(e, s_dve)
            e.memset(ones[:], 1.0).then_inc(s_set, 1)
            e.memset(eps[:], EPS).then_inc(s_set, 1)
            for half in range(2):
                e.memset(k_ctx[64 - 64 * half:128 - 64 * half, half, :], 0.0).then_inc(s_set, 1)
            e.nop().then_inc(s_lo, RAW)
            e.nop().then_inc(s_free, ACC)
            e.wait_ge(s_const, 64)
            e.tensor_copy(ident_b[:], ident[:]).then_inc(s_set, 1)
            e.tensor_copy(masks_b[:], masks[:]).then_inc(s_set, 1)

            def split(g, k, j):
                u = g.unit0 + j
                w = g.width(j)
                e.wait_ge(s_hi, g.unit0 + k + 1)
                e.tensor_tensor(w_lo[:, u % SPLIT, 0:w], raw[:, u % RAW, 0:w], w_hi[:, u % SPLIT, 0:w].bitcast(F32),
                                ALU.subtract).then_inc(s_lo, 1)

            def begin(g):
                for k in range(SPLIT):
                    split(g, k, k)

            def lagged(g, evac, steps=None):
                def one(k, j, i):
                    if not isinstance(k, int) or k + SPLIT < g.units:
                        split(g, k + SPLIT, j + SPLIT)
                    evac(k, j, i)
                over(e, g, one, steps, peel=1)

            def low(dst, full, hi):
                return e.tensor_tensor(dst, full, hi.bitcast(F32), ALU.subtract)

            def reciprocal_std(n, T):
                e.wait_ge(s_std, n + 1)
                e.reciprocal(rstd[:, 0:T], std[:, 0:T]).then_inc(s_rstd, 1)
                e.wait_ge(s_rstd, n + 1)

            def pre(i, n, st):
                T, xs = st["T"], x[st["kind"]]
                reciprocal_std(n, T)
                for kt in range(KT + 1):
                    if kt < KT:
                        if kt >= 2:
                            e.wait_ge(s_hf, KT * i + kt - 1)
                        e.tensor_tensor(tmp[:, kt % 2, 0:T], xs[:, kt, 0:T], rstd[:, 0:T], ALU.mult).then_inc(s_t, 1)
                    if kt >= 1:
                        b = kt - 1
                        e.wait_ge(s_hf, KT * i + b + 1)
                        low(h_lo[:, b, 0:T], tmp[:, 2 + b % 2, 0:T], h_hi[:, b, 0:T]).then_inc(s_h, 1)

            def post(n, which, st):
                T, xs, c = st["T"], x[st["kind"]], st["col"]
                reciprocal_std(n, T)
                for kt in range(KT):
                    step.seq(e.tensor_tensor(tmp[:, 2 + kt % 2, 0:T], y[:, kt, 0:T], rstd[:, 0:T], ALU.mult))
                    e.scalar_tensor_tensor(out=xs[:, kt, 0:T], in0=tmp[:, 2 + kt % 2, 0:T], scalar=coef[:, 2 * which + 1, kt, c:c + 1],
                                           in1=xs[:, kt, 0:T], op0=ALU.mult, op1=ALU.add).then_inc(s_xu, 1)

            def modulation(L, a_, b_):
                for c in range(2):
                    i_ = step.inc(e.tensor_tensor(mod[:, a_:b_, c], psO[:, 2 * a_ + c:2 * b_:2], v(L, "b_mod", a_, b_ - a_), ALU.add))
                step.wait(i_)

            def coefs(L, kinds):
                names = ("g_pre_mix", "g_post_mix", "g_pre_ffn", "g_post_ffn")
                for q in kinds:
                    t0 = 24 * (q // 2) + 8 + 8 * (q % 2)
                    for c in range(2):
                        if q % 2 == 0:
                            last = e.scalar_tensor_tensor(out=coef[:, q, :, c], in0=mod[:, t0:t0 + 8, c], scalar=1.0,
                                                          in1=v(L, names[q], 0, 8), op0=ALU.add, op1=ALU.mult)
                        else:
                            last = e.tensor_tensor(coef[:, q, :, c], mod[:, t0:t0 + 8, c], v(L, names[q], 0, 8), ALU.mult)
                last.then_inc(s_coef, 1)

            def filters(st):
                L, T, nt, f0, taps0, g = st["layer"], st["T"], st["nt"], st["full0"], taps_before(st), st["gemm"]["filt"]
                hv = lambda q: v(L, "hy_vec", q)[0:HY_W]
                w_ = slice(0, T)
                for r, src in enumerate((psN, psS)):
                    e.wait_ge(s_fmm, (2 * f0 + taps0) + r + 1)
                    if r == 1:
                        e.wait_ge(s_fsin, 2 * f0 + 1)
                    step.seq(e.tensor_scalar(f_arg[:, w_], src[0:HY_W, w_], hv(2 * r), hv(2 * r + 1), ALU.add, ALU.mult))
                    step.seq(e.tensor_scalar(f_k[:, w_], f_arg[:, w_], float(1 / (2 * np.pi)), MAGIC, ALU.mult, ALU.add))
                    step.seq(e.tensor_scalar(f_k[:, w_], f_k[:, w_], MAGIC, None, ALU.subtract))
                    for part in TWO_PI:
                        step.seq(e.scalar_tensor_tensor(out=f_arg[:, w_], in0=f_k[:, w_], scalar=-part, in1=f_arg[:, w_],
                                                        op0=ALU.mult, op1=ALU.add))
                    e.tensor_scalar(f_arg[:, w_], f_arg[:, w_], PI_IN, -PI_IN, ALU.min, ALU.max).then_inc(s_farg, 1)
                begin(g)
                for tt in range(nt):
                    e.wait_ge(s_fmm, 2 * f0 + taps0 + 2 + tt + 1)
                    for r in range(2):
                        dec = decay[:, tt, 256 * r:256 * r + 256].unsqueeze(1).to_broadcast([P, 2, 256])
                        i_ = step.inc(e.tensor_tensor(tmp[:, r, :].rearrange("p (o c) -> p o c", o=2),
                                                      psS[:, 512 * r:512 * r + 512].rearrange("p (o c) -> p o c", o=2), dec, ALU.mult))
                    step.wait(i_)
                    if tt == 0:
                        step.seq(e.tensor_tensor(tmp[0:1, 0, :], tmp[0:1, 0, :], f_bias[:], ALU.add))
                    for r, op in enumerate((ALU.add, ALU.subtract)):
                        e.tensor_tensor(tmp[:, 2 + r, :], tmp[:, 0, :], tmp[:, 1, :], op).then_inc(s_tsum, 1)
                    for r in range(2):
                        e.wait_ge(s_thi, 2 * (taps0 + tt) + r + 1)
                        low(taps[r][1][:, tt, :], tmp[:, 2 + r, :], taps[r][0][:, tt, :]).then_inc(s_tlo, 1)

            def attention_and_mixers(st):
                L, T, nt, g, H, a0, f0 = st["layer"], st["T"], st["nt"], st["gemm"], st["heads"], st["att0"], st["full0"]
                taps0 = taps_before(st)
                rotated = [rope_before(st)]

                def rotate(t_):
                    i_ = step.inc(e.stream_shuffle(tmp[:, 0, :], p[:, t_, :], [(i + 16) % 32 for i in range(32)]))
                    i_ = step.inc(e.tensor_tensor(tmp[:, 1, :], p[:, t_, :], rope[:, 0, :], ALU.mult))
                    step.wait(i_)
                    step.seq(e.tensor_tensor(tmp[:, 0, :], tmp[:, 0, :], rope[:, 1, :], ALU.mult))
                    if t_ == T_K:
                        for half in range(2):
                            hp = slice(64 * half, 64 * half + 64)
                            last = e.tensor_tensor(k_lat[half][hp, :], tmp[hp, 0, :], tmp[hp, 1, :], ALU.add)
                            if half == 0:
                                step.seq(last)
                    else:
                        last = e.tensor_tensor(p[:, t_, :], tmp[:, 0, :], tmp[:, 1, :], ALU.add)
                    last.then_inc(s_rope, 1)
                    rotated[0] += 1
                    e.wait_ge(s_rope, rotated[0])

                def maxes(w):
                    h = H[w]
                    r = (a0 + w) % 2
                    hd = h["j"] + 4 * h["half"]
                    e.wait_ge(s_score, a0 + w + 1)
                    step.seq(e.tensor_reduce(small[:, 8 + r:9 + r], psS[:, 0:h["width"]], AX.X, ALU.max))
                    step.seq(e.tensor_scalar(small[:, 10 + r:11 + r], small[:, 8 + r:9 + r], SCALE, v(L, "sink", hd), ALU.mult, ALU.max))
                    e.tensor_scalar(small[:, 2 + r:3 + r], small[:, 10 + r:11 + r], -1.0, None, ALU.mult).then_inc(s_max, 1)

                def normalise(w):
                    h = H[w]
                    r = (a0 + w) % 2
                    e.wait_ge(s_prob, a0 + w + 1)
                    step.seq(e.tensor_tensor(small[:, 12 + r:13 + r], small[:, 4 + r:5 + r], small[:, 6 + r:7 + r], ALU.add))
                    step.seq(e.reciprocal(small[:, 14 + r:15 + r], small[:, 12 + r:13 + r]))
                    e.tensor_scalar(prob[:, w % 2, 0:h["width"]], prob[:, w % 2, 0:h["width"]], small[:, 14 + r:15 + r], None,
                                    ALU.mult).then_inc(s_pn, 1)

                def out_lo(w):
                    h = H[w]
                    e.wait_ge(s_ohi, (a0 + w) // 2 + 1)
                    sl = slice(h["n"] * P, (h["n"] + 1) * P)
                    low(mix_lo[:, h["j"], sl], psO[:, 0:P], mix_hi[:, h["j"], sl]).then_inc(s_olo, 1)

                two = lambda t: t.rearrange("p (r c) -> p r c", r=2)

                def mixer(what, *arg):
                    if what == "split":
                        split(g[arg[0]], arg[1], arg[1])
                    elif what == "short":
                        q, = arg
                        if q == 1:
                            e.wait_ge(s_short, 6 * f0 + 2)
                        for c in range(2):
                            hs = lambda i: v(L, "hy_short", 4 * (2 * q + c) + i)
                            src, dst = p[:, T_X1 + 2 * q + c, 0:T], (short_x1, short_x2, short_z)[q][:, c, 0:T]
                            step.seq(e.tensor_scalar(dst, src, hs(1), hs(3), ALU.mult, ALU.add))
                            step.seq(e.scalar_tensor_tensor(out=dst[:, 1:T], in0=src[:, 0:T - 1], scalar=hs(0), in1=dst[:, 1:T], op0=ALU.mult, op1=ALU.add))
                            e.scalar_tensor_tensor(out=dst[:, 0:T - 1], in0=src[:, 1:T], scalar=hs(2), in1=dst[:, 0:T - 1], op0=ALU.mult,
                                                   op1=ALU.add).then_inc(s_short, 1)
                    elif what == "z":
                        h, = arg
                        e.wait_ge(s_hz, hz0(st) + h + 1)
                        low(z_lo[:, 2 * h:2 * h + 2, :], psN[:].rearrange("p (n d) -> p n d", n=2), z_hi[:, 2 * h:2 * h + 2, :]).then_inc(s_hzl, 1)
                    elif what == "spectrum":
                        o, k = arg
                        gf = g[f"fwd{o}"]
                        e.wait_ge(s_used, SPLIT + gf.unit0 + k + 1)
                        U = two(psA[:, (gf.out0 + k) % ACC, :])
                        Hs_ = [spec[r][:, k, 256 * o:256 * o + 256].unsqueeze(1).to_broadcast([P, 2, 256]) for r in range(2)]
                        i_ = step.inc(e.tensor_tensor(two(tmp[:, 0, :]), U, Hs_[0], ALU.mult))
                        e.tensor_tensor(two(tmp[:, 1, :]), U, Hs_[1], ALU.mult).then_inc(s_free, 1)
                        e.wait_ge(s_free, ACC + gf.out0 + k + 1)
                        step.wait(i_)
                        if k >= 1:
                            e.wait_ge(s_yhi, 2 * taps0 + nt * o + k)
                        e.tensor_tensor(tmp[:, 2, 0:256], tmp[:, 0, 0:256], tmp[:, 1, 256:512], ALU.subtract)
                        e.tensor_tensor(tmp[:, 2, 256:512], tmp[:, 0, 256:512], tmp[:, 1, 0:256], ALU.add).then_inc(s_yf, 1)
                        e.wait_ge(s_yhi, 2 * taps0 + nt * o + k + 1)
                        low(y_lo[:, 2 * k:2 * k + 2, :], two(tmp[:, 2, :]), y_hi[:, 2 * k:2 * k + 2, :]).then_inc(s_ylo, 1)
                    elif what == "gate" and arg[0] == 0:
                        k = arg[1]
                        gi = g["inv0"]
                        e.wait_ge(s_x1t, halves_before(st) + nt // 2)
                        e.wait_ge(s_used, SPLIT + gi.unit0 + k + 1)
                        e.wait_ge(s_hzl, hz0(st) + nt // 2 + k)
                        e.tensor_tensor(tmp[:, 3, 0:256], psA[:, (gi.out0 + k) % ACC, 0:256], x1t[:, k, :], ALU.mult).then_inc(s_gout, 1)
                        e.wait_ge(s_gout, gout0(st) + k + 1)
                        e.nop().then_inc(s_free, 1)
                        e.wait_ge(s_hz, hz0(st) + nt // 2 + k + 1)
                        low(z_lo[:, k, :], tmp[:, 3, 0:256], z_hi[:, k, :]).then_inc(s_hzl, 1)
                    elif what == "ln_centre":
                        e.wait_ge(s_lna, 6 * f0 + 1)
                        for c in range(2):
                            e.tensor_tensor(p[:, T_A + c, 0:T], p[:, T_A + c, 0:T], std[:, 0:T], ALU.subtract).then_inc(s_lnd, 1)
                    elif what == "ln_scale":
                        e.wait_ge(s_lna, 6 * f0 + 4)
                        e.reciprocal(rstd[:, 0:T], std[:, 0:T]).then_inc(s_lnd, 1)
                        e.wait_ge(s_lnd, 5 * f0 + 3)
                        for c in range(2):
                            e.tensor_tensor(p[:, T_A + c, 0:T], p[:, T_A + c, 0:T], rstd[:, 0:T], ALU.mult).then_inc(s_lnd, 1)

                _, side_plan = mixer_plan(nt)
                if st["kind"] == "lat":
                    e.wait_ge(s_rt, 16)
                    for half in range(2):
                        e.memset(k_lat[half][64 - 64 * half:128 - 64 * half, :], 0.0)
                    for t_ in (T_K, 0):
                        rotate(t_)
                maxes(0)
                for w in range(len(H)):
                    normalise(w)
                    if w + 1 < len(H):
                        maxes(w + 1)
                    if st["kind"] == "lat" and w in (0, 2, 4):
                        rotate(1 + w // 2)
                    for what in side_plan.get(w, ()):
                        mixer(*what)
                    if w >= 2 and w % 2 == 0:
                        out_lo(w - 1)
                out_lo(len(H) - 1)
                e.wait_ge(s_yT, f0 + 1)
                for c in range(2):
                    e.tensor_tensor(tmp[:, c, 0:T], psT[:, c * 512:c * 512 + T], short_x2[:, c, 0:T], ALU.mult).then_inc(s_gout, 1)
                for c in range(2):
                    e.wait_ge(s_ghi, 2 * f0 + c + 1)
                    low(mix_lo[:, 4 + c, 0:T], tmp[:, c, 0:T], mix_hi[:, 4 + c, 0:T]).then_inc(s_mix, 1)
                for c in range(2):
                    e.wait_ge(s_lna, 6 * f0 + 4 + c + 1)
                    low(mix_lo[:, 6 + c, 0:T], tmp[:, 2 + c, 0:T], mix_hi[:, 6 + c, 0:T]).then_inc(s_mix, 1)

            def filter_splits(st):
                g = st["gemm"]["filt"]
                for k in range(SPLIT, g.units):
                    split(g, k, k)

            for st in streams:
                L, T, nt, g, f0 = st["layer"], st["T"], st["nt"], st["gemm"], st["full0"]
                n0 = st["norm0"]
                if st["index"] == 0:
                    filters(st)
                    filter_splits(st)
                    e.wait_ge(s_modu, 16)
                    modulation(0, 0, 16)
                    coefs(0, (0,))
                    e.wait_ge(s_x, 16)
                elif L == 1 and st["kind"] == "ctx":
                    e.wait_ge(s_modu, 96)
                    modulation(1, 0, 48)
                    coefs(1, range(4))
                elif st["index"] == 1:
                    e.wait_ge(s_xl, 16)
                pre(st["pre0"], n0, st)
                begin(g["w_in"])
                lagged(g["w_in"], lambda k, j, i: None)
                if st["index"] == 0:
                    e.wait_ge(s_modu, 48)
                    modulation(0, 16, 48)
                    coefs(0, (1, 2, 3))
                    e.wait_ge(s_coef, 2)
                if not st["full"]:
                    continue
                e.wait_ge(s_free, ACC + g["w_in"].out0 + 16)
                attention_and_mixers(st)
                begin(g["w_out"])
                lagged(g["w_out"], lambda k, j, i: None)
                post(n0 + 1, 0, st)
                pre(st["pre0"] + 1, n0 + 2, st)
                gu = g["w_up"]
                begin(gu)

                def evac_up(k, j, i):
                    jj = i * 2 + j // 2
                    r = (j // 2) % 2
                    src = psA[:, (gu.out0 + j) % ACC, :]
                    if j % 2 == 0:
                        e.wait_ge(s_ft, FT * f0 + jj + 1)
                        t_ = tmp[:, r, :]
                        step.seq(e.scalar_tensor_tensor(out=t_[:, 1:T], in0=src[:, 0:T - 1], scalar=v(L, "ffn_dw", jj * 4), in1=t_[:, 1:T],
                                                        op0=ALU.mult, op1=ALU.add))
                        e.scalar_tensor_tensor(out=t_[:, 0:T - 1], in0=src[:, 1:T], scalar=v(L, "ffn_dw", jj * 4 + 2), in1=t_[:, 0:T - 1],
                                               op0=ALU.mult, op1=ALU.add).then_inc(s_fc, 1)
                        e.wait_ge(s_fc, FT * f0 + jj + 1)
                        e.nop().then_inc(s_free, 1)
                    else:
                        e.wait_ge(s_used, SPLIT + gu.unit0 + k + 1)
                        e.wait_ge(s_fsi, FT * f0 + jj + 1)
                        e.tensor_tensor(tmp[:, 2 + r, 0:T], tmp[:, r, 0:T], src[:, 0:T], ALU.mult).then_inc(s_fa, 1)
                        e.wait_ge(s_fa, FT * f0 + jj + 1)
                        e.nop().then_inc(s_free, 1)
                        e.wait_ge(s_fhi, FT * f0 + jj + 1)
                        low(dynt(act_lo, jj, T), tmp[:, 2 + r, 0:T], dynt(act_hi, jj, T)).then_inc(s_flo, 1)

                step.per_round = 2
                lagged(gu, evac_up, step)
                gd = g["w_down"]
                begin(gd)
                lagged(gd, lambda k, j, i: None)
                if follows(st):
                    filters(follows(st))
                post(n0 + 3, 1, st)
                if follows(st):
                    filter_splits(follows(st))

        @block.gpsimd
        def _(e):
            step = Steps(e, s_pool)
            e.wait_ge(s_const, 64)
            for st in streams:
                if not st["full"]:
                    continue
                L, T, f0 = st["layer"], st["T"], st["full0"]
                for c in range(2):
                    e.wait_ge(s_sig, 2 * f0 + c + 1)
                    step.seq(e.tensor_tensor(glu[:, c, 0:T], p[:, T_A + c, 0:T], p[:, T_GATE + c, 0:T], ALU.mult))
                    dst = p[:, T_A + c, :]
                    mid = CV_K // 2
                    step.seq(e.tensor_scalar(dst[:, 0:T], glu[:, c, 0:T], v(L, "cv_w", 31 * c + mid), v(L, "cv_b", c), ALU.mult, ALU.add))
                    for k in range(CV_K):
                        if k == mid:
                            continue
                        lo, hi = max(0, mid - k), min(T, T + mid - k)
                        step.seq(e.tensor_scalar(tap[:, lo:hi], glu[:, c, lo + k - mid:hi + k - mid], v(L, "cv_w", 31 * c + k), 0.0,
                                                 ALU.mult, ALU.add))
                        ins = e.tensor_tensor(dst[:, lo:hi], dst[:, lo:hi], tap[:, lo:hi], ALU.add)
                        if k < CV_K - 1:
                            step.seq(ins)
                    ins.then_inc(s_conv, 1)



def shape_tables():
    t = {}
    pos = np.arange(SEQ)
    inv = (10000.0 ** (-np.arange(0, 32, 2, dtype=np.float32) / np.float32(32))).astype(np.float32)
    cos, sin = np.zeros((P, SEQ), np.float32), np.zeros((P, SEQ), np.float32)
    for q in range(P):
        d = q % HEAD
        where = (pos // GRID_W if d < 32 else pos % GRID_W).astype(np.float32)
        ang = where * inv[d % 16]
        cos[q] = np.cos(ang)
        sin[q] = np.sin(ang) * (-1 if d % 32 < 16 else 1)
    t["rope"] = np.stack([cos, sin], 1)
    i = np.arange(P)
    t["masks"] = np.stack([np.where(i[None] >= i[:, None], 0, NEG), np.where(i[None] <= i[:, None], 0, NEG)], 1).astype(np.float32)
    t["ident"] = np.eye(P, dtype=np.float32)
    deltas = np.abs(np.linspace(np.log(1e-2) / 1.5, np.log(1e-2) / 0.3, HY_CH))
    for T in (SEQ, CTX):
        nt = T // P
        lin = np.linspace(0.0, 1.0, T)[:, None]
        w = (2.0 * np.pi / T) * np.arange(T)[:, None]
        f = np.linspace(1e-4, HY_BANDS - 1, HY_BANDS)[None]
        t[f"emb{T}"] = np.concatenate([lin, np.cos(f * w), -np.sin(f * w)], -1).T.astype(np.float32)
        dec = np.exp(-lin * deltas)
        dec2 = dec.copy()
        dec2[0] = 0
        both = np.stack([dec, dec2], 1).reshape(nt, P, 2 * HY_CH)
        t[f"decay{T}"] = both.transpose(1, 0, 2).astype(np.float32)
        ang = np.pi * (2 * np.arange(T)[None] + 1) * np.arange(T)[:, None] / (2 * T) * 1.0
        cs = np.stack([np.cos(ang), np.sin(ang)])
        blk = cs.reshape(2, nt, P, nt, P)
        t[f"fwd{T}"] = blk.transpose(3, 2, 0, 1, 4).reshape(nt, P, 2 * nt * P).astype(np.float32)
        t[f"inv{T}"] = (blk.transpose(1, 4, 3, 0, 2).reshape(nt, P, 2 * nt * P) / T).astype(np.float32)
    return {k: np.ascontiguousarray(x) for k, x in t.items()}


def lay_out(inp):
    c_ = np.ascontiguousarray
    A = {k: np.asarray(x) for k, x in inp.items()}

    def rows(t):
        return c_(t.T.reshape(KT, P, -1).transpose(1, 0, 2))

    def units(w):
        L, K, M = w.shape
        return c_(w.reshape(L, K // P, P, M // P, P).transpose(0, 3, 2, 1, 4).reshape(L, M // P, P, K))

    def cols(t):
        return t.reshape(t.shape[0], -1, P).transpose(2, 0, 1)

    o = {"x_lat": rows(A["x"][0]), "x_ctx": rows(A["ctx"][0])}
    o["cond"] = c_(np.stack([A["c"][0], A["c_ctx"]], -1).reshape(KT, P, 2).transpose(1, 0, 2))
    o["w_mod"] = units(A["w_mod"])
    order = np.concatenate([np.r_[64 * j:64 * j + 64, 64 * (j + 4):64 * (j + 4) + 64] for j in range(4)])
    w_in = A["w_in"]
    o["w_in"] = units(np.concatenate([w_in[:, :, order], w_in[:, :, 512:]], -1))
    w_out = A["w_out"]
    o["w_out"] = units(np.concatenate([w_out[:, order], w_out[:, 512:]], 1))
    w_up = A["w_up"].reshape(LAYERS, D, 2, FT, P)
    o["w_up"] = units(w_up[:, :, ::-1].transpose(0, 1, 3, 2, 4).reshape(LAYERS, D, 2 * D_FF))
    o["w_down"] = units(A["w_down"])
    taps_bias = lambda w, b: np.concatenate([w, b[:, None]], 1)
    hs = taps_bias(A["hy_short_w"], A["hy_short_b"]).reshape(LAYERS, 4, 6, P).transpose(3, 0, 2, 1).reshape(P, LAYERS, 24)
    fd = taps_bias(A["ffn_dw_w"], A["ffn_dw_b"]).reshape(LAYERS, 4, FT, P).transpose(3, 0, 2, 1).reshape(P, LAYERS, 4 * FT)
    cw = A["cv_dw_w"].reshape(LAYERS, CV_K, 2, P).transpose(3, 0, 2, 1).reshape(P, LAYERS, 62)
    hv = np.zeros((P, LAYERS, 4), np.float32)
    for q, n in enumerate(("hy_b1", "hy_freq1", "hy_b2", "hy_freq2")):
        hv[0:HY_W, :, q] = A[n].T
    sink = np.broadcast_to(A["attn_sink"][None], (P, LAYERS, HEADS))
    parts = [cols(A[n]) for n in ("b_mod", "g_pre_mix", "g_post_mix", "g_pre_ffn", "g_post_ffn")]
    parts += [hs, cw, cols(A["cv_dw_b"]), cols(A["cv_ln_g"]), cols(A["cv_ln_b"]), fd, sink, hv]
    o["vec"] = c_(np.concatenate(parts, -1))
    f12 = np.zeros((LAYERS, HY_W, 2, HY_W), np.float32)
    f12[:, 0:HY_EMB, 0] = A["hy_w1"]
    f12[:, :, 1] = A["hy_w2"]
    o["f_w12"] = f12
    o["f_w3"] = c_(A["hy_w3"].reshape(LAYERS, HY_W, 2, 2, HY_CH).transpose(0, 1, 3, 2, 4).reshape(LAYERS, HY_W, 1024))
    o["f_bias"] = c_(A["hy_bias"].reshape(LAYERS, 1, 2 * HY_CH))
    return o


def kernel(**inputs):
    import concourse.bacc as bacc
    from concourse.bass_utils import run_bass_kernel_spmd

    arrays = {f"in_{k}": v for k, v in {**lay_out(inputs), **shape_tables()}.items()}
    nc = bacc.Bacc("TRN2", target_bir_lowering=False, num_devices=1)
    aps = {k[3:]: nc.dram_tensor(k, v.shape, mybir.dt.from_np(v.dtype), kind="ExternalInput").ap() for k, v in arrays.items()}
    out = nc.dram_tensor("out_x", (P, KT, SEQ), F32, kind="ExternalOutput").ap()
    build_kernel(nc, aps, out)
    r = run_bass_kernel_spmd(nc, [arrays], core_ids=[0])
    y = r.results[0]["out_x"]
    return np.ascontiguousarray(y.transpose(2, 1, 0).reshape(1, SEQ, D))
```

```python
from contextlib import ExitStack

import numpy as np

import concourse.bass as bass
from concourse import mybir
from concourse.alu_op_type import AluOpType as ALU

F32 = mybir.dt.float32
F32R = mybir.dt.float32r
BF16 = mybir.dt.bfloat16
ACT = mybir.ActivationFunctionType
AX = mybir.AxisListType

P = 128
D = 1024
KT = D // P
LAYERS = 2
SEQ, CTX = 512, 256
GRID_W = 64
HEADS, KV_HEADS, HEAD = 8, 2, 64
HY_CH = CV_CH = 256
HY_EMB, HY_BANDS, HY_W = 33, 16, 64
CV_K = 31
D_FF = 2816
FT = D_FF // P
EPS = 1e-6
SCALE = HEAD ** -0.5
NEG = -1e30
MAGIC = 12582912.0
TWO_PI = [6.28125, 0.0019340515136718750, 1.2556659146e-06]
PI_IN = 3.1415925

T_A, T_GATE, T_Q, T_K, T_V, T_X1, T_X2, T_Z, IN_T = 0, 2, 4, 8, 9, 10, 12, 14, 16

DOWN_UNITS = [(0, 6), (6, 12), (12, 17), (17, 22)]

VEC = {}
_at = 0
for _name, _n in [("g_pre_mix", 8), ("g_post_mix", 8), ("g_pre_ffn", 8), ("g_post_ffn", 8),
                  ("hy_short", 24), ("cv_w", 62), ("cv_b", 2), ("ln_g", 2), ("ln_b", 2),
                  ("ffn_dw", 4 * FT), ("sink", HEADS), ("hy_vec", 4)]:
    VEC[_name] = (_at, _n)
    _at += _n
NVEC = _at

SLOTS, AHEAD, ACC = 4, 3, 2
MOD_GROUPS = LAYERS * 6 * D // 512
MOD_START = [(0, 1), (1, 2), (2, 7)]
MOD_RIDE = {(0, "w_in"): 7, (0, "w_out"): 11, (1, "w_up"): 13}


class Gemm:

    def __init__(self, name, units, blocks, outs_per_body, body=4, rider=None):
        self.name, self.units, self.blocks, self.body = name, units, blocks, body
        self.outs = units * outs_per_body // body
        self.unit0 = self.out0 = 0
        self.rider = rider
        if rider is not None:
            self.units, self.body = 2 * units, 2 * body

    def own(self, k, j, i):
        if self.rider is None:
            return k, j
        if j % 2 == 0:
            return None
        return (k // 2 if isinstance(k, int) else i * 4 + j // 2), j // 2

    def mod(self, k, j, i):
        if self.rider is None or j % 2:
            return None
        return self.rider + (k // 8 if isinstance(k, int) else i), j % 8 // 2

    def width(self, k):
        b = self.blocks
        return P * (b[k % len(b)] if isinstance(b, tuple) else b)


def plan():
    streams = []
    for layer in range(LAYERS):
        last = layer == LAYERS - 1
        for kind, t in (("ctx", CTX), ("lat", SEQ)):
            full = kind == "lat" or not last
            nt = t // P
            ride = {n: MOD_RIDE.get((len(streams), n)) for n in ("w_in", "w_out", "w_up")}
            g = {"w_in": Gemm("w_in", IN_T if full else 2, 8, 4, rider=ride["w_in"])}
            if full:
                g["filt"] = Gemm("filt", nt, 2 * nt, 8)
                for o in range(2):
                    g[f"fwd{o}"] = Gemm("fwd", nt, 2 * nt, 4)
                    g[f"inv{o}"] = Gemm("inv", nt, 2 * nt, 4)
                g["w_out"] = Gemm("w_out", KT, 8, 4, rider=ride["w_out"])
                g["w_up"] = Gemm("w_up", 2 * FT, 8, 4, rider=ride["w_up"])
                g["w_down"] = Gemm("w_down", 4 * KT, tuple(b - a for a, b in DOWN_UNITS), 2, 8)
            streams.append(dict(layer=layer, kind=kind, T=t, nt=nt, full=full, gemm=g, col=int(kind == "ctx")))
    by = {(s["layer"], s["kind"]): s for s in streams}
    starts = [Gemm("mod", 4 * (b - a), 8, 0) for a, b in MOD_START]
    streams[0]["mod"] = starts
    order = list(starts)
    for s in streams:
        if s["full"]:
            order.append(s["gemm"]["filt"])
            other = by[(s["layer"], "ctx")]
            if not other["full"]:
                order.append(other["gemm"]["w_in"])
            order += [g for n, g in s["gemm"].items() if n != "filt"]
    unit = out = norm = pre = post = full = 0
    for g in order:
        g.unit0, g.out0 = unit, out
        unit += g.units
        out += g.outs
    for s in streams:
        s["norm0"], s["pre0"], s["post0"], s["full0"] = norm, pre, post, full
        norm += 4 if s["full"] else 1
        pre += 2 if s["full"] else 1
        post += 2 if s["full"] else 0
        full += s["full"]
    att = 0
    for n, s in enumerate(streams):
        s["index"] = n
        s["att0"] = att
        if s["full"]:
            s["heads"] = attention_steps(s)
            att += len(s["heads"])
    return streams


SHORT = (2, 0, 1)


def mixer_plan(nt):
    pe, side = {}, {}

    def add(where, slot, *what):
        where.setdefault(slot, []).append(what)

    for t in range(3):
        add(side, t, "short", SHORT[t])
    halves = nt // 2
    for h in range(halves):
        add(pe, 1 + h, "z_t", h)
        add(side, 1 + h, "z", h)
    s = 1 + halves
    for o in range(2):
        for name, what in (("fwd", "spectrum"), ("inv", "gate")):
            for k in range(nt):
                side.setdefault(s + k - 1, []).insert(0, ("split", f"{name}{o}", k))
                add(pe, s + k, name, o, k)
                add(side, s + k + 1, what, o, k)
            if o == 0 and name == "fwd":
                for h in range(halves):
                    add(pe, s + 1 + h, "x1_t", h)
                    add(side, s + 1 + h, "x1", h)
            s += nt + 1
    last = 8 * nt - 1
    add(pe, last - 2, "ln_sum")
    add(side, last - 2, "ln_centre")
    add(pe, last, "ln_square_sum")
    return pe, side


def attention_steps(s):
    steps = []
    for n in range(s["nt"]):
        for j in range(HEADS // 2):
            for half in range(2):
                a, b = (max(0, n - 1), min(s["nt"], n + 2)) if s["kind"] == "lat" else (0, 0)
                steps.append(dict(n=n, j=j, half=half, a=a, b=b, width=CTX + P * (b - a)))
    return steps


def build_kernel(nc, a, out):
    streams = plan()
    ctx = ExitStack()
    with ctx:
        def sb(name, shape, dt=F32):
            return ctx.enter_context(nc.sbuf_tensor(name, shape, dt))

        def ps(name, shape):
            return ctx.enter_context(nc.psum_tensor(name, shape, F32))

        def sem(name):
            return ctx.enter_context(nc.semaphore(name))

        base = (nc.sbuf_base + 63) // 64 * 64
        H0, W0, R0 = base, base + 32768, base + 32768 + 90112
        sb("regions", [P, (R0 + 4096 * SLOTS - nc.sbuf_base + 3) // 4])

        def at(name, shape, offset, dt=F32):
            return nc.alloc_sbuf_tensor_at(name, shape, dt, offset=offset)

        x = {"lat": sb("x_lat", [P, KT, SEQ]), "ctx": sb("x_ctx", [P, KT, CTX])}
        w_raw, w_lo = at("w_raw", [P, SLOTS, 8 * P], R0), at("w_lo", [P, SLOTS, 8 * P], R0, F32R)
        w_hi = sb("w_hi", [P, SLOTS, 8 * P], F32R)
        mod_rows = sb("mod_rows", [P, 512])
        b_mod = sb("b_mod", [P, LAYERS * 48])
        cond_parts = sb("cond_parts", [P, KT, 4], F32R)
        tmp = sb("tmp", [P, 4, SEQ])
        std = sb("std", [P, SEQ])
        rstd = sb("rstd", [P, SEQ])
        rope = sb("rope", [P, 2, SEQ])
        ident = sb("ident", [P, P])
        ones = sb("ones", [P, P])
        ident_b = sb("ident_b", [P, P], BF16)
        masks_b = sb("masks_b", [P, 2, P], BF16)
        vec = sb("vec", [P, LAYERS, NVEC])
        cond = sb("cond", [P, KT, 2])
        mod = sb("mod", [P, LAYERS * 48, 2])
        coef = sb("coef", [P, 4, KT, 2])
        k_ctx = sb("k_ctx", [P, 2, CTX])
        v_ctx = sb("v_ctx", [P, CTX // P, P])
        small = sb("small", [P, 16])
        neg_sink = sb("neg_sink", [P, LAYERS, HEADS])
        eps = sb("eps", [P, 1])

        h_hi, h_lo = at("h_hi", [P, KT, SEQ], H0, F32R), at("h_lo", [P, KT, SEQ], H0 + 16384, F32R)
        z_hi, z_lo = at("z_hi", [P, 4, HY_CH], H0, F32R), at("z_lo", [P, 4, HY_CH], H0 + 4096, F32R)
        y_hi, y_lo = at("y_hi", [P, 8, HY_CH], H0 + 8192, F32R), at("y_lo", [P, 8, HY_CH], H0 + 16384, F32R)
        short_z, short_x1 = at("short_z", [P, 2, SEQ], H0 + 8192), at("short_x1", [P, 2, SEQ], H0 + 12288)
        conv2 = at("conv2", [P, 4, HY_CH], H0)
        x1t = at("x1t", [P, 4, HY_CH], H0 + 24576)
        v_lat = at("v_lat", [P, SEQ // P, P], H0 + 28672)
        y = at("y", [P, KT, SEQ], H0)

        act_hi, act_lo = at("act_hi", [P, FT, SEQ], W0, F32R), at("act_lo", [P, FT, SEQ], W0 + 45056, F32R)
        p = at("p", [P, IN_T, SEQ], W0)
        mix_hi, mix_lo = at("mix_hi", [P, KT, SEQ], W0 + 32768, F32R), at("mix_lo", [P, KT, SEQ], W0 + 49152, F32R)
        spec = [at("spec_r", [P, 4, SEQ], W0 + 65536), at("spec_s", [P, 4, SEQ], W0 + 73728)]
        masks = at("masks", [P, 2, P], W0 + 65536)
        glu = at("glu", [P, 2, SEQ], W0 + 81920)
        short_x2 = p[:, T_Z:T_Z + 2, :]
        tap = at("tap", [P, SEQ], W0 + 88064)
        prob = at("prob", [P, 2, 640], W0 + 40960)
        probT = [at("probT0", [P, 2, 640], W0 + 57344), sb("probT1", [P, 2, 640])]
        k_lat = [at("k_lat0", [P, SEQ], W0 + 46080), at("k_lat1", [P, SEQ], W0 + 62464)]
        taps = [[at(f"taps_{n}_{m}", [P, 4, SEQ], W0 + 8192 * (2 * i + k), F32R) for k, m in enumerate(("hi", "lo"))]
                for i, n in enumerate(("sum", "dif"))]
        decay = at("decay", [P, 4, SEQ], W0 + 32768)
        emb = at("emb", [HY_EMB, SEQ], H0 + 16384)
        f_w12 = at("f_w12", [HY_W, 2, HY_W], H0 + 18432)
        f_h1 = at("f_h1", [HY_W, SEQ], H0 + 18944)
        f_h2 = at("f_h2", [P, SEQ], H0 + 20992)
        f_arg = at("f_arg", [P, SEQ], H0 + 23040)
        f_k = at("f_k", [P, SEQ], H0 + 25088)
        f_w3 = at("f_w3", [P, 1024], H0 + 27136)
        f_bias = at("f_bias", [1, SEQ], W0 + 86016)

        psA = ps("psA", [P, ACC, 512])
        psS = ps("psS", [P, 1024])
        psT = ps("psT", [P, 1024])
        psO = ps("psO", [P, 512])
        psN = ps("psN", [P, 512])

        s_const = sem("constants_loaded")
        s_x = sem("x_ctx_loaded")
        s_xl = sem("x_lat_loaded")
        s_rt = sem("rope_table_loaded")
        s_set = sem("constants_set")
        s_cond = sem("cond_ready")
        s_condp = sem("cond_parts_ready")
        s_mrow = sem("mod_rows_ready")
        s_mT = sem("mod_rows_transposed")
        s_modh = sem("mod_high_ready")
        s_mod = sem("mod_ready")
        s_coef = sem("coef_ready")
        s_raw = [sem(f"raw_loaded{i}") for i in range(SLOTS)]
        s_hi = sem("w_hi_ready")
        s_lo = sem("w_lo_ready")
        s_used = sem("unit_multiplied")
        s_free = sem("acc_evacuated")
        s_sq = sem("square_ready")
        s_squsd = sem("square_summed")
        s_std = sem("std_ready")
        s_rstd = sem("rstd_ready")
        s_t = sem("normed_ready")
        s_hh = sem("h_hi_ready")
        s_hf = sem("h_full_ready")
        s_yr = sem("y_scaled")
        s_h = sem("h_lo_ready")
        s_xu = sem("x_updated")
        s_rope = sem("rope_done")
        s_vT = sem("v_transposed")
        s_v = sem("v_ready")
        s_score = sem("scores_ready")
        s_max = sem("max_ready")
        s_exp = sem("exp_ready")
        s_prob = sem("exp_and_sink_ready")
        s_pn = sem("prob_normalised")
        s_pT = sem("prob_transposed")
        s_pTc = sem("probT_ready")
        s_o = sem("attn_out_ready")
        s_ohi = sem("attn_hi_ready")
        s_olo = sem("attn_lo_ready")
        s_filtw = sem("filter_weights_loaded")
        s_filtd = sem("decay_loaded")
        s_fmm = sem("filter_product_ready")
        s_farg = sem("filter_angle_ready")
        s_fsin = sem("filter_sine_ready")
        s_tsum = sem("taps_full_ready")
        s_thi = sem("taps_hi_ready")
        s_tlo = sem("taps_lo_ready")
        s_shc = sem("short_conv_centre_ready")
        s_short = sem("short_conv_ready")
        s_zT = sem("z_transposed")
        s_x1T = sem("x1_transposed")
        s_yT = sem("conv2_transposed")
        s_hz = sem("hyena_hi_ready")
        s_hzl = sem("hyena_lo_ready")
        s_x1t = sem("x1t_ready")
        s_yf = sem("spectrum_full_ready")
        s_yhi = sem("spectrum_hi_ready")
        s_ylo = sem("spectrum_lo_ready")
        s_gout = sem("hyena_gated")
        s_ghi = sem("hyena_out_hi_ready")
        s_sig = sem("sigmoid_ready")
        s_conv = sem("conv31_ready")
        s_lnm = sem("ln_sum_ready")
        s_lna = sem("ln_act_ready")
        s_lnd = sem("ln_centred")
        s_mix = sem("mix_ready")
        s_ft = sem("ffn_gate_started")
        s_fc = sem("ffn_gate_convolved")
        s_fsi = sem("ffn_silu_ready")
        s_fa = sem("ffn_hidden_full_ready")
        s_fhi = sem("ffn_hidden_hi_ready")
        s_flo = sem("ffn_hidden_lo_ready")
        s_dve = sem("vector_step")
        s_act = sem("scalar_step")
        s_pool = sem("pool_step")
        s_out = sem("out_stored")

        def v(layer, name, j=0, n=1):
            o = VEC[name][0] + j
            if isinstance(j, int):
                return vec[:, layer, o:o + n]
            return vec[:, layer, bass.ds(o, n)]

        class Steps:

            def __init__(self, eng, s):
                self.eng, self.s, self.n, self.off = eng, s, 0, 0

            def inc(self, ins):
                ins.then_inc(self.s, 1)
                self.n += 1
                return self.n

            def wait(self, n):
                self.eng.wait_ge(self.s, n + self.off)

            def seq(self, ins):
                self.wait(self.inc(ins))

        FULL = [s for s in streams if s["full"]]

        def taps_before(st):
            return sum(s["nt"] for s in FULL if s["full0"] < st["full0"])

        def halves_before(st):
            return taps_before(st) // 2

        def rope_before(st):
            return 5 * sum(s["kind"] == "lat" for s in FULL if s["full0"] < st["full0"])

        def mods_before(st):
            return MOD_START[-1][1] if st["full0"] == 0 else sum(
                (g.units // 8 for q in streams[:st["index"]] for g in q["gemm"].values() if g.rider is not None), MOD_START[-1][1])

        def follows(st):
            later = [s for s in FULL if s["full0"] == st["full0"] + 1]
            return later[0] if later else None

        def over(eng, g, f, steps=None, peel=0, head=0):
            body = g.body
            rounds = g.units // body - head
            looped = rounds - peel if rounds - peel >= 2 else 0
            for k in range(head * body if looped else 0):
                f(k, k, 0)
            head = head if looped else 0
            if looped:
                if steps:
                    n0 = steps.n
                with eng.Fori(head, head + looped) as i:
                    if steps:
                        steps.off = (i - head) * steps.per_round if head else i * steps.per_round
                    for j in range(body):
                        f(i * body + j, j, i)
                if steps:
                    assert steps.n - n0 == steps.per_round, (g.name, steps.n - n0)
                    steps.n = n0 + looped * steps.per_round
                    steps.off = 0
            for k in range((head + looped) * body, g.units):
                f(k, k, 0)

        def raw_count(g, k, j):
            done = (g.unit0 + j) // SLOTS + 1
            if isinstance(k, int):
                return 16 * ((g.unit0 + k) // SLOTS + 1)
            return 16 * done + (k - j) * (16 // SLOTS)

        def dyn(t, L, k):
            if isinstance(k, int):
                return t[L][k]
            return t[L][bass.ds(k, 1)].rearrange("a p n -> p (a n)")

        def dynt(t, k, T):
            if isinstance(k, int):
                return t[:, k, 0:T]
            return t[:, bass.ds(k, 1), 0:T].rearrange("p a t -> p (a t)")

        def att_pairs(st):
            return st["att0"] // 2

        def hz0(st):
            return sum(s["nt"] // 2 + s["nt"] for s in FULL if s["full0"] < st["full0"])

        def gout0(st):
            return sum(s["nt"] + 2 for s in streams if s["full"] and s["full0"] < st["full0"])

        def filter_tables(e, st):
            e.dma_start(emb[:, 0:st["T"]], a[f"emb{st['T']}"]).then_inc(s_filtw, 16)
            e.dma_start(f_w12[:], a["f_w12"][st["layer"]]).then_inc(s_filtw, 16)
            e.dma_start(f_w3[:], a["f_w3"][st["layer"]]).then_inc(s_filtw, 16)

        def filter_decay(e, st):
            e.dma_start(f_bias[:], a["f_bias"][st["layer"]]).then_inc(s_filtd, 16)
            e.dma_start(decay[:, 0:st["nt"], :], a[f"decay{st['T']}"]).then_inc(s_filtd, 16)

        POST_DVE = 4
        EARLY = [(0, 3), (3, 6), (6, KT + 1)]

        block = ctx.enter_context(nc.Block())

        @block.sync
        def _(e):
            for t, n in ((cond, "cond"), (ident, "ident"), (masks, "masks"), (vec, "vec"), (b_mod, "b_mod")):
                e.dma_start(t[:], a[n]).then_inc(s_const, 16)

            def mod_unit(group, c):
                n = group * 4 + c
                return a["w_mod"][n] if isinstance(n, int) else a["w_mod"][bass.ds(n, 1)].rearrange("a p n -> p (a n)")

            def load(g, src):
                def one(k, j, i):
                    slot = (g.unit0 + j) % SLOTS
                    e.wait_ge(s_used, g.unit0 + k + 1)
                    w = g.width(j)
                    own = g.own(k, j, i)
                    e.dma_start(w_raw[:, slot, 0:w], src(*own, i) if own else mod_unit(*g.mod(k, j, i))).then_inc(s_raw[slot], 16)
                over(e, g, one)

            def filter_units(st):
                for (first, _), g in zip(MOD_START, st.get("mod", ())):
                    load(g, lambda k, j, i: mod_unit(first, k))
                    if first == 0:
                        e.dma_start(x["ctx"][:], a["x_ctx"]).then_inc(s_x, 16)
                load(st["gemm"]["filt"], lambda k, j, i: a[f"fwd{st['T']}"][k])

            for st in streams:
                L, T, g = st["layer"], st["T"], st["gemm"]
                if st["index"] == 0:
                    filter_units(st)
                    e.dma_start(x["lat"][:], a["x_lat"]).then_inc(s_xl, 16)
                    e.dma_start(rope[:], a["rope"]).then_inc(s_rt, 16)
                first = 0 if st["full"] else T_K
                load(g["w_in"], lambda k, j, i: dyn(a["w_in"], L, k + first))
                if not st["full"]:
                    continue
                F, I = a[f"fwd{T}"], a[f"inv{T}"]
                for o in range(2):
                    load(g[f"fwd{o}"], lambda k, j, i: F[k])
                    load(g[f"inv{o}"], lambda k, j, i: I[k])
                load(g["w_out"], lambda k, j, i: dyn(a["w_out"], L, k))
                load(g["w_up"], lambda k, j, i: dyn(a["w_up"], L, k))

                def down(k, j, i):
                    lo, hi = DOWN_UNITS[j % 4]
                    return a["w_down"][L][bass.ds(i * 2 + j // 4, 1)].rearrange("a p n -> p (a n)")[:, lo * P:hi * P]

                load(g["w_down"], down)
                if follows(st):
                    filter_units(follows(st))
            n_out = 0
            for kt in range(0, KT, 2):
                e.wait_ge(s_xu, KT * 5 + kt + 2)
                e.dma_start(out[:, kt:kt + 2, :], x["lat"][:, kt:kt + 2, :]).then_inc(s_out, 16)
                n_out += 16
            e.wait_ge(s_out, n_out)

        @block.tensor
        def _(e):
            e.wait_ge(s_set, 7)
            e.nop().then_inc(s_used, SLOTS)

            def passes(dst, b, hi, lo, slot, first, last):
                wh, wl = w_hi[:, slot, b * P:(b + 1) * P], w_lo[:, slot, b * P:(b + 1) * P]
                e.matmul(dst, wh, hi, start=first, stop=False)
                e.matmul(dst, wh, lo, start=False, stop=False)
                return e.matmul(dst, wl, hi, start=False, stop=last)

            def unit_wait(g, k):
                e.wait_ge(s_lo, g.unit0 + k + 1)

            def norm(n, T):
                for kt in range(KT):
                    norm_tile(n, kt, kt, T)

            def norm_tile(n, kt, j, T, squares=(tmp[:, 0, :], tmp[:, 1, :])):
                e.wait_ge(s_sq, KT * n + kt + 1)
                static = isinstance(kt, int)
                e.matmul(psN[:, 0:T], ones[:], squares[j % 2][:, 0:T], start=static and kt == 0,
                         stop=static and kt == KT - 1).then_inc(s_squsd, 1)

            def mod_unit(g, k, j, group, c):
                unit_wait(g, k)
                if c == 0 and not (isinstance(group, int) and group == 0):
                    e.wait_ge(s_mrow, group)
                slot = (g.unit0 + j) % SLOTS
                for w in (w_hi, w_lo):
                    for b in range(2):
                        kt = 2 * c + b
                        mm = e.matmul(psO[0:4, :], cond_parts[:, kt, :], w[:, slot, b * 512:b * 512 + 512],
                                      start=w is w_hi and kt == 0, stop=w is w_lo and kt == KT - 1)
                mm.then_inc(s_used, 1)

            def mod_transposes(group):
                e.wait_ge(s_mrow, group + 1)
                if not (isinstance(group, int) and group == 0):
                    e.wait_ge(s_mod, group)
                for t in range(4):
                    mm = e.transpose(psT[:, t * P:(t + 1) * P], mod_rows[:, t * P:(t + 1) * P], ident[:])
                mm.then_inc(s_mT, 1)

            def mods(g, first):
                for k in range(g.units):
                    mod_unit(g, k, k, first + k // 4, k % 4)
                    if k >= 4 and k % 4 == 1:
                        mod_transposes(first + k // 4 - 1)
                mod_transposes(first + g.units // 4 - 1)

            def sine_layer(st, r):
                T, f0 = st["T"], st["full0"]
                if r == 0:
                    e.wait_ge(s_filtw, 48 * (f0 + 1))
                    e.matmul(psS[0:HY_W, 512:512 + T], f_w12[0:HY_EMB, 0, :], emb[:, 0:T], start=True, stop=True).then_inc(s_fmm, 1)
                else:
                    e.wait_ge(s_fsin, 2 * f0 + 1)
                    e.matmul(psS[0:HY_W, 0:T], f_w12[:, 1, :], f_h1[:, 0:T], start=True, stop=True).then_inc(s_fmm, 1)

            def filters(st, nxt=None):
                T, nt, f0, taps0, g = st["T"], st["nt"], st["full0"], taps_before(st), st["gemm"]["filt"]
                e.wait_ge(s_fsin, 2 * f0 + 2)
                e.wait_ge(s_mod, mods_before(st))
                for tt in range(nt):
                    if tt >= 2:
                        e.wait_ge(s_tsum, 2 * (taps0 + tt - 1))
                    dst = (psS, psT)[tt % 2]
                    for half in range(2):
                        some = slice(512 * half, 512 * half + 512)
                        mm = e.matmul(dst[:, some], f_h2[:, tt * P:(tt + 1) * P], f_w3[:, some], start=True, stop=True)
                    mm.then_inc(s_fmm, 1)
                    if nxt:
                        if tt == 0:
                            e.wait_ge(s_std, nxt["norm0"])
                        for kt in range(2 * tt, 2 * tt + 2):
                            norm_tile(nxt["norm0"], kt, kt, nxt["T"], (f_arg, f_k))
                e.wait_ge(s_tlo, 2 * (taps0 + nt))
                for k in range(g.units):
                    unit_wait(g, k)
                    for r in range(2):
                        o = g.out0 + 2 * k + r
                        e.wait_ge(s_free, o + 1)
                        for b in range(nt):
                            mm = passes(psA[:, o % ACC, :], r * nt + b, taps[r][0][:, b, :], taps[r][1][:, b, :],
                                        (g.unit0 + k) % SLOTS, b == 0, b == nt - 1)
                    mm.then_inc(s_used, 1)

            def proj(st, name, hi, lo, tile_ready, n=None):
                g, T = st["gemm"][name], st["T"]

                def one(u, uj, i):
                    own = g.own(u, uj, i)
                    if not own:
                        mod_unit(g, u, uj, *g.mod(u, uj, i))
                        return
                    k, j = own
                    unit_wait(g, u)
                    e.wait_ge(s_free, g.out0 + k + 1)
                    dst = psA[:, (g.out0 + j) % ACC, 0:T]
                    for b in range(8):
                        if isinstance(k, int) and k == 0:
                            for wait in tile_ready(b):
                                e.wait_ge(*wait)
                        mm = passes(dst, b, hi[:, b, 0:T], lo[:, b, 0:T], (g.unit0 + uj) % SLOTS, b == 0, b == 7)
                    mm.then_inc(s_used, 1)
                    if n is not None and k:
                        norm_tile(n, k - 1, k - 1, T)
                    if g.rider is not None and uj % 8 == 7:
                        mod_transposes(g.mod(u - 7, uj - 7, i)[0])
                over(e, g, one, head=1)
                if n is not None:
                    norm_tile(n, KT - 1, KT - 1, T)

            def attention_and_mixers(st):
                T, nt, g, H, a0, f0 = st["T"], st["nt"], st["gemm"], st["heads"], st["att0"], st["full0"]
                taps0 = taps_before(st)

                def scores(w):
                    h = H[w]
                    q = p[:, T_Q + h["j"], h["n"] * P:(h["n"] + 1) * P]
                    if st["kind"] == "lat":
                        e.wait_ge(s_rope, rope_before(st) + 2 + h["j"] if h["n"] == 0 else rope_before(st) + 5)
                    if a0 + w >= 1:
                        e.wait_ge(s_exp, a0 + w)
                    blocks = list(range(h["a"], h["b"]))
                    mm = e.matmul(psS[:, 0:CTX], q, k_ctx[:, h["half"], :], start=True, stop=True)
                    for c, some in ((CTX, blocks[:2]), (CTX + 2 * P, blocks[2:])):
                        if not some:
                            continue
                        edge = [(c + P * (b - some[0]), int(b > h["n"])) for b in some if b != h["n"]]
                        mm = e.matmul(psS[:, c:c + P * len(some)], q, k_lat[h["half"]][:, some[0] * P:(some[-1] + 1) * P],
                                      start=True, stop=True)
                        for at_, side_ in edge:
                            mm = e.matmul(psS[:, at_:at_ + P], ident_b[:], masks_b[:, side_, :], start=False, stop=True,
                                          skip_group_check=True)
                    mm.then_inc(s_score, 1)

                def transposes(w):
                    e.wait_ge(s_pn, a0 + w + 1)
                    if a0 + w >= 1:
                        e.wait_ge(s_pTc, a0 + w)
                    for c in range(H[w]["width"] // P):
                        mm = e.transpose(psT[:, c * P:(c + 1) * P], prob[:, w % 2, c * P:(c + 1) * P], ident[:])
                    mm.then_inc(s_pT, 1)

                def values(w):
                    h = H[w]
                    pair = (a0 + w) // 2
                    e.wait_ge(s_pTc, a0 + w + 1)
                    if pair >= 1:
                        e.wait_ge(s_olo, pair)
                    chunks = h["width"] // P
                    for c in range(chunks):
                        for half in range(2):
                            hp = slice(64 * half, 64 * half + 64)
                            val = v_ctx[:, c, hp] if c < 2 else v_lat[:, h["a"] + c - 2, hp]
                            mm = e.matmul(psO[hp, 0:P], val, probT[w // 2 % 2][:, half, c * P:(c + 1) * P],
                                          start=c == 0, stop=c == chunks - 1)
                    mm.then_inc(s_o, 1)

                def transpose_half(src, h, done):
                    for tt in range(2):
                        for c in range(2):
                            at_ = (2 * h + tt) * P
                            mm = e.transpose(psN[:, (2 * tt + c) * P:(2 * tt + c + 1) * P], src[:, c, at_:at_ + P], ident[:])
                    mm.then_inc(done, 1)

                def mixer(what, *arg):
                    if what == "z_t":
                        e.wait_ge(s_short, 6 * f0 + 2)
                        if arg[0]:
                            e.wait_ge(s_hzl, hz0(st) + arg[0])
                        transpose_half(short_z, arg[0], s_zT)
                    elif what == "x1_t":
                        e.wait_ge(s_short, 6 * f0 + 4)
                        e.wait_ge(s_hzl, hz0(st) + nt // 2)
                        if arg[0]:
                            e.wait_ge(s_x1t, halves_before(st) + arg[0])
                        transpose_half(short_x1, arg[0], s_x1T)
                    elif what == "fwd":
                        o, k = arg
                        gf = g[f"fwd{o}"]
                        e.wait_ge(s_hzl, hz0(st) + nt // 2 + nt * o)
                        unit_wait(gf, k)
                        oo = gf.out0 + k
                        e.wait_ge(s_free, oo + 1)
                        for r in range(2):
                            for b in range(nt):
                                mm = passes(psA[:, oo % ACC, r * 256:r * 256 + 256], r * nt + b, z_hi[:, b, :], z_lo[:, b, :],
                                            (gf.unit0 + k) % SLOTS, b == 0, b == nt - 1)
                        mm.then_inc(s_used, 1)
                    elif what == "inv":
                        o, k = arg
                        gi = g[f"inv{o}"]
                        e.wait_ge(s_ylo, 2 * taps0 + nt * (o + 1))
                        unit_wait(gi, k)
                        oo = gi.out0 + k
                        e.wait_ge(s_free, oo + 1)
                        for b in range(2 * nt):
                            mm = passes(psA[:, oo % ACC, 0:256], b, y_hi[:, b, :], y_lo[:, b, :], (gi.unit0 + k) % SLOTS,
                                        b == 0, b == 2 * nt - 1)
                        mm.then_inc(s_used, 1)
                    else:
                        r = int(what == "ln_square_sum")
                        e.wait_ge(s_lna, 6 * f0 + 3) if r else e.wait_ge(s_conv, 2 * (f0 + 1))
                        for c in range(2):
                            mm = e.matmul(psN[:, 0:T], ones[:], p[:, (T_GATE if r else T_A) + c, 0:T], start=c == 0, stop=c == 1)
                        mm.then_inc(s_lnm, 1)

                pe_plan, _ = mixer_plan(nt)
                if g["w_in"].rider is not None:
                    e.wait_ge(s_mod, g["w_in"].rider + 4)
                scores(0)
                for w in range(len(H)):
                    if w + 1 < len(H):
                        scores(w + 1)
                    transposes(w)
                    if w >= 2 and w % 2 == 0:
                        values(w - 1)
                    for what in pe_plan.get(w, ()):
                        mixer(*what)
                values(len(H) - 1)
                e.wait_ge(s_free, ACC + g["inv1"].out0 + nt)
                for c in range(2):
                    for tt in range(nt):
                        mm = e.transpose(psT[:, c * 512 + tt * P:c * 512 + (tt + 1) * P], conv2[:, tt, c * P:(c + 1) * P], ident[:])
                mm.then_inc(s_yT, 1)

            for st in streams:
                L, T, nt, g, f0 = st["layer"], st["T"], st["nt"], st["gemm"], st["full0"]
                if st["index"] == 0:
                    def startup(n):
                        if n == 0:
                            e.wait_ge(s_condp, 2)
                        mods(st["mod"][n], MOD_START[n][0])
                        if n == 0:
                            norm(0, T)
                    sine_layer(st, 0)
                    startup(0)
                    sine_layer(st, 1)
                    startup(1)
                    startup(2)
                    filters(st)
                elif st["index"] == 3:
                    norm(st["norm0"], T)
                proj(st, "w_in", h_hi, h_lo, lambda b: [(s_h, KT * st["pre0"] + b + 1)])
                e.wait_ge(s_free, ACC + g["w_in"].out0 + g["w_in"].outs)
                for n in range(nt):
                    mm = e.transpose(psN[:, n * P:(n + 1) * P], p[:, T_V, n * P:(n + 1) * P], ident[:])
                mm.then_inc(s_vT, 1)
                if not st["full"]:
                    continue
                e.wait_ge(s_v, st["index"] + 1)
                attention_and_mixers(st)
                e.wait_ge(s_olo, att_pairs(st) + 4 * nt)
                proj(st, "w_out", mix_hi, mix_lo,
                     lambda b: [(s_olo, att_pairs(st) + 4 * nt)] if b < 4 else [(s_mix, 4 * f0 + b - 3)], st["norm0"] + 1)
                norm(st["norm0"] + 2, T)
                proj(st, "w_up", h_hi, h_lo, lambda b: [(s_h, KT * (st["pre0"] + 1) + b + 1)])
                gd = g["w_down"]
                nxt = follows(st)
                if nxt:
                    sine_layer(nxt, 0)
                e.wait_ge(s_flo, FT * (f0 + 1))

                def down(k, j, i):
                    c = j % 4
                    lo, hi = DOWN_UNITS[c]
                    unit_wait(gd, k)
                    if c == 0:
                        e.wait_ge(s_free, gd.out0 + i * 2 + j // 4 + 1)
                    for b in range(hi - lo):
                        mm = passes(psA[:, (gd.out0 + j // 4) % ACC, 0:T], b, act_hi[:, lo + b, 0:T], act_lo[:, lo + b, 0:T],
                                    (gd.unit0 + j) % SLOTS, lo + b == 0, lo + b == FT - 1)
                    mm.then_inc(s_used, 1)
                    if nxt and isinstance(k, int) and k == 3:
                        sine_layer(nxt, 1)
                    done = i * 2 + j // 4
                    if c == 3 and not (isinstance(done, int) and done == 0):
                        norm_tile(st["norm0"] + 3, done - 1, j // 4 - 1, T)

                over(e, gd, down, head=1)
                norm_tile(st["norm0"] + 3, KT - 1, KT - 1, T)
                if nxt:
                    filters(nxt, streams[st["index"] + 1])

        @block.scalar
        def _(e):
            nc_ = nc.scalar
            step = Steps(e, s_act)
            e.wait_ge(s_const, 80)
            step.seq(nc_.activation(small[:, 0:1], ident[:, 0:1], ACT.Silu))
            nc_.activation(cond[:], cond[:], ACT.Silu).then_inc(s_cond, 1)
            e.wait_ge(s_cond, 1)
            nc_.copy(cond_parts[:, :, 0:2], cond[:]).then_inc(s_condp, 1)
            e.wait_ge(s_set, 3)

            def split(g, k, j):
                u = g.unit0 + j
                e.wait_ge(s_raw[u % SLOTS], raw_count(g, k, j))
                w = g.width(j)
                nc_.copy(w_hi[:, u % SLOTS, 0:w], w_raw[:, u % SLOTS, 0:w]).then_inc(s_hi, 1)

            def norm(n, src, ready, T):
                for kt in range(KT):
                    if ready is not None:
                        e.wait_ge(*ready(kt))
                    if kt >= 2:
                        e.wait_ge(s_squsd, KT * n + kt - 1)
                    nc_.activation(tmp[:, kt % 2, 0:T], src[:, kt, 0:T], ACT.Square).then_inc(s_sq, 1)
                norm_end(n, T)

            def norm_end(n, T):
                e.wait_ge(s_squsd, KT * (n + 1))
                e.wait_ge(s_rstd, n)
                nc_.activation(std[:, 0:T], psN[:, 0:T], ACT.Sqrt, bias=eps[:, 0:1], scale=1.0 / D).then_inc(s_std, 1)

            def evac_square(n, kt, j, dst, src, T):
                nc_.copy(dst, src)
                e.wait_ge(s_squsd, KT * n + kt - 1)
                nc_.activation(tmp[:, j % 2, 0:T], src, ACT.Square).then_inc(s_sq, 1)
                e.wait_ge(s_sq, KT * n + kt + 1)
                e.nop().then_inc(s_free, 1)

            def pre(i, which, st, tiles=range(KT)):
                T, c = st["T"], st["col"]
                for kt in tiles:
                    e.wait_ge(s_t, KT * i + kt + 1)
                    m = 48 * st["layer"] + 24 * which + kt
                    g_, b_ = coef[:, 2 * which, kt, c:c + 1], mod[:, m, c:c + 1]
                    nc_.activation(h_hi[:, kt, 0:T], tmp[:, kt % 2, 0:T], ACT.Identity, bias=b_, scale=g_).then_inc(s_hh, 1)

            def mod_rows_out(g, k, group):
                e.wait_ge(s_used, SLOTS + g.unit0 + k + 1)
                if not (isinstance(group, int) and group == 0):
                    e.wait_ge(s_mT, group)
                nc_.copy(mod_rows[0:4, :], psO[0:4, :]).then_inc(s_mrow, 1)

            def lagged(g, evac, steps=None, inside=False, head=0):
                def one(k, j, i):
                    def split_next():
                        if not isinstance(k, int) or k + AHEAD < g.units:
                            split(g, k + AHEAD, j + AHEAD)
                    own = g.own(k, j, i)
                    if own and inside:
                        evac(*own, i, k, split_next)
                        return
                    if own:
                        evac(*own, i, k)
                    elif g.mod(k, j, i)[1] == 3:
                        mod_rows_out(g, k, g.mod(k, j, i)[0])
                    split_next()
                over(e, g, one, steps, peel=1, head=head)

            def mods(g, first):
                begin(g)
                lagged(g, lambda k, j, i, u: mod_rows_out(g, k, first + k // 4) if k % 4 == 3 else None)

            def begin(g):
                for k in range(min(AHEAD, g.units)):
                    split(g, k, k)

            def sine(st, r):
                e.wait_ge(s_farg, 2 * st["full0"] + r + 1)
                nc_.activation((f_h1, f_h2)[r][0:HY_W, 0:st["T"]], f_arg[0:HY_W, 0:st["T"]], ACT.Sin).then_inc(s_fsin, 1)

            def filters(st, nxt=None):
                T, nt, f0, taps0, g = st["T"], st["nt"], st["full0"], taps_before(st), st["gemm"]["filt"]
                for tt in range(nt):
                    if nxt:
                        n = nxt["norm0"]
                        if tt == 0:
                            e.wait_ge(s_fsin, 2 * f0 + 2)
                        for kt in range(2 * tt, 2 * tt + 2):
                            if kt >= 2:
                                e.wait_ge(s_squsd, KT * n + kt - 1)
                            nc_.activation((f_arg, f_k)[kt % 2][:, 0:nxt["T"]], x[nxt["kind"]][:, kt, 0:nxt["T"]],
                                           ACT.Square).then_inc(s_sq, 1)
                    for r in range(2):
                        e.wait_ge(s_tsum, 2 * (taps0 + tt) + 1 + r)
                        nc_.copy(taps[r][0][:, tt, :], tmp[:, 2 + r, :]).then_inc(s_thi, 1)
                    if tt < min(AHEAD, g.units):
                        split(g, tt, tt)
                if nxt:
                    norm_end(nxt["norm0"], nxt["T"])
                if st["index"] == 0:
                    e.wait_ge(s_coef, 1)
                    pre(st["pre0"], 0, st)
                for k in range(g.units):
                    if k + AHEAD < g.units:
                        split(g, k + AHEAD, k + AHEAD)
                    e.wait_ge(s_used, SLOTS + g.unit0 + k + 1)
                    for r in range(2):
                        nc_.copy(spec[r][:, k, :], psA[:, (g.out0 + 2 * k + r) % ACC, :]).then_inc(s_free, 1)
                    if nxt and k:
                        if k == 1:
                            e.wait_ge(s_coef, 1 if nxt["layer"] == 0 else 4)
                        pre(nxt["pre0"], 0, nxt, range(EARLY[k - 1][0], min(KT, EARLY[k - 1][1])))
                        if k <= min(AHEAD, nxt["gemm"]["w_in"].units):
                            split(nxt["gemm"]["w_in"], k - 1, k - 1)

            def attention_and_mixers(st):
                L, T, nt, g, H, a0, f0 = st["layer"], st["T"], st["nt"], st["gemm"], st["heads"], st["att0"], st["full0"]
                taps0 = taps_before(st)

                def expo(w):
                    h = H[w]
                    r = (a0 + w) % 2
                    hd = h["j"] + 4 * h["half"]
                    e.wait_ge(s_max, a0 + w + 1)
                    nc_.activation(prob[:, w % 2, 0:h["width"]], psS[:, 0:h["width"]], ACT.Exp, bias=small[:, 2 + r:3 + r],
                                   scale=SCALE, accum_out=small[:, 6 + r:7 + r]).then_inc(s_exp, 1)
                    nc_.activation(small[:, 4 + r:5 + r], v(L, "sink", hd), ACT.Exp, bias=small[:, 2 + r:3 + r]).then_inc(s_prob, 1)

                def back(w):
                    e.wait_ge(s_pT, a0 + w + 1)
                    width = H[w]["width"]
                    nc_.copy(probT[w // 2 % 2][:, w % 2, 0:width], psT[:, 0:width]).then_inc(s_pTc, 1)

                def out_hi(w):
                    h = H[w]
                    e.wait_ge(s_o, (a0 + w) // 2 + 1)
                    nc_.copy(mix_hi[:, h["j"], h["n"] * P:(h["n"] + 1) * P], psO[:, 0:P]).then_inc(s_ohi, 1)

                def mixer(what, *arg):
                    if what == "split":
                        split(g[arg[0]], arg[1], arg[1])
                    elif what == "short":
                        q, = arg
                        if q == 1:
                            e.wait_ge(s_short, 6 * f0 + 2)
                        for c in range(2):
                            o_ = 4 * (2 * q + c)
                            nc_.activation((short_x1, short_x2, short_z)[q][:, c, 0:T], p[:, T_X1 + 2 * q + c, 0:T], ACT.Identity,
                                           scale=v(L, "hy_short", o_ + 1), bias=v(L, "hy_short", o_ + 3)).then_inc(s_shc, 1)
                    elif what == "z":
                        h, = arg
                        e.wait_ge(s_zT, halves_before(st) + h + 1)
                        nc_.copy(z_hi[:, 2 * h:2 * h + 2, :], psN[:].rearrange("p (n d) -> p n d", n=2)).then_inc(s_hz, 1)
                    elif what == "x1":
                        h, = arg
                        e.wait_ge(s_x1T, halves_before(st) + h + 1)
                        nc_.copy(x1t[:, 2 * h:2 * h + 2, :], psN[:].rearrange("p (n d) -> p n d", n=2)).then_inc(s_x1t, 1)
                    elif what == "spectrum":
                        o, k = arg
                        e.wait_ge(s_yf, 2 * taps0 + nt * o + k + 1)
                        nc_.copy(y_hi[:, 2 * k:2 * k + 2, :], tmp[:, 2, :].rearrange("p (r c) -> p r c", r=2)).then_inc(s_yhi, 1)
                    elif what == "gate":
                        o, k = arg
                        gi = g[f"inv{o}"]
                        if o == 0:
                            e.wait_ge(s_gout, gout0(st) + k + 1)
                            nc_.copy(z_hi[:, k, :], tmp[:, 3, 0:256]).then_inc(s_hz, 1)
                        else:
                            e.wait_ge(s_used, SLOTS + gi.unit0 + k + 1)
                            nc_.copy(conv2[:, k, :], psA[:, (gi.out0 + k) % ACC, 0:256]).then_inc(s_free, 1)
                    elif what == "ln_centre":
                        e.wait_ge(s_lnm, 2 * f0 + 1)
                        nc_.activation(std[:, 0:T], psN[:, 0:T], ACT.Copy, scale=1.0 / CV_CH).then_inc(s_lna, 1)
                        for c in range(2):
                            e.wait_ge(s_lnd, 5 * f0 + c + 1)
                            nc_.activation(p[:, T_GATE + c, 0:T], p[:, T_A + c, 0:T], ACT.Square).then_inc(s_lna, 1)
                    elif what == "ln_scale":
                        e.wait_ge(s_lnm, 2 * f0 + 2)
                        nc_.activation(std[:, 0:T], psN[:, 0:T], ACT.Sqrt, bias=eps[:, 0:1], scale=1.0 / CV_CH).then_inc(s_lna, 1)

                _, side_plan = mixer_plan(nt)
                expo(0)
                for w in range(len(H)):
                    back(w)
                    if w + 1 < len(H):
                        expo(w + 1)
                    todo = side_plan.get(w, ())
                    for what in todo:
                        if what[0] == "split":
                            mixer(*what)
                    if w >= 2 and w % 2 == 0:
                        out_hi(w - 1)
                    for what in todo:
                        if what[0] != "split":
                            mixer(*what)
                split(g["w_out"], 0, 0)
                out_hi(len(H) - 1)
                mixer("ln_scale")
                for c in range(2):
                    e.wait_ge(s_gout, gout0(st) + nt + c + 1)
                    nc_.copy(mix_hi[:, 4 + c, 0:T], tmp[:, c, 0:T]).then_inc(s_ghi, 1)
                for k in range(1, AHEAD):
                    split(g["w_out"], k, k)
                for c in range(2):
                    e.wait_ge(s_lnd, 5 * f0 + 3 + c + 1)
                    step.inc(nc_.activation(tmp[:, 2 + c, 0:T], p[:, T_A + c, 0:T], ACT.Silu, bias=v(L, "ln_b", c),
                                            scale=v(L, "ln_g", c)))
                step.wait(step.n)
                for c in range(2):
                    nc_.copy(mix_hi[:, 6 + c, 0:T], tmp[:, 2 + c, 0:T]).then_inc(s_lna, 1)

            for st in streams:
                L, T, nt, g, f0 = st["layer"], st["T"], st["nt"], st["gemm"], st["full0"]
                xs = x[st["kind"]]
                n0 = st["norm0"]
                if st["index"] == 0:
                    for r in range(2):
                        sine(st, r)
                        mods(st["mod"][r], MOD_START[r][0])
                        if r == 0:
                            e.wait_ge(s_x, 16)
                            norm(n0, xs, None, T)
                    mods(st["mod"][2], MOD_START[2][0])
                    filters(st)
                elif st["index"] == 3:
                    norm(n0, xs, lambda kt: (s_xu, 8 * st["post0"]), T)
                if st["index"] in (0, 3):
                    begin(g["w_in"])
                if st["index"] == 3:
                    e.wait_ge(s_coef, 4)
                    pre(st["pre0"], 0, st)
                gi = g["w_in"]
                first = 0 if st["full"] else T_K

                def evac_in(k, j, i, u):
                    e.wait_ge(s_used, SLOTS + gi.unit0 + u + 1)
                    src = psA[:, (gi.out0 + j) % ACC, 0:T]
                    dst = dynt(p, k + first, T)
                    if st["full"] and isinstance(k, int) and T_GATE <= k < T_GATE + 2:
                        nc_.activation(dst, src, ACT.Sigmoid).then_inc(s_free, 1)
                        e.wait_ge(s_free, ACC + gi.out0 + k + 1)
                        e.nop().then_inc(s_sig, 1)
                        return
                    nc_.copy(dst, src).then_inc(s_free, 1)

                lagged(gi, evac_in, head=1)
                dst = v_lat
                if st["kind"] == "ctx":
                    dst = v_ctx
                    e.wait_ge(s_free, ACC + gi.out0 + gi.outs)
                    for half in range(2):
                        hp = slice(64 * half, 64 * half + 64)
                        nc_.copy(k_ctx[hp, half, :], p[hp, T_K, 0:T])
                e.wait_ge(s_vT, st["index"] + 1)
                nc_.copy(dst[:, 0:nt, :], psN[:, 0:T].rearrange("p (n d) -> p n d", n=nt)).then_inc(s_v, 1)
                if not st["full"]:
                    continue
                attention_and_mixers(st)
                go = g["w_out"]

                def evac_out(k, j, i, u):
                    e.wait_ge(s_used, SLOTS + go.unit0 + u + 1)
                    evac_square(n0 + 1, k, j, y[:, k, 0:T], psA[:, (go.out0 + j) % ACC, 0:T], T)

                lagged(go, evac_out)
                norm_end(n0 + 1, T)
                gu = g["w_up"]
                begin(gu)
                norm(n0 + 2, xs, lambda kt: (s_xu, 8 * st["post0"] + kt + 1), T)
                e.wait_ge(s_coef, 2 if L == 0 else 4)
                pre(st["pre0"] + 1, 1, st)
                step.seq(nc_.activation(small[:, 0:1], eps[:, 0:1], ACT.Silu))

                def evac_up(k, j, i, u, split_next):
                    jj = i * 2 + j // 2
                    r = (j // 2) % 2
                    if j % 2 == 0:
                        e.wait_ge(s_used, SLOTS + gu.unit0 + u + 1)
                        nc_.activation(tmp[:, r, 0:T], psA[:, (gu.out0 + j) % ACC, 0:T], ACT.Identity,
                                       scale=v(L, "ffn_dw", jj * 4 + 1), bias=v(L, "ffn_dw", jj * 4 + 3)).then_inc(s_ft, 1)
                        split_next()
                        e.wait_ge(s_fc, FT * f0 + jj + 1)
                        nc_.activation(tmp[:, r, 0:T], tmp[:, r, 0:T], ACT.Silu).then_inc(s_fsi, 1)
                    else:
                        split_next()
                        e.wait_ge(s_fa, FT * f0 + jj + 1)
                        nc_.copy(dynt(act_hi, jj, T), tmp[:, 2 + r, 0:T]).then_inc(s_fhi, 1)

                lagged(gu, evac_up, inside=True)
                gd = g["w_down"]
                begin(gd)
                nxt = follows(st)
                if nxt:
                    sine(nxt, 0)

                def evac_down(k, j, i, u):
                    if nxt and isinstance(k, int) and k == 5:
                        sine(nxt, 1)
                    if j % 4 == 3:
                        e.wait_ge(s_used, SLOTS + gd.unit0 + k + 1)
                        kt = i * 2 + j // 4
                        evac_square(n0 + 3, kt, j // 4, dynt(y, kt, T), psA[:, (gd.out0 + j // 4) % ACC, 0:T], T)

                lagged(gd, evac_down, head=1)
                norm_end(n0 + 3, T)
                if nxt:
                    if st["index"] == 0:
                        e.wait_ge(s_xl, 16)
                    filters(nxt, streams[st["index"] + 1])

        @block.vector
        def _(e):
            step = Steps(e, s_dve)
            e.memset(ones[:], 1.0).then_inc(s_set, 1)
            e.memset(eps[:], EPS).then_inc(s_set, 1)
            e.memset(mod_rows[:], 0.0).then_inc(s_set, 1)
            for half in range(2):
                e.memset(k_ctx[64 - 64 * half:128 - 64 * half, half, :], 0.0).then_inc(s_set, 1)
            e.nop().then_inc(s_free, ACC)
            e.wait_ge(s_const, 80)
            at_ = VEC["sink"][0]
            step.seq(e.tensor_scalar(neg_sink[:], vec[:, :, at_:at_ + HEADS], -1.0, None, ALU.mult))
            e.tensor_copy(ident_b[:], ident[:]).then_inc(s_set, 1)
            e.tensor_copy(masks_b[:], masks[:]).then_inc(s_set, 1)

            e.wait_ge(s_condp, 1)
            e.tensor_tensor(cond_parts[:, :, 2:4], cond[:], cond_parts[:, :, 0:2].bitcast(F32), ALU.subtract).then_inc(s_condp, 1)

            def split(g, k, j):
                u = g.unit0 + j
                w = g.width(j)
                e.wait_ge(s_hi, g.unit0 + k + 1)
                e.tensor_tensor(w_lo[:, u % SLOTS, 0:w], w_raw[:, u % SLOTS, 0:w], w_hi[:, u % SLOTS, 0:w].bitcast(F32),
                                ALU.subtract).then_inc(s_lo, 1)

            def begin(g):
                for k in range(min(AHEAD, g.units)):
                    split(g, k, k)

            def mod_out(group):
                e.wait_ge(s_mT, group + 1)
                static = isinstance(group, int)
                tiles = slice(4 * group, 4 * group + 4) if static else bass.ds(group * 4, 4)
                got = psT[:, 0:512].rearrange("p (t c) -> p t c", t=4)
                bias = b_mod[:, tiles].unsqueeze(2).to_broadcast([P, 4, 2])
                e.tensor_tensor(mod[:, tiles, :], got[:, :, 0:2], bias, ALU.add).then_inc(s_modh, 1)
                e.wait_ge(s_modh, group + 1)
                e.tensor_tensor(mod[:, tiles, :], got[:, :, 2:4], mod[:, tiles, :], ALU.add).then_inc(s_mod, 1)

            def lagged(g, evac, steps=None, inside=False, head=0):
                def one(k, j, i):
                    def split_next():
                        if not isinstance(k, int) or k + AHEAD < g.units:
                            split(g, k + AHEAD, j + AHEAD)
                    own = g.own(k, j, i)
                    if own and inside:
                        evac(*own, i, k, split_next)
                    else:
                        if own:
                            evac(*own, i, k)
                        split_next()
                    if g.rider is not None and j % 8 == 7:
                        mod_out(g.mod(k - 7, j - 7, i)[0])
                over(e, g, one, steps, peel=1, head=head)

            def mods(g, first):
                begin(g)
                def before_last(k, j, i, u):
                    if j % 4 == 1 and not (isinstance(k, int) and k < 4):
                        mod_out(first + k // 4 - 1)
                lagged(g, before_last, head=1)
                mod_out(first + g.units // 4 - 1)

            def low(dst, full, hi):
                return e.tensor_tensor(dst, full, hi.bitcast(F32), ALU.subtract)

            def reciprocal_std(n, T):
                e.wait_ge(s_std, n + 1)
                e.reciprocal(rstd[:, 0:T], std[:, 0:T]).then_inc(s_rstd, 1)
                e.wait_ge(s_rstd, n + 1)

            def pre(i, n, st, tiles=range(KT + 1)):
                T, xs = st["T"], x[st["kind"]]
                if 0 in tiles and n:
                    reciprocal_std(n, T)
                for kt in tiles:
                    if kt < KT:
                        if kt >= 2:
                            e.wait_ge(s_hh, KT * i + kt - 1)
                            e.wait_ge(s_hf, KT * i + kt - 1)
                        e.tensor_tensor(tmp[:, kt % 2, 0:T], xs[:, kt, 0:T], rstd[:, 0:T], ALU.mult).then_inc(s_t, 1)
                    if kt >= 1:
                        b = kt - 1
                        e.wait_ge(s_hh, KT * i + b + 1)
                        e.wait_ge(s_hf, KT * i + b + 1)
                        low(h_lo[:, b, 0:T], tmp[:, 2 + b % 2, 0:T], h_hi[:, b, 0:T]).then_inc(s_h, 1)

            def post(n, which, st):
                T, xs, c = st["T"], x[st["kind"]], st["col"]
                reciprocal_std(n, T)
                i = 2 * st["full0"] + which
                made = {}
                for kt in range(KT + 1):
                    if kt < POST_DVE:
                        if kt >= 2:
                            e.wait_ge(s_xu, KT * i + kt - 1)
                        made[kt] = step.inc(e.tensor_tensor(tmp[:, 2 + kt % 2, 0:T], y[:, kt, 0:T], rstd[:, 0:T], ALU.mult))
                    if kt >= 1:
                        b = kt - 1
                        if b < POST_DVE:
                            scaled = tmp[:, 2 + b % 2, 0:T]
                            step.wait(made[b])
                        else:
                            scaled = y[:, b, 0:T]
                            e.wait_ge(s_yr, (KT - POST_DVE) * i + b - POST_DVE + 1)
                        e.scalar_tensor_tensor(out=xs[:, b, 0:T], in0=scaled, scalar=coef[:, 2 * which + 1, b, c:c + 1],
                                               in1=xs[:, b, 0:T], op0=ALU.mult, op1=ALU.add).then_inc(s_xu, 1)

            counts = [0]

            def coefs(L, kinds, groups):
                names = ("g_pre_mix", "g_post_mix", "g_pre_ffn", "g_post_ffn")
                e.wait_ge(s_mod, groups)
                for q in kinds:
                    t0 = 48 * L + 24 * (q // 2) + 8 + 8 * (q % 2)
                    for c in range(2):
                        if q % 2 == 0:
                            last = e.scalar_tensor_tensor(out=coef[:, q, :, c], in0=mod[:, t0:t0 + 8, c], scalar=1.0,
                                                          in1=v(L, names[q], 0, 8), op0=ALU.add, op1=ALU.mult)
                        else:
                            last = e.tensor_tensor(coef[:, q, :, c], mod[:, t0:t0 + 8, c], v(L, names[q], 0, 8), ALU.mult)
                last.then_inc(s_coef, 1)
                counts[0] += 1
                e.wait_ge(s_coef, counts[0])

            def angle(st, r):
                L, f0, taps0 = st["layer"], st["full0"], taps_before(st)
                hv = lambda q: v(L, "hy_vec", q)[0:HY_W]
                src = (psS[0:HY_W, 512:512 + st["T"]], psS[0:HY_W, 0:st["T"]])[r]
                arg, turns = f_arg[0:HY_W, 0:st["T"]], f_k[0:HY_W, 0:st["T"]]
                e.wait_ge(s_fmm, (2 * f0 + taps0) + r + 1)
                if r == 0:
                    e.memset(f_h2[HY_W:P, :], 0.0)
                else:
                    e.wait_ge(s_fsin, 2 * f0 + 1)
                step.seq(e.tensor_scalar(arg, src, hv(2 * r), hv(2 * r + 1), ALU.add, ALU.mult))
                step.seq(e.tensor_scalar(turns, arg, float(1 / (2 * np.pi)), MAGIC, ALU.mult, ALU.add))
                step.seq(e.tensor_scalar(turns, turns, MAGIC, None, ALU.subtract))
                for part in TWO_PI:
                    step.seq(e.scalar_tensor_tensor(out=arg, in0=turns, scalar=-part, in1=arg, op0=ALU.mult, op1=ALU.add))
                e.tensor_scalar(arg, arg, PI_IN, -PI_IN, ALU.min, ALU.max).then_inc(s_farg, 1)

            def filters(st):
                L, T, nt, f0, taps0, g = st["layer"], st["T"], st["nt"], st["full0"], taps_before(st), st["gemm"]["filt"]
                e.wait_ge(s_filtd, 32 * (f0 + 1))
                for tt in range(nt):
                    e.wait_ge(s_fmm, 2 * f0 + taps0 + 2 + tt + 1)
                    for r in range(2):
                        dec = decay[:, tt, 256 * r:256 * r + 256].unsqueeze(1).to_broadcast([P, 2, 256])
                        src = (psS, psT)[tt % 2]
                        i_ = step.inc(e.tensor_tensor(tmp[:, r, :].rearrange("p (o c) -> p o c", o=2),
                                                      src[:, 512 * r:512 * r + 512].rearrange("p (o c) -> p o c", o=2), dec, ALU.mult))
                    step.wait(i_)
                    if tt == 0:
                        step.seq(e.tensor_tensor(tmp[0:1, 0, :], tmp[0:1, 0, :], f_bias[:], ALU.add))
                    if tt:
                        e.wait_ge(s_tlo, 2 * (taps0 + tt))
                    for r, op in enumerate((ALU.add, ALU.subtract)):
                        e.tensor_tensor(tmp[:, 2 + r, :], tmp[:, 0, :], tmp[:, 1, :], op).then_inc(s_tsum, 1)
                    e.wait_ge(s_tsum, 2 * (taps0 + tt + 1))
                    if tt < min(AHEAD, g.units):
                        split(g, tt, tt)
                e.wait_ge(s_tlo, 2 * (taps0 + nt))

            rotated = [0]

            def rotate(t_):
                i_ = step.inc(e.stream_shuffle(tmp[:, 0, :], p[:, t_, :], [(i + 16) % 32 for i in range(32)]))
                i_ = step.inc(e.tensor_tensor(tmp[:, 1, :], p[:, t_, :], rope[:, 0, :], ALU.mult))
                step.wait(i_)
                step.seq(e.tensor_tensor(tmp[:, 0, :], tmp[:, 0, :], rope[:, 1, :], ALU.mult))
                if t_ == T_K:
                    for half in range(2):
                        hp = slice(64 * half, 64 * half + 64)
                        last = e.tensor_tensor(k_lat[half][hp, :], tmp[hp, 0, :], tmp[hp, 1, :], ALU.add)
                        if half == 0:
                            step.seq(last)
                else:
                    last = e.tensor_tensor(p[:, t_, :], tmp[:, 0, :], tmp[:, 1, :], ALU.add)
                last.then_inc(s_rope, 1)
                rotated[0] += 1
                e.wait_ge(s_rope, rotated[0])

            def attention_and_mixers(st):
                L, T, nt, g, H, a0, f0 = st["layer"], st["T"], st["nt"], st["gemm"], st["heads"], st["att0"], st["full0"]
                taps0 = taps_before(st)

                def maxes(w):
                    h = H[w]
                    r = (a0 + w) % 2
                    hd = h["j"] + 4 * h["half"]
                    e.wait_ge(s_score, a0 + w + 1)
                    step.seq(e.tensor_reduce(small[:, 8 + r:9 + r], psS[:, 0:h["width"]], AX.X, ALU.max))
                    e.tensor_scalar(small[:, 2 + r:3 + r], small[:, 8 + r:9 + r], -SCALE, neg_sink[:, L, hd:hd + 1], ALU.mult,
                                    ALU.min).then_inc(s_max, 1)

                def normalise(w):
                    h = H[w]
                    r = (a0 + w) % 2
                    e.wait_ge(s_prob, a0 + w + 1)
                    step.seq(e.tensor_tensor(small[:, 12 + r:13 + r], small[:, 4 + r:5 + r], small[:, 6 + r:7 + r], ALU.add))
                    step.seq(e.reciprocal(small[:, 14 + r:15 + r], small[:, 12 + r:13 + r]))
                    e.tensor_scalar(prob[:, w % 2, 0:h["width"]], prob[:, w % 2, 0:h["width"]], small[:, 14 + r:15 + r], None,
                                    ALU.mult).then_inc(s_pn, 1)

                def out_lo(w):
                    h = H[w]
                    e.wait_ge(s_ohi, (a0 + w) // 2 + 1)
                    sl = slice(h["n"] * P, (h["n"] + 1) * P)
                    low(mix_lo[:, h["j"], sl], psO[:, 0:P], mix_hi[:, h["j"], sl]).then_inc(s_olo, 1)

                two = lambda t: t.rearrange("p (r c) -> p r c", r=2)

                def mixer(what, *arg):
                    if what == "split":
                        split(g[arg[0]], arg[1], arg[1])
                    elif what == "short":
                        q, = arg
                        for c in range(2):
                            hs = lambda i: v(L, "hy_short", 4 * (2 * q + c) + i)
                            src, dst = p[:, T_X1 + 2 * q + c, 0:T], (short_x1, short_x2, short_z)[q][:, c, 0:T]
                            e.wait_ge(s_shc, 6 * f0 + 2 * SHORT.index(q) + c + 1)
                            step.seq(e.scalar_tensor_tensor(out=dst[:, 1:T], in0=src[:, 0:T - 1], scalar=hs(0), in1=dst[:, 1:T],
                                                            op0=ALU.mult, op1=ALU.add))
                            e.scalar_tensor_tensor(out=dst[:, 0:T - 1], in0=src[:, 1:T], scalar=hs(2), in1=dst[:, 0:T - 1],
                                                   op0=ALU.mult, op1=ALU.add).then_inc(s_short, 1)
                    elif what == "z":
                        h, = arg
                        e.wait_ge(s_hz, hz0(st) + h + 1)
                        low(z_lo[:, 2 * h:2 * h + 2, :], psN[:].rearrange("p (n d) -> p n d", n=2), z_hi[:, 2 * h:2 * h + 2, :]).then_inc(s_hzl, 1)
                    elif what == "spectrum":
                        o, k = arg
                        gf = g[f"fwd{o}"]
                        e.wait_ge(s_used, SLOTS + gf.unit0 + k + 1)
                        U = two(psA[:, (gf.out0 + k) % ACC, :])
                        Hs_ = [spec[r][:, k, 256 * o:256 * o + 256].unsqueeze(1).to_broadcast([P, 2, 256]) for r in range(2)]
                        i_ = step.inc(e.tensor_tensor(two(tmp[:, 0, :]), U, Hs_[0], ALU.mult))
                        e.tensor_tensor(two(tmp[:, 1, :]), U, Hs_[1], ALU.mult).then_inc(s_free, 1)
                        e.wait_ge(s_free, ACC + gf.out0 + k + 1)
                        step.wait(i_)
                        if k >= 1:
                            e.wait_ge(s_yhi, 2 * taps0 + nt * o + k)
                        e.tensor_tensor(tmp[:, 2, 0:256], tmp[:, 0, 0:256], tmp[:, 1, 256:512], ALU.subtract)
                        e.tensor_tensor(tmp[:, 2, 256:512], tmp[:, 0, 256:512], tmp[:, 1, 0:256], ALU.add).then_inc(s_yf, 1)
                    elif what == "spectrum_low":
                        o, k = arg
                        e.wait_ge(s_yhi, 2 * taps0 + nt * o + k + 1)
                        low(y_lo[:, 2 * k:2 * k + 2, :], two(tmp[:, 2, :]), y_hi[:, 2 * k:2 * k + 2, :]).then_inc(s_ylo, 1)
                    elif what == "gate" and arg[0] == 0:
                        k = arg[1]
                        gi = g["inv0"]
                        e.wait_ge(s_x1t, halves_before(st) + nt // 2)
                        e.wait_ge(s_used, SLOTS + gi.unit0 + k + 1)
                        e.wait_ge(s_hzl, hz0(st) + nt // 2 + k)
                        e.tensor_tensor(tmp[:, 3, 0:256], psA[:, (gi.out0 + k) % ACC, 0:256], x1t[:, k, :], ALU.mult).then_inc(s_gout, 1)
                        e.wait_ge(s_gout, gout0(st) + k + 1)
                        e.nop().then_inc(s_free, 1)
                    elif what == "gate_low" and arg[0] == 0:
                        k = arg[1]
                        e.wait_ge(s_hz, hz0(st) + nt // 2 + k + 1)
                        low(z_lo[:, k, :], tmp[:, 3, 0:256], z_hi[:, k, :]).then_inc(s_hzl, 1)
                    elif what == "ln_centre":
                        e.wait_ge(s_lna, 6 * f0 + 1)
                        for c in range(2):
                            e.tensor_tensor(p[:, T_A + c, 0:T], p[:, T_A + c, 0:T], std[:, 0:T], ALU.subtract).then_inc(s_lnd, 1)
                    elif what == "ln_scale":
                        e.wait_ge(s_lna, 6 * f0 + 4)
                        e.reciprocal(rstd[:, 0:T], std[:, 0:T]).then_inc(s_lnd, 1)
                        e.wait_ge(s_lnd, 5 * f0 + 3)
                        for c in range(2):
                            e.tensor_tensor(p[:, T_A + c, 0:T], p[:, T_A + c, 0:T], rstd[:, 0:T], ALU.mult).then_inc(s_lnd, 1)

                _, side_plan = mixer_plan(nt)
                maxes(0)
                for w in range(len(H)):
                    normalise(w)
                    if w + 1 < len(H):
                        maxes(w + 1)
                    todo = side_plan.get(w, ())
                    for what in todo:
                        if what[0] != "split":
                            mixer(*what)
                    for what in todo:
                        if what[0] == "split":
                            mixer(*what)
                    for name, *arg in todo:
                        mixer(f"{name}_low", *arg)
                    if w >= 2 and w % 2 == 0:
                        out_lo(w - 1)
                split(g["w_out"], 0, 0)
                out_lo(len(H) - 1)
                e.wait_ge(s_yT, f0 + 1)
                for c in range(2):
                    e.tensor_tensor(tmp[:, c, 0:T], psT[:, c * 512:c * 512 + T], short_x2[:, c, 0:T], ALU.mult).then_inc(s_gout, 1)
                mixer("ln_scale")
                for c in range(2):
                    e.wait_ge(s_ghi, 2 * f0 + c + 1)
                    low(mix_lo[:, 4 + c, 0:T], tmp[:, c, 0:T], mix_hi[:, 4 + c, 0:T]).then_inc(s_mix, 1)
                for k in range(1, AHEAD):
                    split(g["w_out"], k, k)
                for c in range(2):
                    e.wait_ge(s_lna, 6 * f0 + 4 + c + 1)
                    low(mix_lo[:, 6 + c, 0:T], tmp[:, 2 + c, 0:T], mix_hi[:, 6 + c, 0:T]).then_inc(s_mix, 1)

            def filter_splits(st):
                g = st["gemm"]["filt"]
                for k in range(AHEAD, g.units):
                    split(g, k, k)

            for st in streams:
                L, T, nt, g, f0 = st["layer"], st["T"], st["nt"], st["gemm"], st["full0"]
                n0 = st["norm0"]
                if st["index"] == 0:
                    for r in range(2):
                        angle(st, r)
                        if r:
                            reciprocal_std(0, T)
                        mods(st["mod"][r], MOD_START[r][0])
                    mods(st["mod"][2], MOD_START[2][0])
                    filters(st)
                    filter_splits(st)
                    coefs(0, (0,), 4)
                    e.wait_ge(s_x, 16)
                    pre(st["pre0"], n0, st)
                    begin(g["w_in"])
                if st["index"] == 3:
                    begin(g["w_in"])
                    pre(st["pre0"], n0, st)

                def rotary(k, j, i, u):
                    if st["kind"] == "ctx" or not isinstance(k, int) or k < IN_T - 4:
                        return
                    if k == IN_T - 4:
                        e.wait_ge(s_rt, 16)
                        e.wait_ge(s_free, ACC + g["w_in"].out0 + T_K + 1)
                        for half in range(2):
                            e.memset(k_lat[half][64 - 64 * half:128 - 64 * half, :], 0.0)
                        rotate(T_K)
                    rotate(T_Q + k - (IN_T - 4))

                lagged(g["w_in"], rotary)
                if not st["full"]:
                    continue
                e.wait_ge(s_free, ACC + g["w_in"].out0 + g["w_in"].outs)
                attention_and_mixers(st)
                lagged(g["w_out"], lambda k, j, i, u: None)
                if st["index"] == 0:
                    coefs(0, (1, 2), 10)
                post(n0 + 1, 0, st)
                gu = g["w_up"]
                begin(gu)
                pre(st["pre0"] + 1, n0 + 2, st)

                def evac_up(k, j, i, u, split_next):
                    jj = i * 2 + j // 2
                    r = (j // 2) % 2
                    src = psA[:, (gu.out0 + j) % ACC, :]
                    if j % 2 == 0:
                        e.wait_ge(s_ft, FT * f0 + jj + 1)
                        t_ = tmp[:, r, :]
                        step.seq(e.scalar_tensor_tensor(out=t_[:, 1:T], in0=src[:, 0:T - 1], scalar=v(L, "ffn_dw", jj * 4),
                                                        in1=t_[:, 1:T], op0=ALU.mult, op1=ALU.add))
                        e.scalar_tensor_tensor(out=t_[:, 0:T - 1], in0=src[:, 1:T], scalar=v(L, "ffn_dw", jj * 4 + 2),
                                               in1=t_[:, 0:T - 1], op0=ALU.mult, op1=ALU.add).then_inc(s_fc, 1)
                        e.wait_ge(s_fc, FT * f0 + jj + 1)
                        e.nop().then_inc(s_free, 1)
                        split_next()
                    else:
                        e.wait_ge(s_used, SLOTS + gu.unit0 + u + 1)
                        e.wait_ge(s_fsi, FT * f0 + jj + 1)
                        e.tensor_tensor(tmp[:, 2 + r, 0:T], tmp[:, r, 0:T], src[:, 0:T], ALU.mult).then_inc(s_fa, 1)
                        e.wait_ge(s_fa, FT * f0 + jj + 1)
                        e.nop().then_inc(s_free, 1)
                        split_next()
                        e.wait_ge(s_fhi, FT * f0 + jj + 1)
                        low(dynt(act_lo, jj, T), tmp[:, 2 + r, 0:T], dynt(act_hi, jj, T)).then_inc(s_flo, 1)

                step.per_round = 2
                lagged(gu, evac_up, step, inside=True)
                if st["index"] == 0:
                    coefs(0, (3,), 12)
                gd = g["w_down"]
                begin(gd)
                nxt = follows(st)
                if nxt:
                    angle(nxt, 0)
                lagged(gd, lambda k, j, i, u: angle(nxt, 1) if nxt and isinstance(k, int) and k == 3 else None, head=1)
                if nxt:
                    filters(nxt)
                post(n0 + 3, 1, st)
                if nxt:
                    filter_splits(nxt)
                    early = streams[st["index"] + 1]
                    if early["layer"] > L:
                        e.wait_ge(s_xu, 8 * early["post0"])
                        coefs(1, range(4), MOD_GROUPS)
                    for n, tiles in enumerate(EARLY):
                        pre(early["pre0"], early["norm0"], early, range(*tiles))
                        if n < min(AHEAD, early["gemm"]["w_in"].units):
                            split(early["gemm"]["w_in"], n, n)

        @block.gpsimd
        def _(e):
            step = Steps(e, s_pool)
            def scale_y(st, which):
                T, i = st["T"], 2 * st["full0"] + which
                e.wait_ge(s_rstd, st["norm0"] + 2 + 2 * which)
                for kt in range(POST_DVE, KT):
                    e.tensor_tensor(y[:, kt, 0:T], y[:, kt, 0:T], rstd[:, 0:T], ALU.mult).then_inc(s_yr, 1)

            def pre(i, which, st):
                T, c = st["T"], st["col"]
                e.wait_ge(s_coef, 4 if st["layer"] else 2 if which else 1)
                for kt in range(KT):
                    m = 48 * st["layer"] + 24 * which + kt
                    e.wait_ge(s_t, KT * i + kt + 1)
                    if kt >= 2:
                        e.wait_ge(s_h, KT * i + kt - 1)
                    e.tensor_scalar(tmp[:, 2 + kt % 2, 0:T], tmp[:, kt % 2, 0:T], coef[:, 2 * which, kt, c:c + 1], mod[:, m, c:c + 1],
                                    ALU.mult, ALU.add).then_inc(s_hf, 1)

            def filters(st):
                f0, taps0 = st["full0"], taps_before(st)
                if f0:
                    last = FULL[f0 - 1]["gemm"]
                    e.wait_ge(s_used, SLOTS + last["w_up"].unit0 + last["w_up"].units)
                filter_tables(e, st)
                if f0:
                    e.wait_ge(s_used, SLOTS + last["w_down"].unit0 + last["w_down"].units)
                filter_decay(e, st)
                for tt in range(st["nt"]):
                    for r in range(2):
                        e.wait_ge(s_thi, 2 * (taps0 + tt) + r + 1)
                        e.tensor_tensor(taps[r][1][:, tt, :], tmp[:, 2 + r, :], taps[r][0][:, tt, :].bitcast(F32),
                                        ALU.subtract).then_inc(s_tlo, 1)

            filters(streams[0])
            e.wait_ge(s_const, 80)
            for st in streams:
                pre(st["pre0"], 0, st)
                if not st["full"]:
                    continue
                L, T, f0 = st["layer"], st["T"], st["full0"]
                for c in range(2):
                    e.wait_ge(s_sig, 2 * f0 + c + 1)
                    step.seq(e.tensor_tensor(glu[:, c, 0:T], p[:, T_A + c, 0:T], p[:, T_GATE + c, 0:T], ALU.mult))
                    dst = p[:, T_A + c, :]
                    mid = CV_K // 2
                    step.seq(e.tensor_scalar(dst[:, 0:T], glu[:, c, 0:T], v(L, "cv_w", 31 * c + mid), v(L, "cv_b", c),
                                             ALU.mult, ALU.add))
                    for k in range(CV_K):
                        if k == mid:
                            continue
                        lo, hi = max(0, mid - k), min(T, T + mid - k)
                        step.seq(e.tensor_scalar(tap[:, lo:hi], glu[:, c, lo + k - mid:hi + k - mid], v(L, "cv_w", 31 * c + k), 0.0,
                                                 ALU.mult, ALU.add))
                        ins = e.tensor_tensor(dst[:, lo:hi], dst[:, lo:hi], tap[:, lo:hi], ALU.add)
                        if k < CV_K - 1:
                            step.seq(ins)
                    ins.then_inc(s_conv, 1)
                scale_y(st, 0)
                pre(st["pre0"] + 1, 1, st)
                if follows(st):
                    filters(follows(st))
                scale_y(st, 1)


def shape_tables():
    t = {}
    pos = np.arange(SEQ)
    inv = (10000.0 ** (-np.arange(0, 32, 2, dtype=np.float32) / np.float32(32))).astype(np.float32)
    cos, sin = np.zeros((P, SEQ), np.float32), np.zeros((P, SEQ), np.float32)
    for q in range(P):
        d = q % HEAD
        where = (pos // GRID_W if d < 32 else pos % GRID_W).astype(np.float32)
        ang = where * inv[d % 16]
        cos[q] = np.cos(ang)
        sin[q] = np.sin(ang) * (-1 if d % 32 < 16 else 1)
    t["rope"] = np.stack([cos, sin], 1)
    i = np.arange(P)
    t["masks"] = np.stack([np.where(i[None] >= i[:, None], 0, NEG), np.where(i[None] <= i[:, None], 0, NEG)], 1).astype(np.float32)
    t["ident"] = np.eye(P, dtype=np.float32)
    deltas = np.abs(np.linspace(np.log(1e-2) / 1.5, np.log(1e-2) / 0.3, HY_CH))
    for T in (SEQ, CTX):
        nt = T // P
        lin = np.linspace(0.0, 1.0, T)[:, None]
        w = (2.0 * np.pi / T) * np.arange(T)[:, None]
        f = np.linspace(1e-4, HY_BANDS - 1, HY_BANDS)[None]
        t[f"emb{T}"] = np.concatenate([lin, np.cos(f * w), -np.sin(f * w)], -1).T.astype(np.float32)
        dec = np.exp(-lin * deltas)
        dec2 = dec.copy()
        dec2[0] = 0
        both = np.stack([dec, dec2], 1).reshape(nt, P, 2 * HY_CH)
        t[f"decay{T}"] = both.transpose(1, 0, 2).astype(np.float32)
        ang = np.pi * (2 * np.arange(T)[None] + 1) * np.arange(T)[:, None] / (2 * T) * 1.0
        cs = np.stack([np.cos(ang), np.sin(ang)])
        blk = cs.reshape(2, nt, P, nt, P)
        t[f"fwd{T}"] = blk.transpose(3, 2, 0, 1, 4).reshape(nt, P, 2 * nt * P).astype(np.float32)
        t[f"inv{T}"] = (blk.transpose(1, 4, 3, 0, 2).reshape(nt, P, 2 * nt * P) / T).astype(np.float32)
    return {k: np.ascontiguousarray(x) for k, x in t.items()}


def lay_out(inp):
    c_ = np.ascontiguousarray
    A = {k: np.asarray(x) for k, x in inp.items()}

    def rows(t):
        return c_(t.T.reshape(KT, P, -1).transpose(1, 0, 2))

    def units(w):
        L, K, M = w.shape
        return c_(w.reshape(L, K // P, P, M // P, P).transpose(0, 3, 2, 1, 4).reshape(L, M // P, P, K))

    def cols(t):
        return t.reshape(t.shape[0], -1, P).transpose(2, 0, 1)

    o = {"x_lat": rows(A["x"][0]), "x_ctx": rows(A["ctx"][0])}
    o["cond"] = c_(np.stack([A["c"][0], A["c_ctx"]], -1).reshape(KT, P, 2).transpose(1, 0, 2))
    o["w_mod"] = c_(A["w_mod"].reshape(LAYERS, 4, 2, P, 12, 512).transpose(0, 4, 1, 3, 2, 5).reshape(LAYERS * 48, P, 1024))
    o["b_mod"] = c_(A["b_mod"].reshape(LAYERS * 48, P).T)
    order = np.concatenate([np.r_[64 * j:64 * j + 64, 64 * (j + 4):64 * (j + 4) + 64] for j in range(4)])
    w_in = A["w_in"]
    o["w_in"] = units(np.concatenate([w_in[:, :, 1536:], w_in[:, :, order], w_in[:, :, 512:1536]], -1))
    w_out = A["w_out"]
    o["w_out"] = units(np.concatenate([w_out[:, order], w_out[:, 512:]], 1))
    w_up = A["w_up"].reshape(LAYERS, D, 2, FT, P)
    o["w_up"] = units(w_up[:, :, ::-1].transpose(0, 1, 3, 2, 4).reshape(LAYERS, D, 2 * D_FF))
    o["w_down"] = units(A["w_down"])
    taps_bias = lambda w, b: np.concatenate([w, b[:, None]], 1)
    hs = taps_bias(A["hy_short_w"], A["hy_short_b"]).reshape(LAYERS, 4, 6, P).transpose(3, 0, 2, 1).reshape(P, LAYERS, 24)
    fd = taps_bias(A["ffn_dw_w"], A["ffn_dw_b"]).reshape(LAYERS, 4, FT, P).transpose(3, 0, 2, 1).reshape(P, LAYERS, 4 * FT)
    cw = A["cv_dw_w"].reshape(LAYERS, CV_K, 2, P).transpose(3, 0, 2, 1).reshape(P, LAYERS, 62)
    hv = np.zeros((P, LAYERS, 4), np.float32)
    for q, n in enumerate(("hy_b1", "hy_freq1", "hy_b2", "hy_freq2")):
        hv[0:HY_W, :, q] = A[n].T
    sink = np.broadcast_to(A["attn_sink"][None], (P, LAYERS, HEADS))
    parts = [cols(A[n]) for n in ("g_pre_mix", "g_post_mix", "g_pre_ffn", "g_post_ffn")]
    parts += [hs, cw, cols(A["cv_dw_b"]), cols(A["cv_ln_g"]), cols(A["cv_ln_b"]), fd, sink, hv]
    o["vec"] = c_(np.concatenate(parts, -1))
    f12 = np.zeros((LAYERS, HY_W, 2, HY_W), np.float32)
    f12[:, 0:HY_EMB, 0] = A["hy_w1"]
    f12[:, :, 1] = A["hy_w2"]
    o["f_w12"] = f12
    w3 = np.zeros((LAYERS, P, 1024), np.float32)
    w3[:, 0:HY_W] = A["hy_w3"].reshape(LAYERS, HY_W, 2, 2, HY_CH).transpose(0, 1, 3, 2, 4).reshape(LAYERS, HY_W, 1024)
    o["f_w3"] = w3
    o["f_bias"] = c_(A["hy_bias"].reshape(LAYERS, 1, 2 * HY_CH))
    return o


def kernel(**inputs):
    import concourse.bacc as bacc
    from concourse.bass_utils import run_bass_kernel_spmd

    arrays = {f"in_{k}": v for k, v in {**lay_out(inputs), **shape_tables()}.items()}
    nc = bacc.Bacc("TRN2", target_bir_lowering=False, num_devices=1)
    aps = {k[3:]: nc.dram_tensor(k, v.shape, mybir.dt.from_np(v.dtype), kind="ExternalInput").ap() for k, v in arrays.items()}
    out = nc.dram_tensor("out_x", (P, KT, SEQ), F32, kind="ExternalOutput").ap()
    build_kernel(nc, aps, out)
    r = run_bass_kernel_spmd(nc, [arrays], core_ids=[0])
    y = r.results[0]["out_x"]
    return np.ascontiguousarray(y.transpose(2, 1, 0).reshape(1, SEQ, D))
```
